# Optimizing a Trainium2 kernel written in Bass

```python
import math
import jax, jax.numpy as jnp
from jax import lax
import numpy as np

D_MODEL = 1024
BATCH = 1
SEQ = 512
DEPTH = 1

CHUNK = 64
D_MIX = D_MODEL
D_LRU = D_MIX // 2
LRU_BLOCKS = 8
LRU_BLOCK = D_LRU // LRU_BLOCKS
CONV_WIDTH = 4
LRU_C = 8.0
GLA_HEADS = 4
GLA_DV = (D_MIX - D_LRU) // GLA_HEADS
GLA_DK = GLA_DV // 2
GLA_K = GLA_HEADS * GLA_DK
GLA_V = GLA_HEADS * GLA_DV
GATE_RANK = 16
GATE_TAU = 16.0
D_FF = ((8 * D_MODEL // 3 + 255) // 256) * 256
EPS = 1e-6

SPLIT_SIZES = (D_LRU, D_LRU, GLA_K, GLA_K, GLA_V, GLA_V, GATE_RANK)
P_IN = sum(SPLIT_SIZES)
SPLIT_IDX = tuple(int(v) for v in np.cumsum(SPLIT_SIZES)[:-1])


def rms_norm(x, gain):
    xf = x.astype(jnp.float32)
    y = xf * lax.rsqrt(jnp.mean(xf * xf, axis=-1, keepdims=True) + EPS)
    return (y * gain.astype(jnp.float32)).astype(x.dtype)

def causal_depthwise_conv(x, w, b):
    seq = x.shape[1]
    xp = jnp.pad(x, ((0, 0), (CONV_WIDTH - 1, 0), (0, 0)))
    y = xp[:, 0:seq, :] * w[0]
    for j in range(1, CONV_WIDTH):
        y = y + xp[:, j:j + seq, :] * w[j]
    return y + b

def block_diag_linear(x, w, b):
    xb = x.reshape(x.shape[:-1] + (LRU_BLOCKS, LRU_BLOCK))
    y = jnp.einsum("bsni,nij->bsnj", xb, w.astype(x.dtype))
    return y.reshape(x.shape) + b.astype(x.dtype)

def rg_lru(x, w_a, b_a, w_i, b_i, lam):
    xf = x.astype(jnp.float32)
    r = jax.nn.sigmoid(block_diag_linear(xf, w_a, b_a))
    i = jax.nn.sigmoid(block_diag_linear(xf, w_i, b_i))
    log_a = -LRU_C * r * jax.nn.softplus(-lam.astype(jnp.float32))
    a = jnp.exp(log_a)
    u = jnp.sqrt(-jnp.expm1(2.0 * log_a)) * (i * xf)

    def step(h, au):
        a_t, u_t = au
        h = a_t * h + u_t
        return h, h

    h0 = jnp.zeros((xf.shape[0], xf.shape[2]), jnp.float32)
    _, hs = lax.scan(step, h0, (a.swapaxes(0, 1), u.swapaxes(0, 1)))
    return hs.swapaxes(0, 1).astype(x.dtype)

def gla_chunk_causal(q, k, v, log_alpha):
    bsz, seq = q.shape[:2]
    nc = seq // CHUNK

    def rs(t):
        return t.astype(jnp.float32).reshape(bsz, nc, CHUNK, GLA_HEADS, t.shape[-1])

    q, k, v, la = rs(q), rs(k), rs(v), rs(log_alpha)
    bcum = jnp.cumsum(la, axis=2)
    b_end = bcum[:, :, -1:]
    k_dec = k * jnp.exp(b_end - bcum)
    q_dec = q * jnp.exp(b_end)
    scores = jnp.einsum("bnshd,bnthd->bnhst", q, k_dec)
    o_intra = jnp.einsum("bnhst,bnthv->bnshv", scores, v)
    updates = jnp.einsum("bnthd,bnthv->bnhdv", k_dec, v)
    decay = jnp.exp(b_end[:, :, 0])

    def step(state, inp):
        d, upd = inp
        return d[..., None] * state + upd, state

    s0 = jnp.zeros((bsz, GLA_HEADS, GLA_DK, GLA_DV), jnp.float32)
    _, s_prev = lax.scan(step, s0, (decay.swapaxes(0, 1), updates.swapaxes(0, 1)))
    s_prev = s_prev.swapaxes(0, 1)
    o_inter = jnp.einsum("bnshd,bnhdv->bnshv", q_dec, s_prev)
    return (o_intra + o_inter).reshape(bsz, seq, GLA_HEADS, GLA_DV)

def first_inputs(seed: int = 0) -> dict:
    key = jax.random.key(seed)
    ks = jax.random.split(key, 24)
    f32 = jnp.float32

    def nrm(k, shape, scale):
        return jax.random.normal(k, shape, f32) * scale

    def gain(k, shape):
        return 1.0 + 0.02 * jax.random.normal(k, shape, f32)

    u = jax.random.uniform(ks[10], (DEPTH, D_LRU), f32, 0.9, 0.999)
    s = u ** (1.0 / LRU_C)
    lam = jnp.log(s) - jnp.log1p(-s)
    return {
        "x": jax.random.normal(ks[0], (BATCH, SEQ, D_MODEL), f32),
        "norm1": gain(ks[1], (DEPTH, D_MODEL)),
        "w_in": nrm(ks[2], (DEPTH, D_MODEL, P_IN), D_MODEL ** -0.5),
        "conv_w": nrm(ks[3], (DEPTH, CONV_WIDTH, D_LRU), CONV_WIDTH ** -0.5),
        "conv_b": nrm(ks[4], (DEPTH, D_LRU), 0.02),
        "lru_wa": nrm(ks[5], (DEPTH, LRU_BLOCKS, LRU_BLOCK, LRU_BLOCK), LRU_BLOCK ** -0.5),
        "lru_ba": nrm(ks[6], (DEPTH, D_LRU), 0.02),
        "lru_wi": nrm(ks[7], (DEPTH, LRU_BLOCKS, LRU_BLOCK, LRU_BLOCK), LRU_BLOCK ** -0.5),
        "lru_bi": nrm(ks[8], (DEPTH, D_LRU), 0.02),
        "lru_lambda": lam,
        "gla_w_alpha": nrm(ks[11], (DEPTH, GATE_RANK, GLA_K), GATE_RANK ** -0.5),
        "gla_b_alpha": nrm(ks[12], (DEPTH, GLA_K), 0.02),
        "gla_norm": gain(ks[13], (DEPTH, GLA_DV)),
        "w_out": nrm(ks[14], (DEPTH, D_MIX, D_MODEL), D_MIX ** -0.5),
        "norm2": gain(ks[15], (DEPTH, D_MODEL)),
        "w_ffn_in": nrm(ks[16], (DEPTH, D_MODEL, 2 * D_FF), D_MODEL ** -0.5),
        "w_ffn_out": nrm(ks[17], (DEPTH, D_FF, D_MODEL), D_FF ** -0.5),
        "final_norm": gain(ks[18], (D_MODEL,)),
    }

def first_block(x, norm1, w_in, conv_w, conv_b, lru_wa, lru_ba, lru_wi, lru_bi,
              lru_lambda, gla_w_alpha, gla_b_alpha, gla_norm, w_out, norm2,
              w_ffn_in, w_ffn_out, final_norm):
    bsz, seq, _ = x.shape
    q_scale = GLA_DK ** -0.5
    for l in range(DEPTH):
        h = rms_norm(x, norm1[l])
        p = h @ w_in[l]
        lru_x, lru_g, q, k, v, g, z = jnp.split(p, SPLIT_IDX, axis=-1)

        lru_x = causal_depthwise_conv(lru_x, conv_w[l], conv_b[l])
        lru_o = rg_lru(lru_x, lru_wa[l], lru_ba[l], lru_wi[l], lru_bi[l],
                       lru_lambda[l]) * jax.nn.gelu(lru_g)

        zf = z.astype(jnp.float32) @ gla_w_alpha[l].astype(jnp.float32) + gla_b_alpha[l]
        log_alpha = jax.nn.log_sigmoid(zf) / GATE_TAU
        qh = (q * q_scale).reshape(bsz, seq, GLA_HEADS, GLA_DK)
        kh = k.reshape(bsz, seq, GLA_HEADS, GLA_DK)
        vh = v.reshape(bsz, seq, GLA_HEADS, GLA_DV)
        lah = log_alpha.reshape(bsz, seq, GLA_HEADS, GLA_DK)
        o = gla_chunk_causal(qh, kh, vh, lah)
        o = rms_norm(o, gla_norm[l]).reshape(bsz, seq, GLA_V).astype(x.dtype)
        gla_o = o * jax.nn.silu(g)

        mix = jnp.concatenate([lru_o, gla_o], axis=-1) @ w_out[l]
        x = x + mix

        h = rms_norm(x, norm2[l])
        gate, up = jnp.split(h @ w_ffn_in[l], 2, axis=-1)
        x = x + (jax.nn.silu(gate) * up) @ w_ffn_out[l]
    return rms_norm(x, final_norm)


DEPTH_2 = 2

N_A_LAYERS = DEPTH_2 // 2
N_B_LAYERS = DEPTH_2 - N_A_LAYERS
RMS_EPS = 1e-6

RET_HEADS = 4
RET_QK_DIM = D_MODEL // RET_HEADS
RET_V_DIM = 2 * D_MODEL // RET_HEADS
RET_CHUNK = 128
RET_IN = 2 * RET_HEADS * RET_QK_DIM + 2 * RET_HEADS * RET_V_DIM

FFN_HIDDEN = ((8 * D_MODEL + 3 * 256 - 1) // (3 * 256)) * 256

NSA_HEADS = 16
NSA_GROUPS = 4
NSA_REP = NSA_HEADS // NSA_GROUPS
NSA_HEAD_DIM = 64
CMP_LEN = 32
CMP_STRIDE = 16
CMP_HIDDEN = 256
SEL_LEN = 64
SEL_TOPK = 16
WINDOW = 512
Q_BLOCK = 128
NSA_IN = NSA_HEADS * NSA_HEAD_DIM + 3 * NSA_HEADS
KV_SHARED_OUT = 6 * NSA_GROUPS * NSA_HEAD_DIM

REL_BUCKETS = 32
REL_MAX_DIST = 128


def rms_norm_2(x, g):
    xf = x.astype(jnp.float32)
    y = xf * lax.rsqrt(jnp.mean(xf * xf, axis=-1, keepdims=True) + RMS_EPS)
    return (y * g.astype(jnp.float32)).astype(x.dtype)

def swiglu_ffn(x, w_in, w_out):
    gate, up = jnp.split(x @ w_in, 2, axis=-1)
    return (jax.nn.silu(gate) * up) @ w_out

def rotate_pairs(x, cos, sin):
    x1 = x[..., 0::2]
    x2 = x[..., 1::2]
    return jnp.stack([x1 * cos - x2 * sin, x1 * sin + x2 * cos], axis=-1).reshape(x.shape)

def t5_bucket(dist):
    n = jnp.maximum(dist, 0)
    max_exact = REL_BUCKETS // 2
    nf = jnp.maximum(n, 1).astype(jnp.float32)
    large = max_exact + (jnp.log(nf / max_exact) / math.log(REL_MAX_DIST / max_exact)
                         * (REL_BUCKETS - max_exact)).astype(jnp.int32)
    large = jnp.minimum(large, REL_BUCKETS - 1)
    return jnp.where(n < max_exact, n, large)

def masked_softmax(logits, mask):
    logits = jnp.where(mask, logits, -jnp.inf)
    m = jnp.max(logits, axis=-1, keepdims=True)
    m = jnp.where(jnp.isfinite(m), m, 0.0)
    p = jnp.exp(logits - m)
    return p / jnp.maximum(jnp.sum(p, axis=-1, keepdims=True), jnp.finfo(jnp.float32).tiny)

def retention_mixer(x, w_in, w_out):
    B, S, _ = x.shape
    h, dk, dv, C = RET_HEADS, RET_QK_DIM, RET_V_DIM, RET_CHUNK
    proj = x @ w_in
    q, k, v, g = jnp.split(proj, [h * dk, 2 * h * dk, 2 * h * dk + h * dv], axis=-1)
    q = q.reshape(B, S, h, dk).astype(jnp.float32)
    k = k.reshape(B, S, h, dk).astype(jnp.float32)
    v = v.reshape(B, S, h, dv).astype(jnp.float32)
    pos = jnp.arange(S, dtype=jnp.float32)
    theta = 1.0 / (10000.0 ** jnp.linspace(0.0, 1.0, dk // 2, dtype=jnp.float32))
    ang = pos[:, None] * theta[None, :]
    cos = jnp.cos(ang)[:, None, :]
    sin = jnp.sin(ang)[:, None, :]
    q = rotate_pairs(q, cos, sin)
    k = rotate_pairs(k, cos, sin) * (dk ** -0.5)
    log_gamma = jnp.log(1.0 - 2.0 ** (-5.0 - jnp.arange(h, dtype=jnp.float32)))
    idx = jnp.arange(C, dtype=jnp.float32)
    rel = idx[:, None] - idx[None, :]
    intra_decay = jnp.where(rel >= 0, jnp.exp(jnp.maximum(rel, 0.0) * log_gamma[:, None, None]), 0.0)
    q_decay = jnp.exp((idx + 1.0)[None, :] * log_gamma[:, None])
    k_decay = jnp.exp((C - 1.0 - idx)[None, :] * log_gamma[:, None])
    chunk_decay = jnp.exp(C * log_gamma)
    nC = S // C

    def to_chunks(t):
        return t.reshape(B, nC, C, h, t.shape[-1]).transpose(1, 0, 3, 2, 4)

    def step(state, inp):
        qc, kc, vc = inp
        scores = jnp.einsum('bhid,bhjd->bhij', qc, kc) * intra_decay
        o = (jnp.einsum('bhij,bhje->bhie', scores, vc)
             + jnp.einsum('bhid,bhde->bhie', qc * q_decay[..., None], state))
        state = (state * chunk_decay[:, None, None]
                 + jnp.einsum('bhjd,bhje->bhde', kc * k_decay[..., None], vc))
        return state, o

    state0 = jnp.zeros((B, h, dk, dv), jnp.float32)
    _, o = lax.scan(step, state0, (to_chunks(q), to_chunks(k), to_chunks(v)))
    o = o.transpose(1, 0, 3, 2, 4).reshape(B, S, h, dv)
    o = o * lax.rsqrt(jnp.mean(o * o, axis=-1, keepdims=True) + RMS_EPS)
    o = (o.reshape(B, S, h * dv) * jax.nn.silu(g.astype(jnp.float32))).astype(x.dtype)
    return o @ w_out

def nsa_shared_kv(h, kv_norm, kv_w, cmp_pe_k, cmp_w1_k, cmp_w2_k, cmp_pe_v, cmp_w1_v, cmp_w2_v):
    B, S, _ = h.shape
    G, d = NSA_GROUPS, NSA_HEAD_DIM
    kv = rms_norm_2(h, kv_norm) @ kv_w
    k_c, v_c, k_s, v_s, k_w, v_w = [t.reshape(B, S, G, d) for t in jnp.split(kv, 6, axis=-1)]
    n_cmp = (S - CMP_LEN) // CMP_STRIDE + 1
    blk_idx = np.arange(n_cmp)[:, None] * CMP_STRIDE + np.arange(CMP_LEN)[None, :]

    def compress(t, pe, w1, w2):
        blocks = t[:, blk_idx] + pe[:, None, :]
        blocks = blocks.transpose(0, 1, 3, 2, 4).reshape(B, n_cmp, G, CMP_LEN * d)
        return jax.nn.silu(blocks @ w1) @ w2

    kc = compress(k_c, cmp_pe_k, cmp_w1_k, cmp_w2_k)
    vc = compress(v_c, cmp_pe_v, cmp_w1_v, cmp_w2_v)
    n_sel = S // SEL_LEN
    ks = k_s.reshape(B, n_sel, SEL_LEN, G, d).transpose(0, 3, 1, 2, 4)
    vs = v_s.reshape(B, n_sel, SEL_LEN, G, d).transpose(0, 3, 1, 2, 4)
    pad = ((0, 0), (WINDOW, 0), (0, 0), (0, 0))
    kw = jnp.pad(k_w, pad)
    vw = jnp.pad(v_w, pad)
    return (kc, vc, ks, vs, kw, vw)

def nsa_mixer(x, w_in, w_out, rel_bias, shared):
    B, S, _ = x.shape
    H, G, R, d = NSA_HEADS, NSA_GROUPS, NSA_REP, NSA_HEAD_DIM
    Q = Q_BLOCK
    kc, vc, ks, vs, kw, vw = shared
    proj = x @ w_in
    q = proj[..., :H * d].reshape(B, S, G, R, d)
    gate = jax.nn.sigmoid(proj[..., H * d:].astype(jnp.float32)).reshape(B, S, G, R, 3)
    n_cmp = kc.shape[1]
    n_sel = ks.shape[2]
    n_top = min(SEL_TOPK, n_sel)
    cmp_end = jnp.arange(n_cmp, dtype=jnp.int32) * CMP_STRIDE + CMP_LEN - 1
    ratio = SEL_LEN // CMP_STRIDE
    lead = CMP_LEN // CMP_STRIDE - 1
    span = ratio + lead
    sel_map = ratio * np.arange(n_sel)[:, None] - lead + np.arange(span)[None, :]
    sel_map = np.where((sel_map >= 0) & (sel_map < n_cmp), sel_map, n_cmp)
    bias_tab = rel_bias.astype(jnp.float32)
    bias_gr = bias_tab.reshape(REL_BUCKETS, G, R).transpose(1, 0, 2)
    scale = d ** -0.5
    gather_blocks = jax.vmap(jax.vmap(lambda kb, ib: kb[ib]))
    kc32 = kc.astype(jnp.float32)
    vc32 = vc.astype(jnp.float32)
    sel_ids = jnp.arange(n_sel, dtype=jnp.int32)
    blk_start = sel_ids * SEL_LEN
    win_off = jnp.arange(WINDOW + Q, dtype=jnp.int32)
    g_ids = jnp.arange(G)[None, :, None, None, None]

    def block(qb):
        start = qb * Q
        t = start + jnp.arange(Q, dtype=jnp.int32)
        qblk = lax.dynamic_slice_in_dim(q, start, Q, 1).astype(jnp.float32) * scale
        gg = lax.dynamic_slice_in_dim(gate, start, Q, 1)
        dist_c = t[:, None] - cmp_end[None, :]
        s = jnp.einsum('bqgrd,bngd->bgrqn', qblk, kc32)
        s = s + bias_tab[t5_bucket(dist_c)].reshape(Q, n_cmp, G, R).transpose(2, 3, 0, 1)
        p_c = masked_softmax(s, dist_c >= 0)
        o_c = jnp.einsum('bgrqn,bngd->bqgrd', p_c, vc32)
        imp_c = jnp.sum(p_c, axis=2)
        imp_c = jnp.concatenate([imp_c, jnp.zeros(imp_c.shape[:-1] + (1,), imp_c.dtype)], axis=-1)
        imp = jnp.sum(imp_c[..., sel_map], axis=-1)
        cur = t // SEL_LEN
        valid = blk_start[None, :] <= t[:, None]
        forced = ((sel_ids[None, :] == 0) | (sel_ids[None, :] == cur[:, None])
                  | (sel_ids[None, :] == cur[:, None] - 1))
        imp = jnp.where(forced, jnp.inf, jnp.where(valid, imp, -jnp.inf))
        _, sel_idx = lax.top_k(imp, n_top)
        k_sel = gather_blocks(ks, sel_idx).astype(jnp.float32)
        v_sel = gather_blocks(vs, sel_idx).astype(jnp.float32)
        pos = sel_idx[..., None] * SEL_LEN + jnp.arange(SEL_LEN, dtype=jnp.int32)
        dist_s = t[None, None, :, None, None] - pos
        s = jnp.einsum('bqgrd,bgqnld->bgrqnl', qblk, k_sel)
        s = s + jnp.moveaxis(bias_gr[g_ids, t5_bucket(dist_s)], -1, 2)
        s = s.reshape(B, G, R, Q, n_top * SEL_LEN)
        mask_s = (dist_s >= 0).reshape(B, G, 1, Q, n_top * SEL_LEN)
        p_s = masked_softmax(s, mask_s).reshape(B, G, R, Q, n_top, SEL_LEN)
        o_s = jnp.einsum('bgrqnl,bgqnld->bqgrd', p_s, v_sel)
        kwin = lax.dynamic_slice_in_dim(kw, start, WINDOW + Q, 1).astype(jnp.float32)
        vwin = lax.dynamic_slice_in_dim(vw, start, WINDOW + Q, 1).astype(jnp.float32)
        kpos = start - WINDOW + win_off
        dist_w = t[:, None] - kpos[None, :]
        s = jnp.einsum('bqgrd,bkgd->bgrqk', qblk, kwin)
        s = s + bias_tab[t5_bucket(dist_w)].reshape(Q, WINDOW + Q, G, R).transpose(2, 3, 0, 1)
        mask_w = (dist_w >= 0) & (dist_w < WINDOW) & (kpos[None, :] >= 0)
        p_w = masked_softmax(s, mask_w)
        o_w = jnp.einsum('bgrqk,bkgd->bqgrd', p_w, vwin)
        o = gg[..., 0:1] * o_c + gg[..., 1:2] * o_s + gg[..., 2:3] * o_w
        return o.reshape(B, Q, H * d)

    o = lax.map(block, jnp.arange(S // Q, dtype=jnp.int32))
    o = o.transpose(1, 0, 2, 3).reshape(B, S, H * d).astype(x.dtype)
    return o @ w_out

def second_inputs(seed: int = 0) -> dict:
    key = jax.random.key(seed)
    ks = jax.random.split(key, 24)
    f32 = jnp.float32

    def dense(k, shape, fan_in):
        return jax.random.normal(k, shape, f32) * (fan_in ** -0.5)

    def gain(k, shape):
        return 1.0 + 0.1 * jax.random.normal(k, shape, f32)

    d = NSA_HEAD_DIM
    return {
        "x": jax.random.normal(ks[0], (BATCH, SEQ, D_MODEL), f32),
        "mix_norm_pre": gain(ks[1], (DEPTH_2, D_MODEL)),
        "mix_norm_post": gain(ks[2], (DEPTH_2, D_MODEL)),
        "ffn_norm_pre": gain(ks[3], (DEPTH_2, D_MODEL)),
        "ffn_norm_post": gain(ks[4], (DEPTH_2, D_MODEL)),
        "ffn_w_in": dense(ks[5], (DEPTH_2, D_MODEL, 2 * FFN_HIDDEN), D_MODEL),
        "ffn_w_out": dense(ks[6], (DEPTH_2, FFN_HIDDEN, D_MODEL), FFN_HIDDEN),
        "ret_w_in": dense(ks[7], (N_A_LAYERS, D_MODEL, RET_IN), D_MODEL),
        "ret_w_out": dense(ks[8], (N_A_LAYERS, RET_HEADS * RET_V_DIM, D_MODEL), RET_HEADS * RET_V_DIM),
        "kv_norm": gain(ks[9], (D_MODEL,)),
        "kv_w": dense(ks[10], (D_MODEL, KV_SHARED_OUT), D_MODEL),
        "cmp_pe_k": 0.5 * jax.random.normal(ks[11], (CMP_LEN, d), f32),
        "cmp_w1_k": dense(ks[12], (CMP_LEN * d, CMP_HIDDEN), CMP_LEN * d),
        "cmp_w2_k": dense(ks[13], (CMP_HIDDEN, d), CMP_HIDDEN),
        "cmp_pe_v": 0.5 * jax.random.normal(ks[14], (CMP_LEN, d), f32),
        "cmp_w1_v": dense(ks[15], (CMP_LEN * d, CMP_HIDDEN), CMP_LEN * d),
        "cmp_w2_v": dense(ks[16], (CMP_HIDDEN, d), CMP_HIDDEN),
        "nsa_w_in": dense(ks[17], (N_B_LAYERS, D_MODEL, NSA_IN), D_MODEL),
        "nsa_w_out": dense(ks[18], (N_B_LAYERS, NSA_HEADS * d, D_MODEL), NSA_HEADS * d),
        "rel_bias": 0.5 * jax.random.normal(ks[19], (REL_BUCKETS, NSA_HEADS), f32),
    }

def second_block(x, mix_norm_pre, mix_norm_post, ffn_norm_pre, ffn_norm_post, ffn_w_in, ffn_w_out,
              ret_w_in, ret_w_out, kv_norm, kv_w, cmp_pe_k, cmp_w1_k, cmp_w2_k,
              cmp_pe_v, cmp_w1_v, cmp_w2_v, nsa_w_in, nsa_w_out, rel_bias):
    h = x
    shared = None
    for layer in range(DEPTH_2):
        if layer == N_A_LAYERS:
            shared = nsa_shared_kv(h, kv_norm, kv_w, cmp_pe_k, cmp_w1_k, cmp_w2_k,
                                   cmp_pe_v, cmp_w1_v, cmp_w2_v)
        normed = rms_norm_2(h, mix_norm_pre[layer])
        if layer < N_A_LAYERS:
            mixed = retention_mixer(normed, ret_w_in[layer], ret_w_out[layer])
        else:
            j = layer - N_A_LAYERS
            mixed = nsa_mixer(normed, nsa_w_in[j], nsa_w_out[j], rel_bias, shared)
        h = h + rms_norm_2(mixed, mix_norm_post[layer])
        normed = rms_norm_2(h, ffn_norm_pre[layer])
        h = h + rms_norm_2(swiglu_ffn(normed, ffn_w_in[layer], ffn_w_out[layer]), ffn_norm_post[layer])
    return h


def setup_inputs(seed=0):
    out = dict(first_inputs(seed))
    for name, value in second_inputs(seed + 1).items():
        if name != "x":
            out[name + "_2"] = value
    return out


def reference(
    x, norm1, w_in, conv_w, conv_b, lru_wa, lru_ba, lru_wi, lru_bi, lru_lambda, gla_w_alpha,
    gla_b_alpha, gla_norm, w_out, norm2, w_ffn_in, w_ffn_out, final_norm, mix_norm_pre_2,
    mix_norm_post_2, ffn_norm_pre_2, ffn_norm_post_2, ffn_w_in_2, ffn_w_out_2, ret_w_in_2,
    ret_w_out_2, kv_norm_2, kv_w_2, cmp_pe_k_2, cmp_w1_k_2, cmp_w2_k_2, cmp_pe_v_2, cmp_w1_v_2,
    cmp_w2_v_2, nsa_w_in_2, nsa_w_out_2, rel_bias_2,
):
    x = first_block(
        x, norm1, w_in, conv_w, conv_b, lru_wa, lru_ba, lru_wi, lru_bi, lru_lambda, gla_w_alpha,
        gla_b_alpha, gla_norm, w_out, norm2, w_ffn_in, w_ffn_out, final_norm,
    )
    return second_block(
        x, mix_norm_pre_2, mix_norm_post_2, ffn_norm_pre_2, ffn_norm_post_2, ffn_w_in_2,
        ffn_w_out_2, ret_w_in_2, ret_w_out_2, kv_norm_2, kv_w_2, cmp_pe_k_2, cmp_w1_k_2,
        cmp_w2_k_2, cmp_pe_v_2, cmp_w1_v_2, cmp_w2_v_2, nsa_w_in_2, nsa_w_out_2, rel_bias_2,
    )


_drawn_inputs = setup_inputs


def setup_inputs(seed=0):
    import zlib

    import numpy as np

    out = dict(_drawn_inputs(seed))
    spreads = {}
    factors = {'lru_ba': 8.0, 'lru_bi': 8.0}
    for name, (base, spread) in spreads.items():
        noise = np.random.default_rng([zlib.crc32(name.encode()), seed]).standard_normal(out[name].shape)
        drawn = base * np.exp(spread * noise) if base else spread * noise
        out[name] = __import__('jax').numpy.asarray(drawn.astype(out[name].dtype))
    for name, factor in factors.items():
        out[name] = (out[name] * factor).astype(out[name].dtype)
    return out
```

```python
import math
from contextlib import ExitStack

import concourse.bass as bass
import numpy as np
from concourse import mybir

F32 = mybir.dt.float32
F32R = mybir.dt.float32r
ACT = mybir.ActivationFunctionType
ALU = mybir.AluOpType
AX_X = mybir.AxisListType.X

S = 512
EPS = 1e-6
NEG = -1.0e30
GUARD = -1.0e20
TINY = 1.1754943508222875e-38

RAW_SLOTS = 3
W_SLOTS = 3
LOOK = 2
GEMM_BANKS = 4

VEC_NAMES = [
    ("norm1", 8), ("norm2", 8), ("final_norm", 8), ("mix_pre0", 8), ("mix_post0", 8), ("ffn_pre0", 8),
    ("ffn_post0", 8), ("kv_norm", 8), ("mix_pre1", 8), ("mix_post1", 8), ("ffn_pre1", 8), ("ffn_post1", 8),
    ("conv_w", 16), ("conv_b", 4), ("lru_ba", 4), ("lru_bi", 4), ("lru_lambda", 4), ("b_alpha", 2),
    ("gla_norm", 1), ("pe_k", 16), ("pe_v", 16),
]
VEC_AT = {}
_n = 0
for _name, _w in VEC_NAMES:
    VEC_AT[_name] = _n
    _n += _w
NVEC = _n

FEATURE_MAJOR = {"w_in_t": 8, "w_out": 8, "ffn1_in": 8, "ffn1_out": 22, "ret_t": 8, "ret_out": 16, "ffn2_in": 8,
                 "ffn2_out": 22, "kv_t": 8, "nsa_t": 8, "nsa_out": 8, "ffn3_in": 8, "ffn3_out": 22}
UNITS_TOTAL = 21 + 8 + 68 + 48 + 16 + 68 + 12 + 9 + 8 + 68


class Queue:

    def __init__(self, sem):
        self.sem, self.count, self.items = sem, 0, []

    def __call__(self, fn, *waits, inc=True):
        self.items.append((fn, waits, inc))
        if not inc:
            return None
        self.count += 1
        return (self.sem, self.count)

    def now(self):
        return (self.sem, self.count)

    def play(self, eng):
        seen = {}

        def need(w):
            if w is None:
                return
            if isinstance(w, list):
                for x in w:
                    need(x)
                return
            sem, value = w
            if value > seen.get(sem.name, 0):
                seen[sem.name] = value
                eng.wait_ge(sem, value)

        for fn, waits, inc in self.items:
            need(list(waits))
            ins = fn(eng)
            if inc:
                ins.then_inc(self.sem, 1)


def build(nc, D, out):
    with ExitStack() as ctx:
        def sem(name):
            return ctx.enter_context(nc.semaphore(name))

        def sb(name, shape, dt=F32, stack=ctx):
            return stack.enter_context(nc.sbuf_tensor(name, shape, dt))

        PE, AC, DV, SP, PO = (Queue(sem(n)) for n in ("pe", "act", "dve", "sp", "pool"))
        every = (PE, AC, DV)

        def fence():
            return [q.now() for q in every]

        XT = sb("XT", [128, 8, S])
        AH = sb("AH", [128, 8, S], F32R)
        AL = sb("AL", [128, 8, S], F32R)
        RAW = [sb(f"RAW{i}", [128, 1024]) for i in range(RAW_SLOTS)]
        WH = [sb(f"WH{i}", [128, 1024], F32R) for i in range(W_SLOTS)]
        WL = [sb(f"WL{i}", [128, 1024], F32R) for i in range(W_SLOTS)]
        ident = sb("ident", [128, 128])
        ones = sb("ones", [128, 1])
        RS = sb("RS", [128, S])
        ACC = sb("ACC", [128, S])
        SQ = [sb(f"SQ{i}", [128, S]) for i in range(2)]
        T = [sb(f"T{i}", [128, S]) for i in range(4)]
        vec = sb("vec", [128, NVEC])
        small = sb("small", [128, 64])
        rtok = sb("rtok", [128, 16])
        rstok = sb("rstok", [128, 4])
        rso = sb("rso", [128, 16])
        BANK = [ctx.enter_context(nc.psum_tensor(f"bank{i}", [128, 512], F32)) for i in range(8)]
        bank_free = [[] for _ in range(8)]

        def V(name, i=0, n=1):
            at = VEC_AT[name] + i
            return vec[:, at:at + n]

        s_const = sem("s_const")
        s_x = sem("s_x")
        const_ready = (s_const, 32)
        x_ready = (s_x, 16)
        SP(lambda e: e.dma_start(XT[:, :, :], D["xT"].rearrange("p (f t) -> p f t", f=8)).then_inc(s_x, 16), inc=False)
        SP(lambda e: e.dma_start(vec[:, :], D["vec"]).then_inc(s_const, 16), inc=False)
        SP(lambda e: e.dma_start(ident[:, :], D["ident"]).then_inc(s_const, 16), inc=False)
        t_ones = DV(lambda e: e.memset(ones[:, :], 1.0))

        s_raw = [sem(f"s_raw{i}") for i in range(RAW_SLOTS)]
        units = []
        unit_hi, unit_lo, unit_used = {}, {}, {}
        state = {"dma": 0, "prep": 0, "bank": 0}

        def weight_dma():
            u = state["dma"]
            if u >= UNITS_TOTAL:
                return
            state["dma"] += 1
            r = u % RAW_SLOTS

            def go(e):
                src, n = units[u]
                e.dma_start(RAW[r][:, 0:n], src).then_inc(s_raw[r], 16)
            SP(go, unit_hi.get(u - RAW_SLOTS), unit_lo.get(u - RAW_SLOTS), inc=False)

        def weight_prep():
            u = state["prep"]
            if u >= UNITS_TOTAL:
                return
            state["prep"] += 1
            r, w = u % RAW_SLOTS, u % W_SLOTS
            landed = (s_raw[r], 16 * (u // RAW_SLOTS + 1))
            used = unit_used.get(u - W_SLOTS)
            unit_hi[u] = AC(lambda e: e.activation(WH[w][:, 0:units[u][1]], RAW[r][:, 0:units[u][1]], ACT.Copy),
                            landed, used)
            unit_lo[u] = DV(lambda e: e.tensor_tensor(WL[w][:, 0:units[u][1]], RAW[r][:, 0:units[u][1]],
                                                      WH[w][:, 0:units[u][1]], ALU.subtract),
                            landed, used, unit_hi[u])
            weight_dma()

        for _ in range(RAW_SLOTS):
            weight_dma()

        def next_unit(src, n):
            u = len(units)
            units.append((src, n))
            while state["prep"] <= min(u + LOOK, UNITS_TOTAL - 1):
                weight_prep()
            return u

        def gemm_bank():
            b = state["bank"]
            state["bank"] = (b + 1) % GEMM_BANKS
            return b

        def gemm_tile(name, mt, in_h, in_l, ready, kt=None):
            kt = kt or FEATURE_MAJOR[name]
            b = gemm_bank()
            tok = None
            k0 = 0
            while k0 < kt:
                nk = min(8, kt - k0)
                u = next_unit(D[name][mt, :, k0 * 128:(k0 + nk) * 128], nk * 128)
                w = u % W_SLOTS
                for k in range(nk):
                    kk = k0 + k
                    sl = slice(k * 128, (k + 1) * 128)
                    for n, (wt, x) in enumerate(((WH[w], in_h), (WH[w], in_l), (WL[w], in_h))):
                        first = kk == 0 and n == 0
                        last = kk == kt - 1 and n == 2
                        end = k == nk - 1 and n == 2
                        waits = [ready[kk]] if n < 2 else []
                        if first:
                            waits += [bank_free[b]]
                        waits += [unit_hi[u]] if n == 0 else [unit_lo[u]] if n == 2 else []
                        tok = PE(lambda e, b=b, wt=wt, x=x, sl=sl, kk=kk, first=first, last=last:
                                 e.matmul(BANK[b][:, :], wt[:, sl], x[:, kk, :], start=first, stop=last),
                                 *waits, inc=end)
                unit_used[u] = tok
                k0 += nk
            return b, tok

        def gemm_tokens(name, c, in_h, in_l, ready):
            banks = [gemm_bank() for _ in range(4)]
            toks = [None] * 4
            for q in range(4):
                u = next_unit(D[name][c, :, q * 1024:(q + 1) * 1024], 1024)
                w = u % W_SLOTS
                for tt in range(4):
                    for k in range(2):
                        kk = 2 * q + k
                        sl = slice(k * 512, (k + 1) * 512)
                        for n, (wt, x) in enumerate(((WH[w], in_h), (WH[w], in_l), (WL[w], in_h))):
                            first = kk == 0 and n == 0
                            last = kk == 7 and n == 2
                            waits = [ready[kk]] + ([bank_free[banks[tt]]] if first else [])
                            waits += [unit_hi[u]] if n < 2 else [unit_lo[u]]
                            toks[tt] = PE(lambda e, b=banks[tt], wt=wt, x=x, sl=sl, kk=kk, tt=tt, first=first, last=last:
                                          e.matmul(BANK[b][:, :], x[:, kk, tt * 128:(tt + 1) * 128], wt[:, sl],
                                                   start=first, stop=last),
                                          *waits, inc=(k == 1 and n == 2))
                unit_used[u] = toks[3]
            return banks, toks

        background = []

        def tick(n=1):
            for _ in range(n):
                if background:
                    background.pop(0)()

        def flush():
            while background:
                background.pop(0)()

        st = {"acc": None, "sq": [None, None], "a_free": [], "rs_used": []}

        def square_in(f, src, ready):
            i = f % 2
            t = AC(lambda e: e.activation(SQ[i][:, :] if f else ACC[:, :], src, ACT.Square), *ready,
                   st["sq"][i], None if f else st.get("acc_read"), None if f else st["acc"])
            if f:
                st["acc"] = DV(lambda e: e.tensor_tensor(ACC[:, :], ACC[:, :], SQ[i][:, :], ALU.add), t, st["acc"])
                st["sq"][i] = st["acc"]
            else:
                st["acc"] = t
            return t

        def rms_scale():
            for tt in range(4):
                tok = PE(lambda e, tt=tt: e.matmul(BANK[4][:, tt:tt + 1], ACC[:, tt * 128:(tt + 1) * 128], ones[:, :],
                                                   start=True, stop=True),
                         st["acc"], bank_free[4], t_ones, inc=(tt == 3))
            st["acc_read"] = tok
            a = AC(lambda e: e.activation(rtok[:, 0:4], BANK[4][:, 0:4], ACT.Sqrt, bias=small[:, 63:64],
                                          scale=1.0 / 1024), tok, t_eps, st.get("rtok_read"))
            bank_free[4] = [a]
            r = DV(lambda e: e.reciprocal(rstok[:, :], rtok[:, 0:4]), a, st.get("rstok_read"), *st["rs_used"])
            st["rtok_read"] = r
            for tt in range(4):
                tok = PE(lambda e, tt=tt: e.matmul(BANK[5][:, tt * 128:(tt + 1) * 128],
                                                   rstok[:, tt:tt + 1].broadcast_to([128, 128]), ident[:, :],
                                                   start=True, stop=True),
                         r, bank_free[5], const_ready, inc=(tt == 3))
            st["rstok_read"] = tok
            c = DV(lambda e: e.tensor_copy(RS[:, :], BANK[5][:, :]), tok, *st["rs_used"])
            bank_free[5] = [c]
            st["rs_used"] = []
            return c

        def split_in(f, gain, ready, write_after=()):
            g = V(gain, f)
            h = AC(lambda e: e.activation(AH[:, f, :], XT[:, f, :], ACT.Copy, scale=g), *ready, const_ready,
                   *write_after)
            low = DV(lambda e: e.scalar_tensor_tensor(AL[:, f, :], XT[:, f, :], g, AH[:, f, :], ALU.mult,
                                                      ALU.subtract), h, *ready, *write_after)
            return [h, low]

        t_eps = DV(lambda e: e.memset(small[:, 63:64], EPS))

        a_ready = [None] * 8
        xt_read = [None] * 8

        def split_and_square(f, gain, ready):
            a_ready[f] = split_in(f, gain, ready, st["a_free"])
            xt_read[f] = [a_ready[f][1], square_in(f, XT[:, f, :], ready)]

        for f in range(8):
            split_and_square(f, "norm1", [x_ready])
        t_rs = rms_scale()

        with ExitStack() as ar:
            MH = sb("MH", [128, 8, S], F32R, ar)
            ML = sb("ML", [128, 8, S], F32R, ar)
            XP = [sb(f"XP{i}", [128, S + 3], stack=ar) for i in range(2)]
            LB = [[sb(f"LB{i}_{j}", [128, S], stack=ar) for j in range(5)] for i in range(2)]
            HL = sb("HL", [128, 4, S], stack=ar)
            QG = sb("QG", [128, 2, S], stack=ar)
            KG = sb("KG", [128, 2, S], stack=ar)
            BC = sb("BC", [128, 2, S], stack=ar)
            EG = sb("EG", [128, 2, S], stack=ar)
            KT = sb("KT", [128, 4, 256], stack=ar)
            VG = sb("VG", [128, 4, 512], stack=ar)
            SG = sb("SG", [128, 2, 8, 128], stack=ar)
            bd = sb("bd", [128, 8, 128], stack=ar)
            wal = sb("wal", [16, 256], stack=ar)
            DG = sb("DG", [128, 2, 8], stack=ar)
            s_bd = sem("s_bd")
            m_ready = [None] * 8

            z = DV(lambda e: e.memset(bd[:, :, :], 0.0))
            for i, name in enumerate(("lru_wa", "lru_wi")):
                for half in range(2):
                    rows = slice(64 * half, 64 * half + 64)
                    SP(lambda e, i=i, name=name, rows=rows, half=half: e.dma_start(
                        bd[rows, 4 * i:4 * i + 4, rows], D[name].rearrange("(f a) i j -> a i f j", a=2)[half])
                       .then_inc(s_bd, 16), z, inc=False)
            SP(lambda e: e.dma_start(wal[:, :], D["w_alpha"]).then_inc(s_bd, 16), inc=False)
            bd_ready = (s_bd, 80)
            for i in range(2):
                xp_zero = DV(lambda e, i=i: e.memset(XP[i][:, 0:3], 0.0))

            lam = V("lru_lambda", 0, 4)
            ab, ee, sden, ss, s2, pol, mx = (small[:, 4 * i:4 * i + 4] for i in range(7))
            cneg, cpos = small[:, 28:32], small[:, 32:36]
            t = AC(lambda e: e.activation(ab, lam, ACT.Abs), const_ready)
            t = AC(lambda e: e.activation(ee, ab, ACT.Exp, scale=-1.0), t)
            t = DV(lambda e: e.tensor_scalar(sden, ee, 2.0, None, ALU.add), t)
            t = DV(lambda e: e.reciprocal(sden, sden), t)
            t = DV(lambda e: e.tensor_tensor(ss, ee, sden, ALU.mult), t)
            t = DV(lambda e: e.tensor_tensor(s2, ss, ss, ALU.mult), t)
            t = DV(lambda e: e.tensor_scalar(pol, s2, 2.0 / 19, 2.0 / 17, ALU.mult, ALU.add), t)
            for d in (15, 13, 11, 9, 7, 5, 3, 1):
                t = DV(lambda e: e.tensor_tensor(pol, pol, s2, ALU.mult), t)
                t = DV(lambda e, d=d: e.tensor_scalar(pol, pol, 2.0 / d, None, ALU.add), t)
            t = DV(lambda e: e.tensor_tensor(pol, pol, ss, ALU.mult), t)
            t = DV(lambda e: e.tensor_scalar(mx, lam, -1.0, 0.0, ALU.mult, ALU.max), t, const_ready)
            t = DV(lambda e: e.tensor_tensor(mx, mx, pol, ALU.add), t)
            t = DV(lambda e: e.tensor_scalar(cpos, mx, 8.0, None, ALU.mult), t)
            t_c = DV(lambda e: e.tensor_scalar(cneg, mx, -8.0, None, ALU.mult), t)

            lru = {}
            lset_free = [[xp_zero], [xp_zero]]

            def lru_evac(f, b, tok):
                i = f % 2
                y = LB[i][0]
                t = DV(lambda e: e.tensor_tensor(XP[i][:, 3:S + 3], BANK[b][:, :], RS[:, :], ALU.mult), tok, t_rs,
                       *lset_free[i])
                bank_free[b] = [t]
                w = V("conv_w", 4 * f, 4)
                t = DV(lambda e: e.tensor_scalar(y[:, :], XP[i][:, 0:S], w[:, 0:1], V("conv_b", f), ALU.mult,
                                                 ALU.add), t, const_ready)
                for j in range(1, 4):
                    t = DV(lambda e, j=j: e.scalar_tensor_tensor(y[:, :], XP[i][:, j:j + S], w[:, j:j + 1], y[:, :],
                                                                 ALU.mult, ALU.add), t)
                lru[f] = t

            def lru_gates(f):
                i = f % 2
                y, r, g, a, tt = LB[i]
                ga = PE(lambda e: e.matmul(BANK[6][:, :], bd[:, f, :], y[:, :], start=True, stop=True), lru[f],
                        bank_free[6], bd_ready)
                gi = PE(lambda e: e.matmul(BANK[7][:, :], bd[:, 4 + f, :], y[:, :], start=True, stop=True),
                        bank_free[7])
                tr = AC(lambda e: e.activation(r[:, :], BANK[6][:, :], ACT.Sigmoid, bias=V("lru_ba", f)), ga,
                        *lset_free[i])
                ti = AC(lambda e: e.activation(g[:, :], BANK[7][:, :], ACT.Sigmoid, bias=V("lru_bi", f)), gi)
                bank_free[6], bank_free[7] = [tr], [ti]
                lru[f] = (tr, ti)

            def lru_decay(f):
                i = f % 2
                y, r, g, a, tt = LB[i]
                tr, ti = lru[f]
                ta = AC(lambda e: e.activation(a[:, :], r[:, :], ACT.Exp, scale=cneg[:, f:f + 1]), tr, t_c)
                th = AC(lambda e: e.activation(tt[:, :], r[:, :], ACT.Tanh, scale=cpos[:, f:f + 1]))
                d1 = DV(lambda e: e.tensor_tensor(g[:, :], g[:, :], y[:, :], ALU.mult), ti)
                d2 = DV(lambda e: e.tensor_tensor(r[:, :], a[:, :], a[:, :], ALU.mult), ta, th)
                d3 = DV(lambda e: e.scalar_tensor_tensor(r[:, :], r[:, :], 1.0, tt[:, :], ALU.add, ALU.mult), d2)
                lru[f] = (d1, d3)

            def lru_scan(f):
                i = f % 2
                y, r, g, a, tt = LB[i]
                d1, d3 = lru[f]
                t = AC(lambda e: e.activation(tt[:, :], r[:, :], ACT.Sqrt), d3)
                t = DV(lambda e: e.tensor_tensor(g[:, :], g[:, :], tt[:, :], ALU.mult), t, d1)
                t = DV(lambda e: e.tensor_tensor_scan(HL[:, f, :], a[:, :], g[:, :], 0.0, ALU.mult, ALU.add), t)
                lset_free[i] = [t]
                lru[f] = t

            tfree = [[] for _ in range(4)]

            def lru_out_evac(f, b, tok):
                i = f % 4
                t = DV(lambda e: e.tensor_tensor(T[i][:, :], BANK[b][:, :], RS[:, :], ALU.mult), tok, t_rs, *tfree[i])
                bank_free[b] = [t]
                tg = AC(lambda e: e.activation(T[i][:, :], T[i][:, :], ACT.Gelu_apprx_tanh), t)

                def rest():
                    t = DV(lambda e: e.tensor_tensor(T[i][:, :], T[i][:, :], HL[:, f, :], ALU.mult), tg, lru[f])
                    h = AC(lambda e: e.activation(MH[:, f, :], T[i][:, :], ACT.Copy), t)
                    low = DV(lambda e: e.tensor_tensor(ML[:, f, :], T[i][:, :], MH[:, f, :], ALU.subtract), h)
                    tfree[i] = [low]
                    m_ready[f] = [h, low]
                    hl_read.append(t)
                return rest

            hl_read = []
            for f in range(4):
                b, tok = gemm_tile("w_in_t", f, AH, AL, a_ready)
                tick()
                lru_evac(f, b, tok)
                background.append(lambda f=f: lru_gates(f))
                background.append(lambda f=f: lru_decay(f))
                background.append(lambda f=f: lru_scan(f))
                if f >= 1:
                    tick(1 if f == 1 else 3)
                    if f == 1:
                        tick(2)
            qk = {}
            for f in range(4):
                b, tok = gemm_tile("w_in_t", 8 + f, AH, AL, a_ready)
                tick()
                dst = (QG if f < 2 else KG)[:, f % 2, :]
                qk[f] = DV(lambda e, b=b, dst=dst, c=(0.125 if f < 2 else 1.0): e.scalar_tensor_tensor(
                    dst, BANK[b][:, :], c, RS[:, :], ALU.mult, ALU.mult), tok, t_rs)
                bank_free[b] = [qk[f]]
                tick()
            b, tok = gemm_tile("w_in_t", 16, AH, AL, a_ready)
            flush()
            ZT = T[0]
            tz = DV(lambda e, b=b: e.tensor_tensor(ZT[0:16, :], BANK[b][0:16, :], RS[0:16, :], ALU.mult), tok, t_rs,
                    *tfree[0])
            bank_free[b] = [tz]
            msk = T[3]
            tm = DV(lambda e: e.memset(msk[:, :], 1.0), *tfree[3])
            tm = DV(lambda e: e.memset(msk[:, 0:S:64], 0.0), tm)

            def gla_decay_1():
                for f in range(2):
                    zf = PE(lambda e, f=f: e.matmul(BANK[6 + f][:, :], wal[:, f * 128:(f + 1) * 128], ZT[0:16, :],
                                                    start=True, stop=True), tz, bd_ready, bank_free[6 + f])
                    za = AC(lambda e, f=f: e.activation(BC[:, f, :], BANK[6 + f][:, :], ACT.Identity,
                                                        bias=V("b_alpha", f)), zf)
                    bank_free[6 + f] = [za]
                    ab_ = AC(lambda e, f=f: e.activation(EG[:, f, :], BC[:, f, :], ACT.Abs), za)
                    ex = AC(lambda e, f=f: e.activation(EG[:, f, :], EG[:, f, :], ACT.Exp, scale=-1.0), ab_)
                    qk["l", f] = AC(lambda e, f=f: e.activation(EG[:, f, :], EG[:, f, :], ACT.Ln, bias=1.0), ex)
                tfree[0] = [zf]

            def gla_decay_2():
                for f in range(2):
                    la = DV(lambda e, f=f: e.scalar_tensor_tensor(EG[:, f, :], BC[:, f, :], 0.0, EG[:, f, :],
                                                                  ALU.min, ALU.subtract), qk["l", f])
                    bc = DV(lambda e, f=f: e.tensor_tensor_scan(BC[:, f, :], msk[:, :], EG[:, f, :], 0.0, ALU.mult,
                                                                ALU.add), la, tm)
                    bcv = BC[:, f, :].rearrange("p (c t) -> p c t", t=64)
                    egv = EG[:, f, :].rearrange("p (c t) -> p c t", t=64)
                    df = DV(lambda e, bcv=bcv, egv=egv: e.tensor_tensor(
                        egv, bcv[:, :, 63:64].broadcast_to([128, 8, 64]), bcv, ALU.subtract), bc)
                    qk["d", f] = AC(lambda e, f=f, bcv=bcv: e.activation(DG[:, f, :], bcv[:, :, 63], ACT.Exp,
                                                                        scale=1.0 / 16), bc)
                    ex = AC(lambda e, f=f: e.activation(EG[:, f, :], EG[:, f, :], ACT.Exp, scale=1.0 / 16), df)
                    qk["k", f] = DV(lambda e, f=f: e.tensor_tensor(KG[:, f, :], KG[:, f, :], EG[:, f, :], ALU.mult),
                                    ex, qk[2 + f])
                tfree[3] = [bc]

            def gla_turn():
                for f in range(2):
                    for tt in range(4):
                        tp = PE(lambda e, f=f, tt=tt: e.transpose(BANK[6 + f][:, tt * 128:(tt + 1) * 128],
                                                                  KG[:, f, tt * 128:(tt + 1) * 128], ident[:, :]),
                                qk["k", f], bank_free[6 + f], const_ready, inc=(tt == 3))
                    qk["t", f] = AC(lambda e, f=f: e.activation(
                        KT[:, :, f * 128:(f + 1) * 128], BANK[6 + f][:, :].rearrange("p (a b) -> p a b", b=128),
                        ACT.Copy), tp)
                    bank_free[6 + f] = [qk["t", f]]

            background += [gla_decay_1, gla_decay_2, gla_turn]

            late = []
            for f in range(4):
                b, tok = gemm_tile("w_in_t", 4 + f, AH, AL, a_ready)
                tick()
                for fn in late:
                    fn()
                late = [lru_out_evac(f, b, tok)]
            banks, toks = gemm_tokens("w_in_v", 0, AH, AL, a_ready)
            for fn in late:
                fn()
            flush()
            tv = []
            for tt in range(4):
                tv.append(AC(lambda e, tt=tt, b=banks[tt]: e.activation(VG[:, tt, :], BANK[b][:, :], ACT.Copy,
                                                                        scale=rstok[:, tt:tt + 1]), toks[tt], t_rs))
                bank_free[banks[tt]] = [tv[tt]]
            st["rs_used"].append(tv[3])

            def gla_update(pr):
                for c in range(8):
                    tt, row = c // 2, 64 * (c % 2)
                    b = 4 + (c % 2)
                    for hh in range(2):
                        h = 2 * pr + hh
                        tok = PE(lambda e, c=c, tt=tt, row=row, b=b, hh=hh, h=h: e.matmul(
                            BANK[b][64 * hh:64 * hh + 64, (c // 2) * 128:(c // 2) * 128 + 128],
                            KT[row:row + 64, tt, h * 64:h * 64 + 64], VG[row:row + 64, tt, h * 128:h * 128 + 128],
                            start=True, stop=True), qk["t", pr], tv[tt], bank_free[b], inc=(c >= 6 and hh == 1))
                    if c >= 6:
                        qk["u", pr, c % 2] = tok
                prev = None
                for c in range(8):
                    b = 4 + (c % 2)
                    src = BANK[b][:, (c // 2) * 128:(c // 2) * 128 + 128]
                    if c == 0:
                        prev = DV(lambda e, src=src: e.tensor_copy(SG[:, pr, 0, :], src), qk["u", pr, 0])
                    else:
                        prev = DV(lambda e, src=src, c=c: e.scalar_tensor_tensor(
                            SG[:, pr, c, :], SG[:, pr, c - 1, :], DG[:, pr, c:c + 1], src, ALU.mult, ALU.add),
                            prev, qk["u", pr, c % 2], qk["d", pr])
                bank_free[4] = [prev]
                bank_free[5] = [prev]
                qk["s", pr] = prev

            def gla_out(pr):
                for hh in range(2):
                    h = 2 * pr + hh
                    for c in range(8):
                        tok = PE(lambda e, c=c, hh=hh: e.matmul(
                            BANK[6 + hh][:, c * 64:c * 64 + 64], SG[64 * hh:64 * hh + 64, pr, c, :],
                            QG[64 * hh:64 * hh + 64, pr, c * 64:c * 64 + 64], start=True, stop=True),
                            qk["s", pr], bank_free[6 + hh], qk[pr], inc=(c == 7))
                    i = h % 2
                    to = AC(lambda e, h=h, hh=hh: e.activation(HL[:, h, :], BANK[6 + hh][:, :], ACT.Copy,
                                                               scale=V("gla_norm")), tok, *hl_read)
                    ts = AC(lambda e, i=i, hh=hh: e.activation(SQ[i][:, :], BANK[6 + hh][:, :], ACT.Square), to,
                            st["sq"][i])
                    bank_free[6 + hh] = [ts]
                    for tt in range(4):
                        tok = PE(lambda e, h=h, tt=tt, i=i: e.matmul(
                            BANK[4][:, 4 * h + tt:4 * h + tt + 1], SQ[i][:, tt * 128:(tt + 1) * 128], ones[:, :],
                            start=True, stop=True), ts, bank_free[4], inc=(tt == 3))
                    st["sq"][i] = tok
                    qk["o", h] = to
                    qk["n", h] = tok

            def gla_scale():
                a = AC(lambda e: e.activation(rtok[:, 0:16], BANK[4][:, 0:16], ACT.Sqrt, bias=small[:, 63:64],
                                              scale=1.0 / 128), qk["n", 3], st.get("rtok_read"))
                bank_free[4] = [a]
                r = DV(lambda e: e.reciprocal(rso[:, :], rtok[:, 0:16]), a)
                st["rtok_read"] = r
                qk["r"] = r

            def gla_norm_out(h):
                bb = 5 + h % 2
                for tt in range(4):
                    tok = PE(lambda e, tt=tt: e.matmul(
                        BANK[bb][:, tt * 128:(tt + 1) * 128],
                        rso[:, 4 * h + tt:4 * h + tt + 1].broadcast_to([128, 128]), ident[:, :], start=True,
                        stop=True), qk["r"], bank_free[bb], inc=(tt == 3))
                qk["y", h] = DV(lambda e: e.tensor_tensor(HL[:, h, :], HL[:, h, :], BANK[bb][:, :], ALU.mult), tok,
                                qk["o", h])
                bank_free[bb] = [qk["y", h]]

            background += [lambda: gla_update(0), lambda: gla_update(1), lambda: gla_out(0), lambda: gla_out(1)]
            late = []

            def silu_gate(h, b, tok):
                i = h % 4
                t = DV(lambda e: e.tensor_tensor(T[i][:, :], BANK[b][:, :], RS[:, :], ALU.mult), tok, *tfree[i])
                bank_free[b] = [t]
                ts = AC(lambda e: e.activation(T[i][:, :], T[i][:, :], ACT.Silu), t)
                st["rs_used"].append(t)

                def rest():
                    t = DV(lambda e: e.tensor_tensor(T[i][:, :], T[i][:, :], HL[:, h, :], ALU.mult), ts, qk["y", h])
                    hi = AC(lambda e: e.activation(MH[:, 4 + h, :], T[i][:, :], ACT.Copy), t)
                    low = DV(lambda e: e.tensor_tensor(ML[:, 4 + h, :], T[i][:, :], MH[:, 4 + h, :], ALU.subtract),
                             hi)
                    tfree[i] = [low]
                    m_ready[4 + h] = [hi, low]
                return rest

            for h in range(4):
                b, tok = gemm_tile("w_in_t", 12 + h, AH, AL, a_ready)
                tick()
                late.append(silu_gate(h, b, tok))
            st["a_free"] = [PE.now()]
            flush()
            gla_scale()
            for h in range(4):
                gla_norm_out(h)
            for fn in late:
                fn()

            def residual_mix1(f, b, tok):
                t = DV(lambda e: e.tensor_tensor(XT[:, f, :], XT[:, f, :], BANK[b][:, :], ALU.add), tok, *xt_read[f])
                bank_free[b] = [t]
                split_and_square(f, "norm2", [t])

            for f in range(8):
                b, tok = gemm_tile("w_out", f, MH, ML, m_ready)
                residual_mix1(f, b, tok)
        F = fence()
        st["rs_used"] = []

        def ffn_layer(names, finish, tag):
            fence_in = fence()
            with ExitStack() as ar:
                HH = sb("HH" + tag, [128, 22, S], F32R, ar)
                HLO = sb("HLO" + tag, [128, 22, S], F32R, ar)
                h_ready = [None] * 22
                late = []

                def pair(j, bg, tg, bu, tu):
                    a, c = T[2 * (j % 2)], T[2 * (j % 2) + 1]
                    fa, fc = tfree[2 * (j % 2)], tfree[2 * (j % 2) + 1]
                    t1 = DV(lambda e: e.tensor_tensor(a[:, :], BANK[bg][:, :], RS[:, :], ALU.mult), tg, st["rs"], *fa)
                    bank_free[bg] = [t1]
                    t2 = AC(lambda e: e.activation(a[:, :], a[:, :], ACT.Silu), t1)
                    t3 = DV(lambda e: e.tensor_tensor(c[:, :], BANK[bu][:, :], RS[:, :], ALU.mult), tu, *fc)
                    bank_free[bu] = [t3]
                    st["rs_used"] = [t3]

                    def rest():
                        t4 = DV(lambda e: e.tensor_tensor(a[:, :], a[:, :], c[:, :], ALU.mult), t2, t3)
                        hi = AC(lambda e: e.activation(HH[:, j, :], a[:, :], ACT.Copy), t4, *fence_in)
                        low = DV(lambda e: e.tensor_tensor(HLO[:, j, :], a[:, :], HH[:, j, :], ALU.subtract), hi,
                                 *fence_in)
                        tfree[2 * (j % 2)] = [low]
                        tfree[2 * (j % 2) + 1] = [t4]
                        h_ready[j] = [hi, low]
                    return rest

                for j in range(22):
                    bg, tg = gemm_tile(names[0], 2 * j, AH, AL, a_ready)
                    if j == 0:
                        st["rs"] = rms_scale()
                    for fn in late:
                        fn()
                    bu, tu = gemm_tile(names[0], 2 * j + 1, AH, AL, a_ready)
                    late = [pair(j, bg, tg, bu, tu)]
                st["a_free"] = [PE.now()]
                for fn in late:
                    fn()
                for f in range(8):
                    b, tok = gemm_tile(names[1], f, HH, HLO, h_ready)
                    finish(f, b, tok)

        def finish_block1(f, b, tok):
            t = DV(lambda e: e.tensor_tensor(XT[:, f, :], XT[:, f, :], BANK[b][:, :], ALU.add), tok, *xt_read[f])
            bank_free[b] = [t]
            final["x", f] = [t, square_in(f, XT[:, f, :], [t])]

        final = {}
        ffn_layer(("ffn1_in", "ffn1_out"), finish_block1, "1")
        st["rs"] = rms_scale()
        for f in range(8):
            t = DV(lambda e, f=f: e.scalar_tensor_tensor(XT[:, f, :], XT[:, f, :], V("final_norm", f), RS[:, :],
                                                         ALU.mult, ALU.mult), final["x", f], st["rs"])
            st["rs_used"] = [t]
            split_and_square(f, "mix_pre0", [t])

        def post_norm(M, m_tok, post, pre):
            rs = rms_scale()
            for f in range(8):
                t = DV(lambda e, f=f: e.scalar_tensor_tensor(M[:, f, :], M[:, f, :], V(post, f), RS[:, :], ALU.mult,
                                                             ALU.mult), m_tok[f], st["acc_read"], rs)
                st["rs_used"] = [t]
                t = DV(lambda e, f=f: e.tensor_tensor(XT[:, f, :], XT[:, f, :], M[:, f, :], ALU.add), t, *xt_read[f])
                final["h", f] = t
                if pre:
                    split_and_square(f, pre, [t])

        def branch_out(M, m_tok, b, tok, f, after=()):
            t = AC(lambda e: e.activation(M[:, f, :], BANK[b][:, :], ACT.Copy), tok, *after)
            bank_free[b] = [t]
            m_tok[f] = t
            square_in(f, M[:, f, :], [t])

        fence_in = fence()
        with ExitStack() as ar:
            RH = sb("RH", [128, 16, S], F32R, ar)
            RL = sb("RL", [128, 16, S], F32R, ar)
            CS = sb("CS", [128, 2, S], stack=ar)
            DEC = sb("DEC", [128, S], stack=ar)
            s_cs, s_dec = sem("s_cs"), sem("s_dec")
            PO(lambda e: e.dma_start(CS[:, :, :], D["cossin"].rearrange("p (a t) -> p a t", a=2)).then_inc(s_cs, 16),
               *fence_in, inc=False)
            r_ready = [None] * 16
            with ExitStack() as ar2:
                QR = sb("QR", [128, 2, S], stack=ar2)
                KR = sb("KR", [128, 2, S], stack=ar2)
                VR = sb("VR", [128, 4, 512], stack=ar2)
                OR = sb("OR", [128, 4, S], stack=ar2)
                ST = [sb(f"ST{j}", [128, S - 128 * j], stack=ar2) for j in range(4)]
                q_read, v_read, st_read, dec_read, or_read = [], [], [None] * 4, [], []
                ret = {}

                def rotate(h, dst, b0, t0, b1, t1):
                    rd = list(q_read)
                    d = [DV(lambda e: e.tensor_tensor(T[0][:, :], BANK[b0][:, :], CS[:, 0, :], ALU.mult), t0,
                            ret["cs"], *tfree[0]),
                         DV(lambda e: e.tensor_tensor(T[1][:, :], BANK[b0][:, :], CS[:, 1, :], ALU.mult), *tfree[1])]
                    bank_free[b0] = [d[1]]
                    d += [DV(lambda e: e.tensor_tensor(T[2][:, :], BANK[b1][:, :], CS[:, 1, :], ALU.mult), t1,
                             *tfree[2]),
                          DV(lambda e: e.tensor_tensor(T[3][:, :], BANK[b1][:, :], CS[:, 0, :], ALU.mult),
                             *tfree[3])]
                    bank_free[b1] = [d[3]]
                    e0 = DV(lambda e: e.tensor_tensor(dst[:, 0, :], T[0][:, :], T[2][:, :], ALU.subtract), d[2], *rd,
                            *fence_in)
                    e1 = DV(lambda e: e.tensor_tensor(dst[:, 1, :], T[1][:, :], T[3][:, :], ALU.add), d[3], *rd)
                    tfree[0], tfree[2] = [e0], [e0]
                    tfree[1], tfree[3] = [e1], [e1]
                    return e1

                def heads_qkv(h):
                    b0, t0 = gemm_tile("ret_t", 8 * h, AH, AL, a_ready)
                    if h == 0:
                        st["rs"] = rms_scale()
                        c = DV(lambda e: e.tensor_tensor(CS[:, 0, :], CS[:, 0, :], RS[:, :], ALU.mult), st["rs"],
                               (s_cs, 16))
                        ret["cs"] = DV(lambda e: e.tensor_tensor(CS[:, 1, :], CS[:, 1, :], RS[:, :], ALU.mult), c)
                    b1, t1 = gemm_tile("ret_t", 8 * h + 1, AH, AL, a_ready)
                    ret["q"] = rotate(h, QR, b0, t0, b1, t1)
                    b0, t0 = gemm_tile("ret_t", 8 * h + 2, AH, AL, a_ready)
                    b1, t1 = gemm_tile("ret_t", 8 * h + 3, AH, AL, a_ready)
                    ret["k"] = rotate(h, KR, b0, t0, b1, t1)
                    banks, toks = gemm_tokens("ret_v", h, AH, AL, a_ready)
                    ret["v"] = []
                    for tt in range(4):
                        ret["v"].append(AC(lambda e, tt=tt, b=banks[tt]: e.activation(
                            VR[:, tt, :], BANK[b][:, :], ACT.Copy, scale=rstok[:, tt:tt + 1]), toks[tt], st["rs"],
                            *v_read, *fence_in))
                        bank_free[banks[tt]] = [ret["v"][tt]]
                    PO(lambda e: e.dma_start(DEC[:, :], D["decay"][h]).then_inc(s_dec, 16), *dec_read, *fence_in,
                       inc=False)
                    ret["dec"] = (s_dec, 16 * (h + 1))

                def scores(h):
                    for j in range(4):
                        n = S - 128 * j
                        b = gemm_bank()
                        for d in range(2):
                            tok = PE(lambda e, d=d, j=j, n=n, b=b: e.matmul(
                                BANK[b][:, 0:n], KR[:, d, j * 128:(j + 1) * 128], QR[:, d, j * 128:S],
                                start=(d == 0), stop=(d == 1)), ret["q"], ret["k"], bank_free[b], inc=(d == 1))
                        ret["s", j] = DV(lambda e, j=j, n=n, b=b: e.tensor_tensor(
                            ST[j][:, :], BANK[b][:, 0:n], DEC[:, 0:n], ALU.mult), tok, ret["dec"], st_read[j],
                            *fence_in)
                        bank_free[b] = [ret["s", j]]
                    q_read[:] = [tok]
                    dec_read[:] = [ret["s", 3]]

                def values(h):
                    for j in range(4):
                        n = S - 128 * j
                        for et in range(4):
                            tok = PE(lambda e, et=et, j=j, n=n: e.matmul(
                                BANK[4 + et][:, j * 128:S], VR[:, j, et * 128:(et + 1) * 128], ST[j][:, :],
                                start=(j == 0), stop=(j == 3)), ret["s", j], ret["v"][j],
                                bank_free[4 + et] if j == 0 else None, inc=(j == 3 or et == 3))
                            if j == 3:
                                ret["o", et] = tok
                        st_read[j] = tok
                    v_read[:] = [tok]
                    for et in range(4):
                        ret["oc", et] = AC(lambda e, et=et: e.activation(OR[:, et, :], BANK[4 + et][:, :], ACT.Copy),
                                           ret["o", et], *or_read, *fence_in)
                        bank_free[4 + et] = [ret["oc", et]]

                def head_norm(h):
                    for et in range(4):
                        square_in(et, OR[:, et, :], [ret["oc", et]])
                    for tt in range(4):
                        tok = PE(lambda e, tt=tt: e.matmul(BANK[4][:, tt:tt + 1], ACC[:, tt * 128:(tt + 1) * 128],
                                                           ones[:, :], start=True, stop=True),
                                 st["acc"], bank_free[4], inc=(tt == 3))
                    st["acc_read"] = tok
                    a = AC(lambda e: e.activation(rtok[:, 0:4], BANK[4][:, 0:4], ACT.Sqrt, bias=small[:, 63:64],
                                                  scale=1.0 / 512), tok, st.get("rtok_read"))
                    bank_free[4] = [a]
                    r = DV(lambda e: e.reciprocal(rso[:, 0:4], rtok[:, 0:4]), a, ret.get("rso_read"))
                    st["rtok_read"] = r
                    ret["rso"] = r

                def head_norm_spread(h):
                    for tt in range(4):
                        tok = PE(lambda e, tt=tt: e.matmul(
                            BANK[5][:, tt * 128:(tt + 1) * 128], rso[:, tt:tt + 1].broadcast_to([128, 128]),
                            ident[:, :], start=True, stop=True), ret["rso"], bank_free[5], inc=(tt == 3))
                    ret["rso_read"] = tok
                    for et in range(4):
                        ret["on", et] = DV(lambda e, et=et: e.tensor_tensor(OR[:, et, :], OR[:, et, :],
                                                                           BANK[5][:, :], ALU.mult), tok,
                                           st["acc"], ret["oc", et])
                    bank_free[5] = [ret["on", 3]]

                def gate_evac(h, et, b, tok):
                    i = et % 4
                    t = DV(lambda e: e.tensor_tensor(T[i][:, :], BANK[b][:, :], RS[:, :], ALU.mult), tok, *tfree[i])
                    bank_free[b] = [t]
                    st["rs_used"] = [t, ret["v"][3]]
                    ts = AC(lambda e: e.activation(T[i][:, :], T[i][:, :], ACT.Silu), t)

                    def rest():
                        k = 4 * h + et
                        t = DV(lambda e: e.tensor_tensor(T[i][:, :], T[i][:, :], OR[:, et, :], ALU.mult), ts,
                               ret["on", et])
                        hi = AC(lambda e: e.activation(RH[:, k, :], T[i][:, :], ACT.Copy), t, *fence_in)
                        low = DV(lambda e: e.tensor_tensor(RL[:, k, :], T[i][:, :], RH[:, k, :], ALU.subtract), hi,
                                 *fence_in)
                        tfree[i] = [low]
                        r_ready[k] = [hi, low]
                        or_read[:] = [t]
                    return rest

                for h in range(4):
                    heads_qkv(h)
                    scores(h)
                    background += [lambda h=h: values(h), lambda h=h: head_norm(h), lambda h=h: head_norm_spread(h)]
                    late = []
                    for et in range(4):
                        b, tok = gemm_tile("ret_t", 8 * h + 4 + et, AH, AL, a_ready)
                        tick()
                        late.append(gate_evac(h, et, b, tok))
                    for fn in late:
                        fn()
                st["a_free"] = [PE.now()]
            fence_m = fence()
            MR = sb("MR", [128, 8, S], stack=ar)
            m_tok = [None] * 8
            for f in range(8):
                b, tok = gemm_tile("ret_out", f, RH, RL, r_ready)
                branch_out(MR, m_tok, b, tok, f, fence_m)
            post_norm(MR, m_tok, "mix_post0", "ffn_pre0")

        def ffn_block2(names, post, pre, tag):
            fence_m = fence()
            with ExitStack() as am:
                MF = sb("MF" + tag, [128, 8, S], stack=am)
                m_tok = [None] * 8
                ffn_layer(names, lambda f, b, tok: branch_out(MF, m_tok, b, tok, f, fence_m), tag)
                post_norm(MF, m_tok, post, pre)

        ffn_block2(("ffn2_in", "ffn2_out"), "ffn_post0", "kv_norm", "2")

        fence_in = fence()
        with ExitStack() as ar:
            TT = sb("TT", [128, 16, S], stack=ar)
            KS = sb("KS", [128, 2, S], stack=ar)
            KW = sb("KW", [128, 2, S], stack=ar)
            VS = sb("VS", [128, 4, 512], stack=ar)
            GT = sb("GT", [128, 4, 48], stack=ar)
            KC = sb("KC", [128, 2, 32], stack=ar)
            VC = sb("VC", [32, 4, 64], stack=ar)
            s_bias, s_w1, s_w2, s_tt, s_scr = (sem(n) for n in ("s_bias", "s_w1", "s_w2", "s_tt", "s_scr"))
            at = {}
            with ExitStack() as ac:
                CK = sb("CK", [128, 4, S], stack=ac)
                X2 = sb("X2", [128, 16, 124], stack=ac)
                W1 = sb("W1", [128, 16, 256], stack=ac)
                HC = sb("HC", [128, 2, 124], stack=ac)
                W2 = sb("W2", [128, 2, 2, 64], stack=ac)
                OH = sb("OH", [32, 656], stack=ac)
                BV = sb("BV", [16, 640], stack=ac)
                MK = sb("MK", [16, 640], stack=ac)
                PO(lambda e: e.dma_start(OH[:, :], D["onehot"]).then_inc(s_bias, 16), *fence_in, inc=False)
                PO(lambda e: e.dma_start(MK[:, :], D["future"]).then_inc(s_bias, 16), inc=False)
                PO(lambda e: e.dma_start(W2[:, :, :, :], D["cmp_w2"]).then_inc(s_w2, 16), inc=False)
                PO(lambda e: e.dma_start(W1[:, :, :], D["cmp_w1"][0]).then_inc(s_w1, 16), inc=False)
                for n in range(2):
                    cols = slice(320 * n, 320 * n + 320)
                    t = PE(lambda e, n=n, cols=cols: e.matmul(BANK[6 + n][0:16, 0:320], OH[:, 640:656], OH[:, cols],
                                                              start=True, stop=True), (s_bias, 32), bank_free[6 + n])
                    t = DV(lambda e, n=n, cols=cols: e.tensor_tensor(BV[:, cols], BANK[6 + n][0:16, 0:320],
                                                                     MK[:, cols], ALU.add), t, (s_bias, 32),
                           *fence_in)
                    bank_free[6 + n] = [t]
                PO(lambda e: e.dma_start(D["scratch"], BV[:, :]).then_inc(s_scr, 16), t, inc=False)
                PO(lambda e: e.dma_start(TT[:, :, :], bass.AP(D["scratch"].tensor, 0, [[1, 128], [640, 16], [1, 512]]))
                   .then_inc(s_tt, 16), (s_scr, 16), inc=False)

                for n in range(8):
                    b, tok = gemm_tile("kv_t", n, AH, AL, a_ready)
                    if n == 0:
                        st["rs"] = rms_scale()
                    dst = CK[:, n, :] if n < 4 else (KS if n < 6 else KW)[:, n % 2, :]
                    t = DV(lambda e, b=b, dst=dst: e.tensor_tensor(dst, BANK[b][:, :], RS[:, :], ALU.mult), tok,
                           st["rs"], *fence_in)
                    bank_free[b] = [t]
                    at["kv", n] = t

                def spread(i):
                    for g in range(4):
                        for par in range(2):
                            src = CK[64 * (g % 2):64 * (g % 2) + 64, 2 * i + g // 2, :]
                            win = bass.AP(src.tensor, src.offset + par, [src.ap[0], [2, 16], [16, 31]])
                            t = DV(lambda e, g=g, par=par, win=win: e.tensor_copy(
                                X2[64 * par:64 * par + 64, :, 31 * g:31 * g + 31], win), at["kv", 2 * i + g // 2],
                                at.get("hid"), *fence_in)
                    pe = V("pe_k" if i == 0 else "pe_v", 0, 16).rearrange("p (l o) -> p l o", o=1)
                    at["x2"] = DV(lambda e: e.tensor_tensor(X2[:, :, :], X2[:, :, :],
                                                            pe.broadcast_to([128, 16, 124]), ALU.add), t)

                def hidden(i):
                    for ht in range(2):
                        for lp in range(16):
                            t = PE(lambda e, ht=ht, lp=lp: e.matmul(
                                BANK[4 + ht][:, 0:124], W1[:, lp, ht * 128:ht * 128 + 128], X2[:, lp, :],
                                start=(lp == 0), stop=(lp == 15)), at["x2"], (s_w1, 16 * (i + 1)),
                                bank_free[4 + ht], inc=(lp == 15))
                        at["hc", ht] = AC(lambda e, ht=ht: e.activation(HC[:, ht, :], BANK[4 + ht][:, 0:124], ACT.Silu),
                                          t, at.get("hc_read"), *fence_in)
                        bank_free[4 + ht] = [at["hc", ht]]
                    at["hid"] = t
                    if i == 0:
                        PO(lambda e: e.dma_start(W1[:, :, :], D["cmp_w1"][1]).then_inc(s_w1, 16), t, inc=False)

                def compressed(i):
                    b = 6 + i
                    for g in range(4):
                        for ht in range(2):
                            if i == 0:
                                row = 64 * (g % 2)
                                t = PE(lambda e, g=g, ht=ht, row=row: e.matmul(
                                    BANK[b][row:row + 64, 32 * (g // 2):32 * (g // 2) + 31], W2[:, 0, ht, :],
                                    HC[:, ht, 31 * g:31 * g + 31], start=(ht == 0), stop=(ht == 1)),
                                    at["hc", ht], (s_w2, 16), bank_free[b], inc=(g == 3 and ht == 1))
                            else:
                                t = PE(lambda e, g=g, ht=ht: e.matmul(
                                    BANK[b][0:31, 64 * g:64 * g + 64], HC[:, ht, 31 * g:31 * g + 31],
                                    W2[:, 1, ht, :], start=(ht == 0), stop=(ht == 1)),
                                    at["hc", ht], (s_w2, 16), bank_free[b], inc=(g == 3 and ht == 1))
                    at["hc_read"] = t
                    if i == 0:
                        t = DV(lambda e: e.tensor_copy(KC[:, :, 0:31], BANK[b][:, 0:64].rearrange(
                            "p (a n) -> p a n", a=2)[:, :, 0:31]), t, *fence_in)
                        at["kc"] = t
                    else:
                        t = DV(lambda e: e.tensor_copy(VC[0:31, :, :], BANK[b][0:31, 0:256].rearrange(
                            "p (g d) -> p g d", g=4)), t, *fence_in)
                        at["vc"] = t
                    bank_free[b] = [t]

                spread(0)
                banks, toks = gemm_tokens("kv_v", 0, AH, AL, a_ready)
                st["a_free"] = [PE.now()]
                at["v"] = []
                for tt in range(4):
                    at["v"].append(AC(lambda e, tt=tt, b=banks[tt]: e.activation(
                        VS[:, tt, :], BANK[b][:, :], ACT.Copy, scale=rstok[:, tt:tt + 1]), toks[tt], st["rs"],
                        *fence_in))
                    bank_free[banks[tt]] = [at["v"][tt]]
                for f in range(8):
                    a_ready[f] = split_in(f, "mix_pre1", [final["h", f]], st["a_free"])
                    xt_read[f] = [xt_read[f], a_ready[f]]
                hidden(0)
                spread(1)
                compressed(0)
                hidden(1)
                compressed(1)
            fence_q = fence()
            QN = sb("QN", [128, 8, S], stack=ar)
            OT = sb("OT", [128, 4, 1024], stack=ar)
            SS = [sb(f"SS{i}", [128, S], stack=ar) for i in range(3)]
            PT = [sb(f"PT{i}", [128, S], stack=ar) for i in range(3)]
            NM = sb("NM", [128, 8], stack=ar)
            SM = sb("SM", [128, 2, 4], stack=ar)
            CF = sb("CF", [128, 2, 4], stack=ar)
            fence_w1 = (s_w1, 32)

            b, tok = gemm_tile("nsa_t", 8, AH, AL, a_ready)
            t = DV(lambda e, b=b: e.tensor_tensor(T[0][0:48, :], BANK[b][0:48, :], RS[0:48, :], ALU.mult), tok,
                   st["rs"], *tfree[0])
            bank_free[b] = [t]
            t_sig = AC(lambda e: e.activation(T[0][0:48, :], T[0][0:48, :], ACT.Sigmoid), t)
            for n in range(8):
                b, tok = gemm_tile("nsa_t", n, AH, AL, a_ready)
                t = DV(lambda e, n=n, b=b: e.scalar_tensor_tensor(QN[:, n, :], BANK[b][:, :], 0.125, RS[:, :],
                                                                  ALU.mult, ALU.mult), tok, st["rs"], *fence_q,
                       fence_w1)
                bank_free[b] = [t]
                at["q", n] = t
                if n == 0:
                    for tt in range(4):
                        tok = PE(lambda e, tt=tt: e.transpose(BANK[6][:, 48 * tt:48 * tt + 48],
                                                              T[0][0:48, tt * 128:(tt + 1) * 128], ident[0:48, 0:48]),
                                 t_sig, bank_free[6], inc=(tt == 3))
                    tfree[0] = [tok]
                    at["gate"] = DV(lambda e: e.tensor_copy(GT[:, :, :], BANK[6][:, 0:192].rearrange(
                        "p (a b) -> p a b", a=4)), tok, *fence_in)
                    bank_free[6] = [at["gate"]]
            st["rs_used"] = [t, at["v"][3]]
            st["a_free"] = [PE.now()]

            steps = [(n, par, i, br) for i in range(4) for n in range(8) for par in range(2) for br in range(3)]
            info = {}
            ss_free, pt_free, nm_free = [[]] * 3, [[]] * 3, {}

            def step_scores(s):
                n, par, i, br = steps[s]
                gp, r = n // 4, n % 4
                h = (2 * gp + par) * 4 + r
                rows = slice(64 * par, 64 * par + 64)
                keys = 7 + 8 * i if br == 0 else 128 * (i + 1)
                K = (KC, KS, KW)[br]
                b = s % 3
                t = PE(lambda e: e.matmul(BANK[b][:, 0:keys], QN[rows, n, i * 128:(i + 1) * 128],
                                          K[rows, gp, 0:keys], start=True, stop=True), at["q", n], at["kc"],
                       at["kv", 5], at["kv", 7], bank_free[b])
                row = TT[:, h, :]
                bias = bass.AP(row.tensor, row.offset + 128 * i + (96 if br == 0 else 127),
                               [row.ap[0], [-16 if br == 0 else -1, keys]])
                m = s % 8
                t = DV(lambda e: e.tensor_tensor_reduce(SS[s % 3][:, 0:keys], BANK[b][:, 0:keys], bias, -1.0, -GUARD,
                                                        ALU.add, ALU.min, NM[:, m:m + 1]), t, (s_tt, 16),
                       *ss_free[s % 3], nm_free.get(s - 8), *fence_q)
                bank_free[b] = [t]
                o = (s // 3) % 2
                t = AC(lambda e: e.activation(SS[s % 3][:, 0:keys], SS[s % 3][:, 0:keys], ACT.Exp,
                                              bias=NM[:, m:m + 1], scale=-1.0, accum_out=SM[:, o, br:br + 1]), t,
                       info.get(("cf", s // 3 - 2)), *fence_q)
                nm_free[s] = t
                info["e", s] = t
                if br == 2:
                    c = SM[:, o, 0:3]
                    t = DV(lambda e: e.tensor_scalar(c, c, TINY, None, ALU.max), t)
                    t = DV(lambda e: e.reciprocal(c, c), t)
                    info["cf", s // 3] = DV(lambda e: e.tensor_tensor(CF[:, o, 0:3], c, GT[:, i, 3 * h:3 * h + 3],
                                                                      ALU.mult), t, at["gate"],
                                            info.get(("done", s // 3 - 2)), *fence_q)

            def step_turn(s):
                n, par, i, br = steps[s]
                b = 3 + s % 3
                if br == 0:
                    k = 7 + 8 * i
                    t = PE(lambda e: e.transpose(BANK[b][0:k, 0:128], SS[s % 3][:, 0:k], ident[:, :]), info["e", s],
                           bank_free[b])
                    cols, k = 128, k
                else:
                    for j in range(i + 1):
                        t = PE(lambda e, j=j: e.transpose(BANK[b][:, j * 128:(j + 1) * 128],
                                                          SS[s % 3][:, j * 128:(j + 1) * 128], ident[:, :]),
                               info["e", s], bank_free[b], inc=(j == i))
                    cols, k = 128 * (i + 1), 128
                ss_free[s % 3] = [t]
                eng = DV if br == 1 else AC
                if br == 1:
                    t = DV(lambda e: e.tensor_copy(PT[s % 3][0:k, 0:cols], BANK[b][0:k, 0:cols]), t, *pt_free[s % 3],
                           *fence_q)
                else:
                    t = AC(lambda e: e.activation(PT[s % 3][0:k, 0:cols], BANK[b][0:k, 0:cols], ACT.Copy), t,
                           *pt_free[s % 3], *fence_q)
                bank_free[b] = [t]
                info["p", s] = t

            def step_values(s):
                n, par, i, br = steps[s]
                gp, r = n // 4, n % 4
                g = 2 * gp + par
                h = g * 4 + r
                b = 6 + (s // 3) % 2
                k = 7 + 8 * i
                if br == 0:
                    t = PE(lambda e: e.matmul(BANK[b][:, 0:64], PT[s % 3][0:k, 0:128], VC[0:k, g, :], start=True,
                                              stop=True), info["p", s], at["vc"], bank_free[b])
                else:
                    c = 64 * g + 256 * (br - 1)
                    for j in range(i + 1):
                        t = PE(lambda e, j=j: e.matmul(BANK[b][:, 64 * br:64 * br + 64],
                                                       PT[s % 3][:, j * 128:(j + 1) * 128], VS[:, j, c:c + 64],
                                                       start=(j == 0), stop=(j == i)), info["p", s], at["v"][j],
                               inc=(j == i))
                pt_free[s % 3] = [t]
                if br == 2:
                    o = (s // 3) % 2
                    dst = OT[:, i, 64 * h:64 * h + 64]
                    t = DV(lambda e: e.tensor_scalar(dst, BANK[b][:, 0:64], CF[:, o, 0:1], None, ALU.mult), t,
                           info["cf", s // 3], *fence_q)
                    for q in (1, 2):
                        t = DV(lambda e, q=q: e.scalar_tensor_tensor(dst, BANK[b][:, 64 * q:64 * q + 64],
                                                                     CF[:, o, q:q + 1], dst, ALU.mult, ALU.add), t)
                    bank_free[b] = [t]
                    info["done", s // 3] = t

            N = len(steps)
            for s in range(N + 2):
                if s < N:
                    step_scores(s)
                if 1 <= s <= N:
                    step_turn(s - 1)
                if s >= 2:
                    step_values(s - 2)
            fence_o = [DV.now()]
            for f in range(8):
                b = 3 + f % 3
                for i in range(4):
                    t = PE(lambda e, f=f, i=i, b=b: e.transpose(BANK[b][:, i * 128:(i + 1) * 128],
                                                               OT[:, i, f * 128:(f + 1) * 128], ident[:, :]),
                           *fence_o, bank_free[b], inc=(i == 3))
                hi = AC(lambda e, f=f, b=b: e.activation(AH[:, f, :], BANK[b][:, :], ACT.Copy), t, *st["a_free"])
                low = DV(lambda e, f=f, b=b: e.tensor_tensor(AL[:, f, :], BANK[b][:, :], AH[:, f, :], ALU.subtract),
                         hi, *st["a_free"])
                bank_free[b] = [low]
                a_ready[f] = [hi, low]
        fence_m = fence()
        with ExitStack() as ar:
            MN = sb("MN", [128, 8, S], stack=ar)
            m_tok = [None] * 8
            for f in range(8):
                b, tok = gemm_tile("nsa_out", f, AH, AL, a_ready)
                branch_out(MN, m_tok, b, tok, f, fence_m)
            st["a_free"] = [PE.now()]
            post_norm(MN, m_tok, "mix_post1", "ffn_pre1")
        ffn_block2(("ffn3_in", "ffn3_out"), "ffn_post1", None, "3")

        s_out = sem("s_out")
        for f in range(8):
            SP(lambda e, f=f: e.dma_start(out[f], XT[:, f, :]).then_inc(s_out, 16), final["h", f], inc=False)
        assert len(units) == UNITS_TOTAL, len(units)

        block = ctx.enter_context(nc.Block())

        @block.sync
        def _(eng):
            SP.play(eng)
            eng.wait_ge(s_out, 128)

        @block.scalar
        def _(eng):
            AC.play(eng)

        @block.vector
        def _(eng):
            DV.play(eng)

        @block.tensor
        def _(eng):
            PE.play(eng)

        @block.gpsimd
        def _(eng):
            PO.play(eng)


def feature_tiles(w, columns=None):
    w = w if columns is None else w[:, columns]
    k, m = w.shape
    if m % 128:
        w = np.concatenate([w, np.zeros((k, 128 - m % 128), w.dtype)], axis=1)
        m = w.shape[1]
    return np.ascontiguousarray(w.reshape(k // 128, 128, m // 128, 128).transpose(2, 1, 0, 3).reshape(m // 128, 128, k))


def token_tiles(w):
    k, m = w.shape
    return np.ascontiguousarray(w.reshape(8, 128, m // 512, 512).transpose(2, 1, 0, 3).reshape(m // 512, 128, 4096))


def shape_constants():
    f32 = np.float32
    pos = np.arange(S, dtype=f32)
    theta = (f32(1.0) / np.power(f32(10000.0), np.linspace(0.0, 1.0, 128, dtype=f32))).astype(f32)
    ang = (theta[:, None] * pos[None, :]).astype(f32)
    cossin = np.concatenate([np.cos(ang), np.sin(ang)], axis=1).astype(f32)
    log_gamma = np.log(f32(1.0) - np.power(f32(2.0), f32(-5.0) - np.arange(4, dtype=f32))).astype(f32)
    rel = pos[None, :] - np.arange(128, dtype=f32)[:, None]
    decay = np.where(rel >= 0, np.exp(np.maximum(rel, 0.0)[None] * log_gamma[:, None, None]), 0.0) / 16.0
    dist = np.arange(640) - 127
    n = np.maximum(dist, 0)
    large = 16 + (np.log(np.maximum(n, 1).astype(f32) / f32(16)) / f32(math.log(8.0)) * f32(16)).astype(np.int32)
    bucket = np.where(n < 16, n, np.minimum(large, 31))
    onehot = (bucket[None, :] == np.arange(32)[:, None]) & (dist >= 0)[None, :]
    future = np.broadcast_to(np.where(dist >= 0, 0.0, NEG), (16, 640))
    return {"ident": np.eye(128, dtype=f32), "cossin": cossin, "decay": decay.astype(f32),
            "onehot": onehot.astype(f32), "future": np.ascontiguousarray(future.astype(f32))}


def laid_out(inp):
    a = {k: np.asarray(v) for k, v in inp.items()}
    cols = lambda v: v.reshape(-1, 128).T
    vecs = {
        "norm1": cols(a["norm1"][0]), "norm2": cols(a["norm2"][0]), "final_norm": cols(a["final_norm"]),
        "mix_pre0": cols(a["mix_norm_pre_2"][0]), "mix_post0": cols(a["mix_norm_post_2"][0]),
        "ffn_pre0": cols(a["ffn_norm_pre_2"][0]), "ffn_post0": cols(a["ffn_norm_post_2"][0]),
        "kv_norm": cols(a["kv_norm_2"]),
        "mix_pre1": cols(a["mix_norm_pre_2"][1]), "mix_post1": cols(a["mix_norm_post_2"][1]),
        "ffn_pre1": cols(a["ffn_norm_pre_2"][1]), "ffn_post1": cols(a["ffn_norm_post_2"][1]),
        "conv_w": a["conv_w"][0].reshape(4, 4, 128).transpose(2, 1, 0).reshape(128, 16),
        "conv_b": cols(a["conv_b"][0]), "lru_ba": cols(a["lru_ba"][0]), "lru_bi": cols(a["lru_bi"][0]),
        "lru_lambda": cols(a["lru_lambda"][0]), "b_alpha": cols(a["gla_b_alpha"][0]),
        "gla_norm": cols(a["gla_norm"][0]),
        "pe_k": a["cmp_pe_k_2"].reshape(16, 128).T, "pe_v": a["cmp_pe_v_2"].reshape(16, 128).T,
    }
    c = shape_constants()
    d = {
        "xT": a["x"][0].reshape(S, 8, 128).transpose(2, 1, 0).reshape(128, 8 * S),
        "vec": np.concatenate([vecs[n] for n, _ in VEC_NAMES], axis=1),
        "ident": c["ident"], "cossin": c["cossin"], "decay": c["decay"], "future": c["future"],
        "onehot": np.concatenate([c["onehot"], a["rel_bias_2"]], axis=1),
        "lru_wa": a["lru_wa"][0], "lru_wi": a["lru_wi"][0], "w_alpha": a["gla_w_alpha"][0],
    }
    w = a["w_in"][0]
    d["w_in_t"] = feature_tiles(w, np.r_[0:1536, 2048:2576])
    d["w_in_v"] = token_tiles(w[:, 1536:2048])
    d["w_out"] = feature_tiles(a["w_out"][0])
    half = 2816
    gate_up = np.concatenate([np.r_[128 * j:128 * j + 128, half + 128 * j:half + 128 * j + 128] for j in range(22)])
    for n, (wi, wo) in enumerate(((a["w_ffn_in"][0], a["w_ffn_out"][0]), (a["ffn_w_in_2"][0], a["ffn_w_out_2"][0]),
                                  (a["ffn_w_in_2"][1], a["ffn_w_out_2"][1])), 1):
        d[f"ffn{n}_in"] = feature_tiles(wi, gate_up)
        d[f"ffn{n}_out"] = feature_tiles(wo)
    w = a["ret_w_in_2"][0]
    order = []
    for h in range(4):
        for base in (0, 1024):
            at = base + 256 * h
            order += [np.arange(at, at + 256, 2), np.arange(at + 1, at + 256, 2)]
        order.append(np.arange(4096 + 512 * h, 4096 + 512 * h + 512))
    d["ret_t"] = feature_tiles(w, np.concatenate(order))
    d["ret_v"] = token_tiles(w[:, 2048:4096])
    d["ret_out"] = feature_tiles(a["ret_w_out_2"][0])
    w = a["kv_w_2"]
    d["kv_t"] = feature_tiles(w, np.r_[0:512, 512:768, 1024:1280])
    d["kv_v"] = token_tiles(w[:, np.r_[768:1024, 1280:1536]])
    w = a["nsa_w_in_2"][0]
    order = [np.arange(64) + 64 * ((2 * (n // 4) + par) * 4 + n % 4) for n in range(8) for par in range(2)]
    d["nsa_t"] = feature_tiles(w, np.concatenate(order + [np.arange(1024, 1072)]))
    d["nsa_out"] = feature_tiles(a["nsa_w_out_2"][0])
    w1 = [a[n].reshape(16, 128, 256).transpose(1, 0, 2) for n in ("cmp_w1_k_2", "cmp_w1_v_2")]
    d["cmp_w1"] = np.stack(w1)
    w2 = [a[n].reshape(2, 128, 64).transpose(1, 0, 2) for n in ("cmp_w2_k_2", "cmp_w2_v_2")]
    d["cmp_w2"] = np.stack(w2, axis=1)
    return {k: np.ascontiguousarray(v) for k, v in d.items()}


def kernel(**inputs):
    import concourse.bacc as _bacc
    from concourse.bass_utils import run_bass_kernel_spmd as _run

    arrays = laid_out(inputs)
    nc = _bacc.Bacc("TRN2", target_bir_lowering=False, num_devices=1)
    D = {n: nc.dram_tensor("in_" + n, a.shape, F32, kind="ExternalInput").ap() for n, a in arrays.items()}
    D["scratch"] = nc.dram_tensor("scratch", (16, 640), F32, kind="Internal").ap()
    out = nc.dram_tensor("out", (8, 128, S), F32, kind="ExternalOutput").ap()
    build(nc, D, out)
    r = _run(nc, [{"in_" + n: a for n, a in arrays.items()}], core_ids=[0])
    got = np.asarray(r.results[0]["out"])
    return got.reshape(1024, S).T.reshape(1, S, 1024)
```

```python
import math
from contextlib import ExitStack

import concourse.bass as bass
import numpy as np
from concourse import mybir

F32 = mybir.dt.float32
F32R = mybir.dt.float32r
ACT = mybir.ActivationFunctionType
ALU = mybir.AluOpType
AX_X = mybir.AxisListType.X

S = 512
EPS = 1e-6
NEG = -1.0e30
GUARD = -1.0e20
TINY = 1.1754943508222875e-38

RAW_SLOTS = 3
W_SLOTS = 3
LOOK = 2
GEMM_BANKS = 4

VEC_NAMES = [
    ("norm1", 8), ("norm2", 8), ("final_norm", 8), ("mix_pre0", 8), ("mix_post0", 8), ("ffn_pre0", 8),
    ("ffn_post0", 8), ("kv_norm", 8), ("mix_pre1", 8), ("mix_post1", 8), ("ffn_pre1", 8), ("ffn_post1", 8),
    ("conv_w", 16), ("conv_b", 4), ("lru_ba", 4), ("lru_bi", 4), ("lru_lambda", 4), ("b_alpha", 2),
    ("gla_norm", 1), ("pe_k", 16), ("pe_v", 16),
]
VEC_AT = {}
_n = 0
for _name, _w in VEC_NAMES:
    VEC_AT[_name] = _n
    _n += _w
NVEC = _n

FEATURE_MAJOR = {"w_in_t": 8, "w_out": 8, "ffn1_in": 8, "ffn1_out": 22, "ret_t": 8, "ret_out": 16, "ffn2_in": 8,
                 "ffn2_out": 22, "kv_t": 8, "nsa_t": 8, "nsa_out": 8, "ffn3_in": 8, "ffn3_out": 22}
UNITS_TOTAL = 21 + 8 + 68 + 48 + 16 + 68 + 12 + 9 + 8 + 68


class Queue:

    def __init__(self, sem):
        self.sem, self.count, self.items = sem, 0, []

    def __call__(self, fn, *waits, inc=True):
        self.items.append((fn, waits, inc))
        if not inc:
            return None
        self.count += 1
        return (self.sem, self.count)

    def now(self):
        return (self.sem, self.count)

    def play(self, eng):
        seen = {}

        def need(w):
            if w is None:
                return
            if isinstance(w, list):
                for x in w:
                    need(x)
                return
            sem, value = w
            if value > seen.get(sem.name, 0):
                seen[sem.name] = value
                eng.wait_ge(sem, value)

        for fn, waits, inc in self.items:
            need(list(waits))
            ins = fn(eng)
            if inc:
                ins.then_inc(self.sem, 1)


def build(nc, D, out):
    with ExitStack() as ctx:
        def sem(name):
            return ctx.enter_context(nc.semaphore(name))

        def sb(name, shape, dt=F32, stack=ctx):
            return stack.enter_context(nc.sbuf_tensor(name, shape, dt))

        PE, AC, DV, SP, PO = (Queue(sem(n)) for n in ("pe", "act", "dve", "sp", "pool"))
        every = (PE, AC, DV)

        def fence():
            return [q.now() for q in every]

        XT = sb("XT", [128, 8, S])
        AH = sb("AH", [128, 8, S], F32R)
        AL = sb("AL", [128, 8, S], F32R)
        RAW = [sb(f"RAW{i}", [128, 1024]) for i in range(RAW_SLOTS)]
        WH = [sb(f"WH{i}", [128, 1024], F32R) for i in range(W_SLOTS)]
        WL = [sb(f"WL{i}", [128, 1024], F32R) for i in range(W_SLOTS)]
        ident = sb("ident", [128, 128])
        ones = sb("ones", [128, 1])
        RS = sb("RS", [128, S])
        ACC = sb("ACC", [128, S])
        SQ = [sb(f"SQ{i}", [128, S]) for i in range(2)]
        T = [sb(f"T{i}", [128, S]) for i in range(4)]
        vec = sb("vec", [128, NVEC])
        small = sb("small", [128, 64])
        rtok = sb("rtok", [128, 16])
        rstok = sb("rstok", [128, 4])
        rso = sb("rso", [128, 16])
        BANK = [ctx.enter_context(nc.psum_tensor(f"bank{i}", [128, 512], F32)) for i in range(8)]
        bank_free = [[] for _ in range(8)]

        def V(name, i=0, n=1):
            at = VEC_AT[name] + i
            return vec[:, at:at + n]

        s_const = sem("s_const")
        s_x = sem("s_x")
        const_ready = (s_const, 32)
        x_ready = (s_x, 16)
        SP(lambda e: e.dma_start(XT[:, :, :], D["xT"].rearrange("p (f t) -> p f t", f=8)).then_inc(s_x, 16), inc=False)
        SP(lambda e: e.dma_start(vec[:, :], D["vec"]).then_inc(s_const, 16), inc=False)
        SP(lambda e: e.dma_start(ident[:, :], D["ident"]).then_inc(s_const, 16), inc=False)
        t_ones = DV(lambda e: e.memset(ones[:, :], 1.0))

        s_raw = [sem(f"s_raw{i}") for i in range(RAW_SLOTS)]
        units = []
        unit_hi, unit_lo, unit_used = {}, {}, {}
        state = {"dma": 0, "prep": 0, "bank": 0}

        def weight_dma():
            u = state["dma"]
            if u >= UNITS_TOTAL:
                return
            state["dma"] += 1
            r = u % RAW_SLOTS

            def go(e):
                src, n = units[u]
                e.dma_start(RAW[r][:, 0:n], src).then_inc(s_raw[r], 16)
            SP(go, unit_hi.get(u - RAW_SLOTS), unit_lo.get(u - RAW_SLOTS), inc=False)

        def weight_prep():
            u = state["prep"]
            if u >= UNITS_TOTAL:
                return
            state["prep"] += 1
            r, w = u % RAW_SLOTS, u % W_SLOTS
            landed = (s_raw[r], 16 * (u // RAW_SLOTS + 1))
            used = unit_used.get(u - W_SLOTS)
            unit_hi[u] = AC(lambda e: e.activation(WH[w][:, 0:units[u][1]], RAW[r][:, 0:units[u][1]], ACT.Copy),
                            landed, used)
            unit_lo[u] = DV(lambda e: e.tensor_tensor(WL[w][:, 0:units[u][1]], RAW[r][:, 0:units[u][1]],
                                                      WH[w][:, 0:units[u][1]], ALU.subtract),
                            landed, used, unit_hi[u])
            weight_dma()

        for _ in range(RAW_SLOTS):
            weight_dma()

        def next_unit(src, n):
            u = len(units)
            units.append((src, n))
            while state["prep"] <= min(u + LOOK, UNITS_TOTAL - 1):
                weight_prep()
            return u

        def gemm_bank():
            b = state["bank"]
            state["bank"] = (b + 1) % GEMM_BANKS
            return b

        def gemm_parts(name, mt, in_h, in_l, ready, b):
            kt = FEATURE_MAJOR[name]
            done = []
            parts = []
            for kk in range(kt):
                def part(kk=kk):
                    k = kk % 8
                    if k == 0:
                        nk = min(8, kt - kk)
                        part_unit[0] = next_unit(D[name][mt, :, kk * 128:(kk + nk) * 128], nk * 128)
                    u = part_unit[0]
                    w = u % W_SLOTS
                    sl = slice(k * 128, (k + 1) * 128)
                    end = k == 7 or kk == kt - 1
                    for n, (wt, x) in enumerate(((WH[w], in_h), (WH[w], in_l), (WL[w], in_h))):
                        first, last = kk == 0 and n == 0, kk == kt - 1 and n == 2
                        waits = [ready[kk]] if n < 2 else []
                        if first:
                            waits += [bank_free[b]]
                        waits += [unit_hi[u]] if n == 0 else [unit_lo[u]] if n == 2 else []
                        tok = PE(lambda e, wt=wt, x=x, first=first, last=last: e.matmul(
                            BANK[b][:, :], wt[:, sl], x[:, kk, :], start=first, stop=last), *waits,
                            inc=end and n == 2)
                    if end:
                        unit_used[u] = tok
                    if kk == kt - 1:
                        done.append(tok)
                parts.append(part)
            part_unit = [None]
            return parts, done

        def gemm_tile(name, mt, in_h, in_l, ready):
            b = gemm_bank()
            parts, done = gemm_parts(name, mt, in_h, in_l, ready, b)
            for part in parts:
                part()
            return b, done[0]

        def gemm_tokens(name, c, in_h, in_l, ready):
            banks = [gemm_bank() for _ in range(4)]
            toks = [None] * 4
            for q in range(4):
                u = next_unit(D[name][c, :, q * 1024:(q + 1) * 1024], 1024)
                w = u % W_SLOTS
                for tt in range(4):
                    for k in range(2):
                        kk = 2 * q + k
                        sl = slice(k * 512, (k + 1) * 512)
                        for n, (wt, x) in enumerate(((WH[w], in_h), (WH[w], in_l), (WL[w], in_h))):
                            first = kk == 0 and n == 0
                            last = kk == 7 and n == 2
                            waits = [ready[kk]] + ([bank_free[banks[tt]]] if first else [])
                            waits += [unit_hi[u]] if n < 2 else [unit_lo[u]]
                            toks[tt] = PE(lambda e, b=banks[tt], wt=wt, x=x, sl=sl, kk=kk, tt=tt, first=first, last=last:
                                          e.matmul(BANK[b][:, :], x[:, kk, tt * 128:(tt + 1) * 128], wt[:, sl],
                                                   start=first, stop=last),
                                          *waits, inc=(k == 1 and n == 2))
                unit_used[u] = toks[3]
            return banks, toks

        background = []

        def tick(n=1):
            for _ in range(n):
                if background:
                    background.pop(0)()

        def flush():
            while background:
                background.pop(0)()

        st = {"acc": None, "sq": [None, None], "a_free": [], "rs_used": []}

        def square_in(f, src, ready):
            i = f % 2
            t = AC(lambda e: e.activation(SQ[i][:, :] if f else ACC[:, :], src, ACT.Square), *ready,
                   st["sq"][i], None if f else st.get("acc_read"), None if f else st["acc"])
            if f:
                st["acc"] = DV(lambda e: e.tensor_tensor(ACC[:, :], ACC[:, :], SQ[i][:, :], ALU.add), t, st["acc"])
                st["sq"][i] = st["acc"]
            else:
                st["acc"] = t
            return t

        def rms_scale():
            for tt in range(4):
                tok = PE(lambda e, tt=tt: e.matmul(BANK[4][:, tt:tt + 1], ACC[:, tt * 128:(tt + 1) * 128], ones[:, :],
                                                   start=True, stop=True),
                         st["acc"], bank_free[4], t_ones, inc=(tt == 3))
            st["acc_read"] = tok
            a = AC(lambda e: e.activation(rtok[:, 0:4], BANK[4][:, 0:4], ACT.Sqrt, bias=small[:, 63:64],
                                          scale=1.0 / 1024), tok, t_eps, st.get("rtok_read"))
            bank_free[4] = [a]
            r = DV(lambda e: e.reciprocal(rstok[:, :], rtok[:, 0:4]), a, st.get("rstok_read"), *st["rs_used"])
            st["rtok_read"] = r
            for tt in range(4):
                tok = PE(lambda e, tt=tt: e.matmul(BANK[5][:, tt * 128:(tt + 1) * 128],
                                                   rstok[:, tt:tt + 1].broadcast_to([128, 128]), ident[:, :],
                                                   start=True, stop=True),
                         r, bank_free[5], const_ready, inc=(tt == 3))
            st["rstok_read"] = tok
            c = DV(lambda e: e.tensor_copy(RS[:, :], BANK[5][:, :]), tok, *st["rs_used"])
            bank_free[5] = [c]
            st["rs_used"] = []
            return c

        def split_in(f, gain, ready, write_after=()):
            g = V(gain, f)
            h = AC(lambda e: e.activation(AH[:, f, :], XT[:, f, :], ACT.Copy, scale=g), *ready, const_ready,
                   *write_after)
            low = DV(lambda e: e.scalar_tensor_tensor(AL[:, f, :], XT[:, f, :], g, AH[:, f, :], ALU.mult,
                                                      ALU.subtract), h, *ready, *write_after)
            return [h, low]

        t_eps = DV(lambda e: e.memset(small[:, 63:64], EPS))

        a_ready = [None] * 8
        xt_read = [None] * 8

        def split_and_square(f, gain, ready):
            a_ready[f] = split_in(f, gain, ready, st["a_free"])
            xt_read[f] = [a_ready[f][1], square_in(f, XT[:, f, :], ready)]

        for f in range(8):
            split_and_square(f, "norm1", [x_ready])
        t_rs = rms_scale()

        with ExitStack() as ar:
            MH = sb("MH", [128, 8, S], F32R, ar)
            ML = sb("ML", [128, 8, S], F32R, ar)
            XP = [sb(f"XP{i}", [128, S + 3], stack=ar) for i in range(2)]
            LB = [[sb(f"LB{i}_{j}", [128, S], stack=ar) for j in range(5)] for i in range(2)]
            HL = sb("HL", [128, 4, S], stack=ar)
            QG = sb("QG", [128, 2, S], stack=ar)
            KG = sb("KG", [128, 2, S], stack=ar)
            BC = sb("BC", [128, 2, S], stack=ar)
            EG = sb("EG", [128, 2, S], stack=ar)
            KT = sb("KT", [128, 4, 256], stack=ar)
            VG = sb("VG", [128, 4, 512], stack=ar)
            SG = sb("SG", [128, 2, 8, 128], stack=ar)
            bd = sb("bd", [128, 8, 128], stack=ar)
            wal = sb("wal", [16, 256], stack=ar)
            DG = sb("DG", [128, 2, 8], stack=ar)
            s_bd = sem("s_bd")
            m_ready = [None] * 8

            z = DV(lambda e: e.memset(bd[:, :, :], 0.0))
            for i, name in enumerate(("lru_wa", "lru_wi")):
                for half in range(2):
                    rows = slice(64 * half, 64 * half + 64)
                    SP(lambda e, i=i, name=name, rows=rows, half=half: e.dma_start(
                        bd[rows, 4 * i:4 * i + 4, rows], D[name].rearrange("(f a) i j -> a i f j", a=2)[half])
                       .then_inc(s_bd, 16), z, inc=False)
            SP(lambda e: e.dma_start(wal[:, :], D["w_alpha"]).then_inc(s_bd, 16), inc=False)
            bd_ready = (s_bd, 80)
            for i in range(2):
                xp_zero = DV(lambda e, i=i: e.memset(XP[i][:, 0:3], 0.0))

            lam = V("lru_lambda", 0, 4)
            ab, ee, sden, ss, s2, pol, mx = (small[:, 4 * i:4 * i + 4] for i in range(7))
            cneg, cpos = small[:, 28:32], small[:, 32:36]
            t = AC(lambda e: e.activation(ab, lam, ACT.Abs), const_ready)
            t = AC(lambda e: e.activation(ee, ab, ACT.Exp, scale=-1.0), t)
            t = DV(lambda e: e.tensor_scalar(sden, ee, 2.0, None, ALU.add), t)
            t = DV(lambda e: e.reciprocal(sden, sden), t)
            t = DV(lambda e: e.tensor_tensor(ss, ee, sden, ALU.mult), t)
            t = DV(lambda e: e.tensor_tensor(s2, ss, ss, ALU.mult), t)
            t = DV(lambda e: e.tensor_scalar(pol, s2, 2.0 / 19, 2.0 / 17, ALU.mult, ALU.add), t)
            for d in (15, 13, 11, 9, 7, 5, 3, 1):
                t = DV(lambda e: e.tensor_tensor(pol, pol, s2, ALU.mult), t)
                t = DV(lambda e, d=d: e.tensor_scalar(pol, pol, 2.0 / d, None, ALU.add), t)
            t = DV(lambda e: e.tensor_tensor(pol, pol, ss, ALU.mult), t)
            t = DV(lambda e: e.tensor_scalar(mx, lam, -1.0, 0.0, ALU.mult, ALU.max), t, const_ready)
            t = DV(lambda e: e.tensor_tensor(mx, mx, pol, ALU.add), t)
            t = DV(lambda e: e.tensor_scalar(cpos, mx, 8.0, None, ALU.mult), t)
            t_c = DV(lambda e: e.tensor_scalar(cneg, mx, -8.0, None, ALU.mult), t)

            lru = {}
            lset_free = [[xp_zero], [xp_zero]]

            def lru_evac(f, b, tok):
                i = f % 2
                y = LB[i][0]
                t = DV(lambda e: e.tensor_tensor(XP[i][:, 3:S + 3], BANK[b][:, :], RS[:, :], ALU.mult), tok, t_rs,
                       *lset_free[i])
                bank_free[b] = [t]
                w = V("conv_w", 4 * f, 4)
                t = DV(lambda e: e.tensor_scalar(y[:, :], XP[i][:, 0:S], w[:, 0:1], V("conv_b", f), ALU.mult,
                                                 ALU.add), t, const_ready)
                for j in range(1, 4):
                    t = DV(lambda e, j=j: e.scalar_tensor_tensor(y[:, :], XP[i][:, j:j + S], w[:, j:j + 1], y[:, :],
                                                                 ALU.mult, ALU.add), t)
                lru[f] = t

            def lru_gates(f):
                i = f % 2
                y, r, g, a, tt = LB[i]
                ga = PE(lambda e: e.matmul(BANK[6][:, :], bd[:, f, :], y[:, :], start=True, stop=True), lru[f],
                        bank_free[6], bd_ready)
                gi = PE(lambda e: e.matmul(BANK[7][:, :], bd[:, 4 + f, :], y[:, :], start=True, stop=True),
                        bank_free[7])
                tr = AC(lambda e: e.activation(r[:, :], BANK[6][:, :], ACT.Sigmoid, bias=V("lru_ba", f)), ga,
                        *lset_free[i])
                ti = AC(lambda e: e.activation(g[:, :], BANK[7][:, :], ACT.Sigmoid, bias=V("lru_bi", f)), gi)
                bank_free[6], bank_free[7] = [tr], [ti]
                lru[f] = (tr, ti)

            def lru_decay(f):
                i = f % 2
                y, r, g, a, tt = LB[i]
                tr, ti = lru[f]
                ta = AC(lambda e: e.activation(a[:, :], r[:, :], ACT.Exp, scale=cneg[:, f:f + 1]), tr, t_c)
                th = AC(lambda e: e.activation(tt[:, :], r[:, :], ACT.Tanh, scale=cpos[:, f:f + 1]))
                d1 = DV(lambda e: e.tensor_tensor(g[:, :], g[:, :], y[:, :], ALU.mult), ti)
                d2 = DV(lambda e: e.tensor_tensor(r[:, :], a[:, :], a[:, :], ALU.mult), ta, th)
                d3 = DV(lambda e: e.scalar_tensor_tensor(r[:, :], r[:, :], 1.0, tt[:, :], ALU.add, ALU.mult), d2)
                lru[f] = (d1, d3)

            def lru_scan(f):
                i = f % 2
                y, r, g, a, tt = LB[i]
                d1, d3 = lru[f]
                t = AC(lambda e: e.activation(tt[:, :], r[:, :], ACT.Sqrt), d3)
                t = DV(lambda e: e.tensor_tensor(g[:, :], g[:, :], tt[:, :], ALU.mult), t, d1)
                t = DV(lambda e: e.tensor_tensor_scan(HL[:, f, :], a[:, :], g[:, :], 0.0, ALU.mult, ALU.add), t)
                lset_free[i] = [t]
                lru[f] = t

            tfree = [[] for _ in range(4)]

            def lru_out_evac(f, b, tok):
                i = f % 4
                t = DV(lambda e: e.tensor_tensor(T[i][:, :], BANK[b][:, :], RS[:, :], ALU.mult), tok, t_rs, *tfree[i])
                bank_free[b] = [t]
                tg = AC(lambda e: e.activation(T[i][:, :], T[i][:, :], ACT.Gelu_apprx_tanh), t)

                def rest():
                    t = DV(lambda e: e.tensor_tensor(T[i][:, :], T[i][:, :], HL[:, f, :], ALU.mult), tg, lru[f])
                    h = AC(lambda e: e.activation(MH[:, f, :], T[i][:, :], ACT.Copy), t)
                    low = DV(lambda e: e.tensor_tensor(ML[:, f, :], T[i][:, :], MH[:, f, :], ALU.subtract), h)
                    tfree[i] = [low]
                    m_ready[f] = [h, low]
                    hl_read.append(t)
                return rest

            hl_read = []
            for f in range(4):
                b, tok = gemm_tile("w_in_t", f, AH, AL, a_ready)
                tick()
                lru_evac(f, b, tok)
                background.append(lambda f=f: lru_gates(f))
                background.append(lambda f=f: lru_decay(f))
                background.append(lambda f=f: lru_scan(f))
                if f >= 1:
                    tick(1 if f == 1 else 3)
                    if f == 1:
                        tick(2)
            qk = {}
            for f in range(4):
                b, tok = gemm_tile("w_in_t", 8 + f, AH, AL, a_ready)
                tick()
                dst = (QG if f < 2 else KG)[:, f % 2, :]
                qk[f] = DV(lambda e, b=b, dst=dst, c=(0.125 if f < 2 else 1.0): e.scalar_tensor_tensor(
                    dst, BANK[b][:, :], c, RS[:, :], ALU.mult, ALU.mult), tok, t_rs)
                bank_free[b] = [qk[f]]
                tick()
            b, tok = gemm_tile("w_in_t", 16, AH, AL, a_ready)
            flush()
            ZT = T[0]
            tz = DV(lambda e, b=b: e.tensor_tensor(ZT[0:16, :], BANK[b][0:16, :], RS[0:16, :], ALU.mult), tok, t_rs,
                    *tfree[0])
            bank_free[b] = [tz]
            msk = T[3]
            tm = DV(lambda e: e.memset(msk[:, :], 1.0), *tfree[3])
            tm = DV(lambda e: e.memset(msk[:, 0:S:64], 0.0), tm)

            def gla_decay_1():
                for f in range(2):
                    zf = PE(lambda e, f=f: e.matmul(BANK[6 + f][:, :], wal[:, f * 128:(f + 1) * 128], ZT[0:16, :],
                                                    start=True, stop=True), tz, bd_ready, bank_free[6 + f])
                    za = AC(lambda e, f=f: e.activation(BC[:, f, :], BANK[6 + f][:, :], ACT.Identity,
                                                        bias=V("b_alpha", f)), zf)
                    bank_free[6 + f] = [za]
                    ab_ = AC(lambda e, f=f: e.activation(EG[:, f, :], BC[:, f, :], ACT.Abs), za)
                    ex = AC(lambda e, f=f: e.activation(EG[:, f, :], EG[:, f, :], ACT.Exp, scale=-1.0), ab_)
                    qk["l", f] = AC(lambda e, f=f: e.activation(EG[:, f, :], EG[:, f, :], ACT.Ln, bias=1.0), ex)
                tfree[0] = [zf]

            def gla_decay_2():
                for f in range(2):
                    la = DV(lambda e, f=f: e.scalar_tensor_tensor(EG[:, f, :], BC[:, f, :], 0.0, EG[:, f, :],
                                                                  ALU.min, ALU.subtract), qk["l", f])
                    bc = DV(lambda e, f=f: e.tensor_tensor_scan(BC[:, f, :], msk[:, :], EG[:, f, :], 0.0, ALU.mult,
                                                                ALU.add), la, tm)
                    bcv = BC[:, f, :].rearrange("p (c t) -> p c t", t=64)
                    egv = EG[:, f, :].rearrange("p (c t) -> p c t", t=64)
                    df = DV(lambda e, bcv=bcv, egv=egv: e.tensor_tensor(
                        egv, bcv[:, :, 63:64].broadcast_to([128, 8, 64]), bcv, ALU.subtract), bc)
                    qk["d", f] = AC(lambda e, f=f, bcv=bcv: e.activation(DG[:, f, :], bcv[:, :, 63], ACT.Exp,
                                                                        scale=1.0 / 16), bc)
                    ex = AC(lambda e, f=f: e.activation(EG[:, f, :], EG[:, f, :], ACT.Exp, scale=1.0 / 16), df)
                    qk["k", f] = DV(lambda e, f=f: e.tensor_tensor(KG[:, f, :], KG[:, f, :], EG[:, f, :], ALU.mult),
                                    ex, qk[2 + f])
                tfree[3] = [bc]

            def gla_turn():
                for f in range(2):
                    for tt in range(4):
                        tp = PE(lambda e, f=f, tt=tt: e.transpose(BANK[6 + f][:, tt * 128:(tt + 1) * 128],
                                                                  KG[:, f, tt * 128:(tt + 1) * 128], ident[:, :]),
                                qk["k", f], bank_free[6 + f], const_ready, inc=(tt == 3))
                    qk["t", f] = AC(lambda e, f=f: e.activation(
                        KT[:, :, f * 128:(f + 1) * 128], BANK[6 + f][:, :].rearrange("p (a b) -> p a b", b=128),
                        ACT.Copy), tp)
                    bank_free[6 + f] = [qk["t", f]]

            background += [gla_decay_1, gla_decay_2, gla_turn]

            late = []
            for f in range(4):
                b, tok = gemm_tile("w_in_t", 4 + f, AH, AL, a_ready)
                tick()
                for fn in late:
                    fn()
                late = [lru_out_evac(f, b, tok)]
            banks, toks = gemm_tokens("w_in_v", 0, AH, AL, a_ready)
            for fn in late:
                fn()
            flush()
            tv = []
            for tt in range(4):
                tv.append(AC(lambda e, tt=tt, b=banks[tt]: e.activation(VG[:, tt, :], BANK[b][:, :], ACT.Copy,
                                                                        scale=rstok[:, tt:tt + 1]), toks[tt], t_rs))
                bank_free[banks[tt]] = [tv[tt]]
            st["rs_used"].append(tv[3])

            def gla_update(pr):
                for c in range(8):
                    tt, row = c // 2, 64 * (c % 2)
                    b = 4 + (c % 2)
                    for hh in range(2):
                        h = 2 * pr + hh
                        tok = PE(lambda e, c=c, tt=tt, row=row, b=b, hh=hh, h=h: e.matmul(
                            BANK[b][64 * hh:64 * hh + 64, (c // 2) * 128:(c // 2) * 128 + 128],
                            KT[row:row + 64, tt, h * 64:h * 64 + 64], VG[row:row + 64, tt, h * 128:h * 128 + 128],
                            start=True, stop=True), qk["t", pr], tv[tt], bank_free[b], inc=(c >= 6 and hh == 1))
                    if c >= 6:
                        qk["u", pr, c % 2] = tok
                prev = None
                for c in range(8):
                    b = 4 + (c % 2)
                    src = BANK[b][:, (c // 2) * 128:(c // 2) * 128 + 128]
                    if c == 0:
                        prev = DV(lambda e, src=src: e.tensor_copy(SG[:, pr, 0, :], src), qk["u", pr, 0])
                    else:
                        prev = DV(lambda e, src=src, c=c: e.scalar_tensor_tensor(
                            SG[:, pr, c, :], SG[:, pr, c - 1, :], DG[:, pr, c:c + 1], src, ALU.mult, ALU.add),
                            prev, qk["u", pr, c % 2], qk["d", pr])
                bank_free[4] = [prev]
                bank_free[5] = [prev]
                qk["s", pr] = prev

            def gla_out(pr):
                for hh in range(2):
                    h = 2 * pr + hh
                    for c in range(8):
                        tok = PE(lambda e, c=c, hh=hh: e.matmul(
                            BANK[6 + hh][:, c * 64:c * 64 + 64], SG[64 * hh:64 * hh + 64, pr, c, :],
                            QG[64 * hh:64 * hh + 64, pr, c * 64:c * 64 + 64], start=True, stop=True),
                            qk["s", pr], bank_free[6 + hh], qk[pr], inc=(c == 7))
                    i = h % 2
                    to = AC(lambda e, h=h, hh=hh: e.activation(HL[:, h, :], BANK[6 + hh][:, :], ACT.Copy,
                                                               scale=V("gla_norm")), tok, *hl_read)
                    ts = AC(lambda e, i=i, hh=hh: e.activation(SQ[i][:, :], BANK[6 + hh][:, :], ACT.Square), to,
                            st["sq"][i])
                    bank_free[6 + hh] = [ts]
                    for tt in range(4):
                        tok = PE(lambda e, h=h, tt=tt, i=i: e.matmul(
                            BANK[4][:, 4 * h + tt:4 * h + tt + 1], SQ[i][:, tt * 128:(tt + 1) * 128], ones[:, :],
                            start=True, stop=True), ts, bank_free[4], inc=(tt == 3))
                    st["sq"][i] = tok
                    qk["o", h] = to
                    qk["n", h] = tok

            def gla_scale():
                a = AC(lambda e: e.activation(rtok[:, 0:16], BANK[4][:, 0:16], ACT.Sqrt, bias=small[:, 63:64],
                                              scale=1.0 / 128), qk["n", 3], st.get("rtok_read"))
                bank_free[4] = [a]
                r = DV(lambda e: e.reciprocal(rso[:, :], rtok[:, 0:16]), a)
                st["rtok_read"] = r
                qk["r"] = r

            def gla_norm_out(h):
                bb = 5 + h % 2
                for tt in range(4):
                    tok = PE(lambda e, tt=tt: e.matmul(
                        BANK[bb][:, tt * 128:(tt + 1) * 128],
                        rso[:, 4 * h + tt:4 * h + tt + 1].broadcast_to([128, 128]), ident[:, :], start=True,
                        stop=True), qk["r"], bank_free[bb], inc=(tt == 3))
                qk["y", h] = DV(lambda e: e.tensor_tensor(HL[:, h, :], HL[:, h, :], BANK[bb][:, :], ALU.mult), tok,
                                qk["o", h])
                bank_free[bb] = [qk["y", h]]

            background += [lambda: gla_update(0), lambda: gla_update(1), lambda: gla_out(0), lambda: gla_out(1)]
            late = []

            def silu_gate(h, b, tok):
                i = h % 4
                t = DV(lambda e: e.tensor_tensor(T[i][:, :], BANK[b][:, :], RS[:, :], ALU.mult), tok, *tfree[i])
                bank_free[b] = [t]
                ts = AC(lambda e: e.activation(T[i][:, :], T[i][:, :], ACT.Silu), t)
                st["rs_used"].append(t)

                def rest():
                    t = DV(lambda e: e.tensor_tensor(T[i][:, :], T[i][:, :], HL[:, h, :], ALU.mult), ts, qk["y", h])
                    hi = AC(lambda e: e.activation(MH[:, 4 + h, :], T[i][:, :], ACT.Copy), t)
                    low = DV(lambda e: e.tensor_tensor(ML[:, 4 + h, :], T[i][:, :], MH[:, 4 + h, :], ALU.subtract),
                             hi)
                    tfree[i] = [low]
                    m_ready[4 + h] = [hi, low]
                return rest

            for h in range(4):
                b, tok = gemm_tile("w_in_t", 12 + h, AH, AL, a_ready)
                tick()
                late.append(silu_gate(h, b, tok))
            st["a_free"] = [PE.now()]
            flush()
            gla_scale()
            for h in range(4):
                gla_norm_out(h)
            for fn in late:
                fn()

            def residual_mix1(f, b, tok):
                t = DV(lambda e: e.tensor_tensor(XT[:, f, :], XT[:, f, :], BANK[b][:, :], ALU.add), tok, *xt_read[f])
                bank_free[b] = [t]
                split_and_square(f, "norm2", [t])

            for f in range(8):
                b, tok = gemm_tile("w_out", f, MH, ML, m_ready)
                residual_mix1(f, b, tok)
        F = fence()
        st["rs_used"] = []

        def ffn_layer(names, finish, tag):
            fence_in = fence()
            with ExitStack() as ar:
                HH = sb("HH" + tag, [128, 22, S], F32R, ar)
                HLO = sb("HLO" + tag, [128, 22, S], F32R, ar)
                h_ready = [None] * 22
                late = []

                def pair(j, bg, tg, bu, tu):
                    a, c = T[2 * (j % 2)], T[2 * (j % 2) + 1]
                    fa, fc = tfree[2 * (j % 2)], tfree[2 * (j % 2) + 1]
                    t1 = DV(lambda e: e.tensor_tensor(a[:, :], BANK[bg][:, :], RS[:, :], ALU.mult), tg, st["rs"], *fa)
                    bank_free[bg] = [t1]
                    t2 = AC(lambda e: e.activation(a[:, :], a[:, :], ACT.Silu), t1)
                    t3 = DV(lambda e: e.tensor_tensor(c[:, :], BANK[bu][:, :], RS[:, :], ALU.mult), tu, *fc)
                    bank_free[bu] = [t3]
                    st["rs_used"] = [t3]

                    def rest():
                        t4 = DV(lambda e: e.tensor_tensor(a[:, :], a[:, :], c[:, :], ALU.mult), t2, t3)
                        hi = AC(lambda e: e.activation(HH[:, j, :], a[:, :], ACT.Copy), t4, *fence_in)
                        low = DV(lambda e: e.tensor_tensor(HLO[:, j, :], a[:, :], HH[:, j, :], ALU.subtract), hi,
                                 *fence_in)
                        tfree[2 * (j % 2)] = [low]
                        tfree[2 * (j % 2) + 1] = [t4]
                        h_ready[j] = [hi, low]
                    return rest

                for j in range(22):
                    bg, tg = gemm_tile(names[0], 2 * j, AH, AL, a_ready)
                    if j == 0:
                        st["rs"] = rms_scale()
                    for fn in late:
                        fn()
                    bu, tu = gemm_tile(names[0], 2 * j + 1, AH, AL, a_ready)
                    late = [pair(j, bg, tg, bu, tu)]
                st["a_free"] = [PE.now()]
                for fn in late:
                    fn()
                for f in range(8):
                    b, tok = gemm_tile(names[1], f, HH, HLO, h_ready)
                    finish(f, b, tok)

        def finish_block1(f, b, tok):
            t = DV(lambda e: e.tensor_tensor(XT[:, f, :], XT[:, f, :], BANK[b][:, :], ALU.add), tok, *xt_read[f])
            bank_free[b] = [t]
            final["x", f] = [t, square_in(f, XT[:, f, :], [t])]

        final = {}
        ffn_layer(("ffn1_in", "ffn1_out"), finish_block1, "1")
        st["rs"] = rms_scale()
        for f in range(8):
            t = DV(lambda e, f=f: e.scalar_tensor_tensor(XT[:, f, :], XT[:, f, :], V("final_norm", f), RS[:, :],
                                                         ALU.mult, ALU.mult), final["x", f], st["rs"])
            st["rs_used"] = [t]
            split_and_square(f, "mix_pre0", [t])

        def post_norm(M, m_tok, post, pre):
            rs = rms_scale()
            for f in range(8):
                t = DV(lambda e, f=f: e.scalar_tensor_tensor(M[:, f, :], M[:, f, :], V(post, f), RS[:, :], ALU.mult,
                                                             ALU.mult), m_tok[f], st["acc_read"], rs)
                st["rs_used"] = [t]
                t = DV(lambda e, f=f: e.tensor_tensor(XT[:, f, :], XT[:, f, :], M[:, f, :], ALU.add), t, *xt_read[f])
                final["h", f] = t
                if pre:
                    split_and_square(f, pre, [t])

        def branch_out(M, m_tok, b, tok, f, after=()):
            t = AC(lambda e: e.activation(M[:, f, :], BANK[b][:, :], ACT.Copy), tok, *after)
            bank_free[b] = [t]
            m_tok[f] = t
            square_in(f, M[:, f, :], [t])

        fence_in = fence()
        with ExitStack() as ar:
            RH = sb("RH", [128, 16, S], F32R, ar)
            RL = sb("RL", [128, 16, S], F32R, ar)
            CS = sb("CS", [128, 2, S], stack=ar)
            DEC = sb("DEC", [128, S], stack=ar)
            s_cs, s_dec = sem("s_cs"), sem("s_dec")
            PO(lambda e: e.dma_start(CS[:, :, :], D["cossin"].rearrange("p (a t) -> p a t", a=2)).then_inc(s_cs, 16),
               *fence_in, inc=False)
            r_ready = [None] * 16
            with ExitStack() as ar2:
                OH = sb("OH", [33, 656], stack=ar2)
                BV = sb("BV", [16, 640], stack=ar2)
                s_bias, s_scr = sem("s_bias"), sem("s_scr")
                PO(lambda e: e.dma_start(OH[:, :], D["onehot"]).then_inc(s_bias, 16), *fence_in, inc=False)

                def distance_bias():
                    for n in range(2):
                        cols = slice(320 * n, 320 * n + 320)
                        t = PE(lambda e, cols=cols, n=n: e.matmul(BANK[6 + n][0:16, 0:320], OH[:, 640:656],
                                                                  OH[:, cols], start=True, stop=True),
                               (s_bias, 16), bank_free[6 + n])
                        t = DV(lambda e, cols=cols, n=n: e.tensor_copy(BV[:, cols], BANK[6 + n][0:16, 0:320]), t,
                               *fence_in)
                        bank_free[6 + n] = [t]
                    PO(lambda e: e.dma_start(D["scratch"], BV[:, :]).then_inc(s_scr, 16), t, inc=False)

                QR = sb("QR", [128, 2, S], stack=ar2)
                KR = sb("KR", [128, 2, S], stack=ar2)
                VR = sb("VR", [128, 4, 512], stack=ar2)
                OR = sb("OR", [128, 4, S], stack=ar2)
                ST = [sb(f"ST{j}", [128, S - 128 * j], stack=ar2) for j in range(4)]
                q_read, v_read, st_read, dec_read, or_read = [], [], [None] * 4, [], []
                ret = {}

                def rotate(h, dst, b0, t0, b1, t1):
                    rd = list(q_read)
                    d = [DV(lambda e: e.tensor_tensor(T[0][:, :], BANK[b0][:, :], CS[:, 0, :], ALU.mult), t0,
                            ret["cs"], *tfree[0]),
                         DV(lambda e: e.tensor_tensor(T[1][:, :], BANK[b0][:, :], CS[:, 1, :], ALU.mult), *tfree[1])]
                    bank_free[b0] = [d[1]]
                    d += [DV(lambda e: e.tensor_tensor(T[2][:, :], BANK[b1][:, :], CS[:, 1, :], ALU.mult), t1,
                             *tfree[2]),
                          DV(lambda e: e.tensor_tensor(T[3][:, :], BANK[b1][:, :], CS[:, 0, :], ALU.mult),
                             *tfree[3])]
                    bank_free[b1] = [d[3]]
                    e0 = DV(lambda e: e.tensor_tensor(dst[:, 0, :], T[0][:, :], T[2][:, :], ALU.subtract), d[2], *rd,
                            *fence_in)
                    e1 = DV(lambda e: e.tensor_tensor(dst[:, 1, :], T[1][:, :], T[3][:, :], ALU.add), d[3], *rd)
                    tfree[0], tfree[2] = [e0], [e0]
                    tfree[1], tfree[3] = [e1], [e1]
                    return e1

                def heads_qkv(h):
                    b0, t0 = gemm_tile("ret_t", 8 * h, AH, AL, a_ready)
                    if h == 0:
                        st["rs"] = rms_scale()
                        c = DV(lambda e: e.tensor_tensor(CS[:, 0, :], CS[:, 0, :], RS[:, :], ALU.mult), st["rs"],
                               (s_cs, 16))
                        ret["cs"] = DV(lambda e: e.tensor_tensor(CS[:, 1, :], CS[:, 1, :], RS[:, :], ALU.mult), c)
                    b1, t1 = gemm_tile("ret_t", 8 * h + 1, AH, AL, a_ready)
                    ret["q"] = rotate(h, QR, b0, t0, b1, t1)
                    b0, t0 = gemm_tile("ret_t", 8 * h + 2, AH, AL, a_ready)
                    b1, t1 = gemm_tile("ret_t", 8 * h + 3, AH, AL, a_ready)
                    ret["k"] = rotate(h, KR, b0, t0, b1, t1)
                    banks, toks = gemm_tokens("ret_v", h, AH, AL, a_ready)
                    ret["v"] = []
                    for tt in range(4):
                        ret["v"].append(AC(lambda e, tt=tt, b=banks[tt]: e.activation(
                            VR[:, tt, :], BANK[b][:, :], ACT.Copy, scale=rstok[:, tt:tt + 1]), toks[tt], st["rs"],
                            *v_read, *fence_in))
                        bank_free[banks[tt]] = [ret["v"][tt]]
                    PO(lambda e: e.dma_start(DEC[:, :], D["decay"][h]).then_inc(s_dec, 16), *dec_read, *fence_in,
                       inc=False)
                    ret["dec"] = (s_dec, 16 * (h + 1))

                def scores(h):
                    for j in range(4):
                        n = S - 128 * j
                        b = gemm_bank()
                        for d in range(2):
                            tok = PE(lambda e, d=d, j=j, n=n, b=b: e.matmul(
                                BANK[b][:, 0:n], KR[:, d, j * 128:(j + 1) * 128], QR[:, d, j * 128:S],
                                start=(d == 0), stop=(d == 1)), ret["q"], ret["k"], bank_free[b], inc=(d == 1))
                        ret["s", j] = DV(lambda e, j=j, n=n, b=b: e.tensor_tensor(
                            ST[j][:, :], BANK[b][:, 0:n], DEC[:, 0:n], ALU.mult), tok, ret["dec"], st_read[j],
                            *fence_in)
                        bank_free[b] = [ret["s", j]]
                    q_read[:] = [tok]
                    dec_read[:] = [ret["s", 3]]

                def values(h):
                    for j in range(4):
                        n = S - 128 * j
                        for et in range(4):
                            tok = PE(lambda e, et=et, j=j, n=n: e.matmul(
                                BANK[4 + et][:, j * 128:S], VR[:, j, et * 128:(et + 1) * 128], ST[j][:, :],
                                start=(j == 0), stop=(j == 3)), ret["s", j], ret["v"][j],
                                bank_free[4 + et] if j == 0 else None, inc=(j == 3 or et == 3))
                            if j == 3:
                                ret["o", et] = tok
                        st_read[j] = tok
                    v_read[:] = [tok]
                    for et in range(4):
                        ret["oc", et] = AC(lambda e, et=et: e.activation(OR[:, et, :], BANK[4 + et][:, :], ACT.Copy),
                                           ret["o", et], *or_read, *fence_in)
                        bank_free[4 + et] = [ret["oc", et]]

                def head_norm(h):
                    for et in range(4):
                        square_in(et, OR[:, et, :], [ret["oc", et]])
                    for tt in range(4):
                        tok = PE(lambda e, tt=tt: e.matmul(BANK[4][:, tt:tt + 1], ACC[:, tt * 128:(tt + 1) * 128],
                                                           ones[:, :], start=True, stop=True),
                                 st["acc"], bank_free[4], inc=(tt == 3))
                    st["acc_read"] = tok
                    a = AC(lambda e: e.activation(rtok[:, 0:4], BANK[4][:, 0:4], ACT.Sqrt, bias=small[:, 63:64],
                                                  scale=1.0 / 512), tok, st.get("rtok_read"))
                    bank_free[4] = [a]
                    r = DV(lambda e: e.reciprocal(rso[:, 0:4], rtok[:, 0:4]), a, ret.get("rso_read"))
                    st["rtok_read"] = r
                    ret["rso"] = r

                def head_norm_spread(h):
                    for tt in range(4):
                        tok = PE(lambda e, tt=tt: e.matmul(
                            BANK[5][:, tt * 128:(tt + 1) * 128], rso[:, tt:tt + 1].broadcast_to([128, 128]),
                            ident[:, :], start=True, stop=True), ret["rso"], bank_free[5], inc=(tt == 3))
                    ret["rso_read"] = tok
                    for et in range(4):
                        ret["on", et] = DV(lambda e, et=et: e.tensor_tensor(OR[:, et, :], OR[:, et, :],
                                                                           BANK[5][:, :], ALU.mult), tok,
                                           st["acc"], ret["oc", et])
                    bank_free[5] = [ret["on", 3]]

                def gate_evac(h, et, b, tok):
                    i = et % 4
                    t = DV(lambda e: e.tensor_tensor(T[i][:, :], BANK[b][:, :], RS[:, :], ALU.mult), tok, *tfree[i])
                    bank_free[b] = [t]
                    st["rs_used"] = [t, ret["v"][3]]
                    ts = AC(lambda e: e.activation(T[i][:, :], T[i][:, :], ACT.Silu), t)

                    def rest():
                        k = 4 * h + et
                        t = DV(lambda e: e.tensor_tensor(T[i][:, :], T[i][:, :], OR[:, et, :], ALU.mult), ts,
                               ret["on", et])
                        hi = AC(lambda e: e.activation(RH[:, k, :], T[i][:, :], ACT.Copy), t, *fence_in)
                        low = DV(lambda e: e.tensor_tensor(RL[:, k, :], T[i][:, :], RH[:, k, :], ALU.subtract), hi,
                                 *fence_in)
                        tfree[i] = [low]
                        r_ready[k] = [hi, low]
                        or_read[:] = [t]
                    return rest

                for h in range(4):
                    heads_qkv(h)
                    if h == 0:
                        distance_bias()
                    scores(h)
                    background += [lambda h=h: values(h), lambda h=h: head_norm(h), lambda h=h: head_norm_spread(h)]
                    late = []
                    for et in range(4):
                        b, tok = gemm_tile("ret_t", 8 * h + 4 + et, AH, AL, a_ready)
                        tick()
                        late.append(gate_evac(h, et, b, tok))
                    for fn in late:
                        fn()
                st["a_free"] = [PE.now()]
            fence_m = fence()
            MR = sb("MR", [128, 8, S], stack=ar)
            m_tok = [None] * 8
            for f in range(8):
                b, tok = gemm_tile("ret_out", f, RH, RL, r_ready)
                branch_out(MR, m_tok, b, tok, f, fence_m)
            post_norm(MR, m_tok, "mix_post0", "ffn_pre0")

        def ffn_block2(names, post, pre, tag):
            fence_m = fence()
            with ExitStack() as am:
                MF = sb("MF" + tag, [128, 8, S], stack=am)
                m_tok = [None] * 8
                ffn_layer(names, lambda f, b, tok: branch_out(MF, m_tok, b, tok, f, fence_m), tag)
                post_norm(MF, m_tok, post, pre)

        ffn_block2(("ffn2_in", "ffn2_out"), "ffn_post0", "kv_norm", "2")

        fence_in = fence()
        with ExitStack() as ar:
            TT = [sb(f"TT{i}", [128, 4, S], stack=ar) for i in range(2)]
            KHH = sb("KHH", [128, 8, S], F32R, ar)
            KLL = sb("KLL", [128, 8, S], F32R, ar)
            VS = sb("VS", [128, 4, 512], stack=ar)
            GT = sb("GT", [128, 4, 48], stack=ar)
            KCH = sb("KCH", [128, 4, 32], F32R, ar)
            KCL = sb("KCL", [128, 4, 32], F32R, ar)
            VC = sb("VC", [32, 4, 64], stack=ar)
            s_w1, s_w2 = sem("s_w1"), sem("s_w2")
            s_tt = [sem(f"s_tt{i}") for i in range(2)]
            at = {}

            def load_bias(g, *free):
                PO(lambda e: e.dma_start(TT[g % 2][:, :, :],
                                         bass.AP(D["scratch"].tensor, 4 * g * 640, [[1, 128], [640, 4], [1, 512]]))
                   .then_inc(s_tt[g % 2], 16), (s_scr, 16), *free, inc=False)

            def stack_parts(src, half, hi_own, hi_other, lo_own, lo_other, ready, *after):
                own = slice(64 * half, 64 * half + 64)
                other = slice(64 - 64 * half, 128 - 64 * half)
                h = AC(lambda e: e.activation(hi_own[own], src[own], ACT.Copy), ready, *after)
                t = [h]
                if hi_other is not None:
                    t.append(AC(lambda e: e.activation(hi_other[other], src[own], ACT.Copy)))
                for dst, rows in ((lo_own, own), (lo_other, other)):
                    if dst is not None:
                        t.append(DV(lambda e, dst=dst, rows=rows: e.tensor_tensor(dst[rows], src[own], hi_own[own],
                                                                                 ALU.subtract), h, *after))
                return t

            with ExitStack() as ac:
                CK = sb("CK", [128, 4, S], stack=ac)
                X2 = sb("X2", [128, 16, 124], stack=ac)
                W1 = sb("W1", [128, 16, 256], stack=ac)
                HC = sb("HC", [128, 2, 124], stack=ac)
                W2 = sb("W2", [128, 2, 2, 128], stack=ac)
                PO(lambda e: e.dma_start(W1[:, :, :], D["cmp_w1"][0]).then_inc(s_w1, 16), *fence_in, inc=False)
                PO(lambda e: e.dma_start(W2[:, :, :, :], D["cmp_w2"]).then_inc(s_w2, 16), inc=False)
                load_bias(0)
                load_bias(1)
                kc_zero = [DV(lambda e, k=k: e.memset(k[:, :, :].bitcast(F32), 0.0), *fence_in) for k in (KCH, KCL)]

                def kv_tile(n):
                    b, tok = gemm_tile("kv_t", n, AH, AL, a_ready)
                    if n == 0:
                        st["rs"] = rms_scale()
                    if n < 4:
                        t = DV(lambda e: e.tensor_tensor(CK[:, n, :], BANK[b][:, :], RS[:, :], ALU.mult), tok,
                               st["rs"], *fence_in)
                        at["kv", n] = t
                    else:
                        i = n % 4
                        t = DV(lambda e: e.tensor_tensor(T[i][:, :], BANK[b][:, :], RS[:, :], ALU.mult), tok,
                               st["rs"], *tfree[i])
                        done = []
                        for half in range(2):
                            k = 4 * (n // 2 - 2) + 2 * (n % 2) + half
                            at["k", k] = stack_parts(T[i], half, KHH[:, k, :], KHH[:, k, :], KLL[:, k, :],
                                                     KLL[:, k, :], t, *fence_in)
                            done += at["k", k]
                        tfree[i] = done
                    bank_free[b] = [t]

                def spread(i):
                    for g in range(4):
                        for par in range(2):
                            src = CK[64 * (g % 2):64 * (g % 2) + 64, 2 * i + g // 2, :]
                            win = bass.AP(src.tensor, src.offset + par, [src.ap[0], [2, 16], [16, 31]])
                            t = DV(lambda e, g=g, par=par, win=win: e.tensor_copy(
                                X2[64 * par:64 * par + 64, :, 31 * g:31 * g + 31], win), at["kv", 2 * i + g // 2],
                                at.get("hid"), *fence_in)
                    pe = V("pe_k" if i == 0 else "pe_v", 0, 16).rearrange("p (l o) -> p l o", o=1)
                    at["x2"] = DV(lambda e: e.tensor_tensor(X2[:, :, :], X2[:, :, :],
                                                            pe.broadcast_to([128, 16, 124]), ALU.add), t)

                def hidden(i):
                    for ht in range(2):
                        for lp in range(16):
                            t = PE(lambda e, ht=ht, lp=lp: e.matmul(
                                BANK[4 + ht][:, 0:124], W1[:, lp, ht * 128:ht * 128 + 128], X2[:, lp, :],
                                start=(lp == 0), stop=(lp == 15)), at["x2"], (s_w1, 16 * (i + 1)),
                                bank_free[4 + ht], inc=(lp == 15))
                        at["hc", ht] = AC(lambda e, ht=ht: e.activation(HC[:, ht, :], BANK[4 + ht][:, 0:124],
                                                                        ACT.Silu), t, at.get("hc_read"), *fence_in)
                        bank_free[4 + ht] = [at["hc", ht]]
                    at["hid"] = t
                    if i == 0:
                        PO(lambda e: e.dma_start(W1[:, :, :], D["cmp_w1"][1]).then_inc(s_w1, 16), t, inc=False)

                def compressed(i):
                    b = 6 + i
                    for g in range(4):
                        for ht in range(2):
                            hc = HC[:, ht, 31 * g:31 * g + 31]
                            w2 = W2[:, i, ht, 0:128 - 64 * i]
                            if i == 0:
                                t = PE(lambda e, g=g, ht=ht, hc=hc, w2=w2: e.matmul(
                                    BANK[b][:, 32 * g:32 * g + 31], w2, hc, start=(ht == 0), stop=(ht == 1)),
                                    at["hc", ht], (s_w2, 16), bank_free[b], inc=(g == 3 and ht == 1))
                            else:
                                t = PE(lambda e, g=g, ht=ht, hc=hc, w2=w2: e.matmul(
                                    BANK[b][0:31, 64 * g:64 * g + 64], hc, w2, start=(ht == 0), stop=(ht == 1)),
                                    at["hc", ht], (s_w2, 16), bank_free[b], inc=(g == 3 and ht == 1))
                    at["hc_read"] = t
                    if i == 0:
                        src = BANK[b][:, 0:128].rearrange("p (g n) -> p g n", g=4)[:, :, 0:31]
                        h = AC(lambda e: e.activation(KCH[:, :, 0:31], src, ACT.Copy), t, *kc_zero)
                        t = DV(lambda e: e.tensor_tensor(KCL[:, :, 0:31], src, KCH[:, :, 0:31], ALU.subtract), h)
                        at["kc"] = t
                    else:
                        t = DV(lambda e: e.tensor_copy(VC[0:31, :, :], BANK[b][0:31, 0:256].rearrange(
                            "p (g d) -> p g d", g=4)), t, *fence_in)
                        at["vc"] = t
                    bank_free[b] = [t]

                for n in range(6):
                    kv_tile(n)
                spread(0)
                kv_tile(6)
                kv_tile(7)
                banks, toks = gemm_tokens("kv_v", 0, AH, AL, a_ready)
                st["a_free"] = [PE.now()]
                at["v"] = []
                for tt in range(4):
                    at["v"].append(AC(lambda e, tt=tt, b=banks[tt]: e.activation(
                        VS[:, tt, :], BANK[b][:, :], ACT.Copy, scale=rstok[:, tt:tt + 1]), toks[tt], st["rs"],
                        *fence_in))
                    bank_free[banks[tt]] = [at["v"][tt]]
                for f in range(8):
                    a_ready[f] = split_in(f, "mix_pre1", [final["h", f]], st["a_free"])
                    xt_read[f] = [xt_read[f], a_ready[f]]
                hidden(0)
                spread(1)
                compressed(0)
                hidden(1)
                compressed(1)
            fence_q = fence() + [(s_w1, 32)]
            QHL = [sb(f"QHL{i}", [128, 4, S], F32R, ar) for i in range(2)]
            OT = sb("OT", [128, 4, 1024], stack=ar)
            SS = [sb(f"SS{i}", [128, S], stack=ar) for i in range(4)] + SQ
            PT = [sb(f"PT{i}", [128, S], stack=ar) for i in range(3)] + [ACC]
            NM = sb("NM", [128, 8], stack=ar)
            SM = sb("SM", [128, 4, 4], stack=ar)
            CF = sb("CF", [128, 4, 4], stack=ar)
            q_read = {}
            info = {}

            def query_evac(n, b, tok):
                g, i = n // 2, n % 4
                t = DV(lambda e: e.scalar_tensor_tensor(T[i][:, :], BANK[b][:, :], 0.125, RS[:, :], ALU.mult,
                                                        ALU.mult), tok, st["rs"], *tfree[i])
                bank_free[b] = [t]
                st["rs_used"] = [t, at["v"][3]]
                done = []
                for half in range(2):
                    q = QHL[g % 2][:, 2 * (n % 2) + half, :]
                    done += stack_parts(T[i], half, q, None, None, q, t, *fence_q, q_read.get(g - 2))
                tfree[i] = done
                at["q", n] = done

            b, tok = gemm_tile("nsa_t", 8, AH, AL, a_ready)
            t = DV(lambda e, b=b: e.tensor_tensor(T[3][0:48, :], BANK[b][0:48, :], RS[0:48, :], ALU.mult), tok,
                   st["rs"], *tfree[3])
            bank_free[b] = [t]
            t_sig = AC(lambda e: e.activation(T[3][0:48, :], T[3][0:48, :], ACT.Sigmoid), t)
            for n in range(2):
                b, tok = gemm_tile("nsa_t", n, AH, AL, a_ready)
                query_evac(n, b, tok)
                if n == 0:
                    for tt in range(4):
                        tok = PE(lambda e, tt=tt: e.transpose(BANK[6][:, 48 * tt:48 * tt + 48],
                                                              T[3][0:48, tt * 128:(tt + 1) * 128], ident[0:48, 0:48]),
                                 t_sig, bank_free[6], inc=(tt == 3))
                    tfree[3] = [tok]
                    at["gate"] = DV(lambda e: e.tensor_copy(GT[:, :, :], BANK[6][:, 0:192].rearrange(
                        "p (a b) -> p a b", a=4)), tok, *fence_in)
                    bank_free[6] = [at["gate"]]

            steps = [(g, i, r, br) for g in range(4) for i in range(4) for r in range(4) for br in range(3)]
            TURN, MIX = 3, 6
            NSS, NPT = len(SS), len(PT)
            ss_free, pt_free = {}, {}
            between = []

            def fill(n=1):
                for _ in range(n):
                    if between:
                        between.pop(0)()


            def step_scores(s):
                g, i, r, br = steps[s]
                h = 4 * g + r
                keys = 7 + 8 * i if br == 0 else 128 * (i + 1)
                even = keys + keys % 2
                b = s % 2
                q = QHL[g % 2][:, r, i * 128:(i + 1) * 128]
                if br == 0:
                    parts = (KCH[:, g, 0:even], KCL[:, g, 0:even])
                    k_ready = [at["kc"]]
                else:
                    parts = (KHH[:, 4 * (br - 1) + g, 0:keys], KLL[:, 4 * (br - 1) + g, 0:keys])
                    k_ready = at["k", 4 * (br - 1) + g]
                for n, k in enumerate(parts):
                    t = PE(lambda e, n=n, k=k: e.matmul(BANK[b][:, 0:even], q, k, start=(n == 0), stop=(n == 1)),
                           at["q", h // 2], k_ready, bank_free[b], inc=(n == 1))
                if (i, r, br) == (3, 3, 2):
                    q_read[g] = t
                row = TT[g % 2][:, r, :]
                bias = bass.AP(row.tensor, row.offset + 128 * i + (96 if br == 0 else 127),
                               [row.ap[0], [-16 if br == 0 else -1, keys]])
                m = s % 8
                t = DV(lambda e: e.tensor_tensor_reduce(SS[s % NSS][:, 0:keys], BANK[b][:, 0:keys], bias, -1.0, -GUARD,
                                                        ALU.add, ALU.min, NM[:, m:m + 1]), t,
                       (s_tt[g % 2], 16 * (g // 2 + 1)), ss_free.get(s - NSS), info.get(("e", s - 8)), *fence_q)
                bank_free[b] = [t]
                fill()
                if (i, r, br) == (3, 3, 2) and g < 2:
                    load_bias(g + 2, t)
                o = (s // 3) % 4
                info["e", s] = AC(lambda e: e.activation(SS[s % NSS][:, 0:keys], SS[s % NSS][:, 0:keys], ACT.Exp,
                                                         bias=NM[:, m:m + 1], scale=-1.0,
                                                         accum_out=SM[:, o, br:br + 1]), t,
                                  info.get(("cf", s // 3 - 4)), *fence_q)

            def step_turn(s):
                g, i, r, br = steps[s]
                b = 2 + s % 2
                k = 7 + 8 * i if br == 0 else 128
                n = 1 if br == 0 else i + 1
                for j in range(n):
                    t = PE(lambda e, j=j: e.transpose(BANK[b][0:k, j * 128:(j + 1) * 128],
                                                      SS[s % NSS][:, j * 128:j * 128 + k], ident[:, :]),
                           info["e", s], bank_free[b], inc=(j == n - 1))
                ss_free[s] = t
                to, frm = PT[s % NPT][0:k, 0:128 * n], BANK[b][0:k, 0:128 * n]
                if br == 1:
                    t = DV(lambda e: e.tensor_copy(to, frm), t, pt_free.get(s - NPT), *fence_q)
                else:
                    t = AC(lambda e: e.activation(to, frm, ACT.Copy), t, pt_free.get(s - NPT), *fence_q)
                bank_free[b] = [t]
                info["p", s] = t

            def step_values(s):
                g, i, r, br = steps[s]
                h = 4 * g + r
                b = 4 + (s // 3) % 2
                k = 7 + 8 * i
                o = (s // 3) % 4
                if br == 0:
                    t = PE(lambda e: e.matmul(BANK[b][:, 0:64], PT[s % NPT][0:k, 0:128], VC[0:k, g, :], start=True,
                                              stop=True), info["p", s], at["vc"], bank_free[b])
                    c = SM[:, o, 0:3]

                    def floor():
                        info["d"] = DV(lambda e: e.tensor_scalar(c, c, TINY, None, ALU.max), info["e", s + 2])

                    def invert():
                        info["d"] = DV(lambda e: e.reciprocal(c, c), info["d"])

                    def weigh():
                        info["cf", s // 3] = DV(lambda e: e.tensor_tensor(
                            CF[:, o, 0:3], c, GT[:, i, 3 * h:3 * h + 3], ALU.mult), info["d"], at["gate"],
                            info.get(("done", s // 3 - 4)), *fence_q)
                    between.extend([floor, invert, weigh])
                else:
                    c = 64 * g + 256 * (br - 1)
                    for j in range(i + 1):
                        t = PE(lambda e, j=j: e.matmul(BANK[b][:, 64 * br:64 * br + 64],
                                                       PT[s % NPT][:, j * 128:(j + 1) * 128], VS[:, j, c:c + 64],
                                                       start=(j == 0), stop=(j == i)), info["p", s], at["v"][j],
                               inc=(j == i))
                pt_free[s] = t
                if br == 2:
                    dst = OT[:, i, 64 * h:64 * h + 64]

                    def first():
                        info["o"] = DV(lambda e: e.tensor_scalar(dst, BANK[b][:, 0:64], CF[:, o, 0:1], None,
                                                                 ALU.mult), t, info["cf", s // 3], *fence_q)

                    def add(q):
                        info["o"] = DV(lambda e: e.scalar_tensor_tensor(
                            dst, BANK[b][:, 64 * q:64 * q + 64], CF[:, o, q:q + 1], dst, ALU.mult, ALU.add),
                            info["o"])
                        if q == 2:
                            bank_free[b] = [info["o"]]
                            info["done", s // 3] = info["o"]
                    between.extend([first, lambda: add(1), lambda: add(2)])

            def projection_pieces(n):
                parts, done = gemm_parts("nsa_t", n, AH, AL, a_ready, 6 + n % 2)

                def last():
                    parts[-1]()
                    query_evac(n, 6 + n % 2, done[0])
                return parts[:-1] + [last]

            N = len(steps)
            for s in range(N + MIX):
                if s < N:
                    g, i, r, br = steps[s]
                    if (i, r, br) == (0, 0, 0) and g < 3:
                        flush()
                        background += projection_pieces(2 * g + 2) + projection_pieces(2 * g + 3)
                    step_scores(s)
                if TURN <= s < N + TURN:
                    step_turn(s - TURN)
                fill()
                if s >= MIX:
                    step_values(s - MIX)
                tick()
            fill(len(between))
            flush()
            assert not between
            st["sq"] = [[PE.now()], [PE.now()]]
            st["acc_read"] = PE.now()
            st["a_free"] = [PE.now()]
            fence_o = [DV.now()]
            for f in range(8):
                b = 2 + f % 4
                for i in range(4):
                    t = PE(lambda e, f=f, i=i, b=b: e.transpose(BANK[b][:, i * 128:(i + 1) * 128],
                                                               OT[:, i, f * 128:(f + 1) * 128], ident[:, :]),
                           *fence_o, bank_free[b], inc=(i == 3))
                hi = AC(lambda e, f=f, b=b: e.activation(AH[:, f, :], BANK[b][:, :], ACT.Copy), t, *st["a_free"])
                low = DV(lambda e, f=f, b=b: e.tensor_tensor(AL[:, f, :], BANK[b][:, :], AH[:, f, :], ALU.subtract),
                         hi, *st["a_free"])
                bank_free[b] = [low]
                a_ready[f] = [hi, low]
        fence_m = fence()
        with ExitStack() as ar:
            MN = sb("MN", [128, 8, S], stack=ar)
            m_tok = [None] * 8
            for f in range(8):
                b, tok = gemm_tile("nsa_out", f, AH, AL, a_ready)
                branch_out(MN, m_tok, b, tok, f, fence_m)
            st["a_free"] = [PE.now()]
            post_norm(MN, m_tok, "mix_post1", "ffn_pre1")
        ffn_block2(("ffn3_in", "ffn3_out"), "ffn_post1", None, "3")

        s_out = sem("s_out")
        for f in range(8):
            SP(lambda e, f=f: e.dma_start(out[f], XT[:, f, :]).then_inc(s_out, 16), final["h", f], inc=False)
        assert len(units) == UNITS_TOTAL, len(units)

        block = ctx.enter_context(nc.Block())

        @block.sync
        def _(eng):
            SP.play(eng)
            eng.wait_ge(s_out, 128)

        @block.scalar
        def _(eng):
            AC.play(eng)

        @block.vector
        def _(eng):
            DV.play(eng)

        @block.tensor
        def _(eng):
            PE.play(eng)

        @block.gpsimd
        def _(eng):
            PO.play(eng)


def feature_tiles(w, columns=None):
    w = w if columns is None else w[:, columns]
    k, m = w.shape
    if m % 128:
        w = np.concatenate([w, np.zeros((k, 128 - m % 128), w.dtype)], axis=1)
        m = w.shape[1]
    return np.ascontiguousarray(w.reshape(k // 128, 128, m // 128, 128).transpose(2, 1, 0, 3).reshape(m // 128, 128, k))


def token_tiles(w):
    k, m = w.shape
    return np.ascontiguousarray(w.reshape(8, 128, m // 512, 512).transpose(2, 1, 0, 3).reshape(m // 512, 128, 4096))


def shape_constants():
    f32 = np.float32
    pos = np.arange(S, dtype=f32)
    theta = (f32(1.0) / np.power(f32(10000.0), np.linspace(0.0, 1.0, 128, dtype=f32))).astype(f32)
    ang = (theta[:, None] * pos[None, :]).astype(f32)
    cossin = np.concatenate([np.cos(ang), np.sin(ang)], axis=1).astype(f32)
    log_gamma = np.log(f32(1.0) - np.power(f32(2.0), f32(-5.0) - np.arange(4, dtype=f32))).astype(f32)
    rel = pos[None, :] - np.arange(128, dtype=f32)[:, None]
    decay = np.where(rel >= 0, np.exp(np.maximum(rel, 0.0)[None] * log_gamma[:, None, None]), 0.0) / 16.0
    dist = np.arange(640) - 127
    n = np.maximum(dist, 0)
    large = 16 + (np.log(np.maximum(n, 1).astype(f32) / f32(16)) / f32(math.log(8.0)) * f32(16)).astype(np.int32)
    bucket = np.where(n < 16, n, np.minimum(large, 31))
    onehot = (bucket[None, :] == np.arange(32)[:, None]) & (dist >= 0)[None, :]
    onehot = np.concatenate([onehot, (dist < 0)[None, :]], axis=0)
    return {"ident": np.eye(128, dtype=f32), "cossin": cossin, "decay": decay.astype(f32),
            "onehot": onehot.astype(f32)}


def laid_out(inp):
    a = {k: np.asarray(v) for k, v in inp.items()}
    cols = lambda v: v.reshape(-1, 128).T
    vecs = {
        "norm1": cols(a["norm1"][0]), "norm2": cols(a["norm2"][0]), "final_norm": cols(a["final_norm"]),
        "mix_pre0": cols(a["mix_norm_pre_2"][0]), "mix_post0": cols(a["mix_norm_post_2"][0]),
        "ffn_pre0": cols(a["ffn_norm_pre_2"][0]), "ffn_post0": cols(a["ffn_norm_post_2"][0]),
        "kv_norm": cols(a["kv_norm_2"]),
        "mix_pre1": cols(a["mix_norm_pre_2"][1]), "mix_post1": cols(a["mix_norm_post_2"][1]),
        "ffn_pre1": cols(a["ffn_norm_pre_2"][1]), "ffn_post1": cols(a["ffn_norm_post_2"][1]),
        "conv_w": a["conv_w"][0].reshape(4, 4, 128).transpose(2, 1, 0).reshape(128, 16),
        "conv_b": cols(a["conv_b"][0]), "lru_ba": cols(a["lru_ba"][0]), "lru_bi": cols(a["lru_bi"][0]),
        "lru_lambda": cols(a["lru_lambda"][0]), "b_alpha": cols(a["gla_b_alpha"][0]),
        "gla_norm": cols(a["gla_norm"][0]),
        "pe_k": a["cmp_pe_k_2"].reshape(16, 128).T, "pe_v": a["cmp_pe_v_2"].reshape(16, 128).T,
    }
    c = shape_constants()
    d = {
        "xT": a["x"][0].reshape(S, 8, 128).transpose(2, 1, 0).reshape(128, 8 * S),
        "vec": np.concatenate([vecs[n] for n, _ in VEC_NAMES], axis=1),
        "ident": c["ident"], "cossin": c["cossin"], "decay": c["decay"],
        "onehot": np.concatenate(
            [c["onehot"], np.concatenate([a["rel_bias_2"], np.full((1, 16), NEG, np.float32)], axis=0)], axis=1),
        "lru_wa": a["lru_wa"][0], "lru_wi": a["lru_wi"][0], "w_alpha": a["gla_w_alpha"][0],
    }
    w = a["w_in"][0]
    d["w_in_t"] = feature_tiles(w, np.r_[0:1536, 2048:2576])
    d["w_in_v"] = token_tiles(w[:, 1536:2048])
    d["w_out"] = feature_tiles(a["w_out"][0])
    half = 2816
    gate_up = np.concatenate([np.r_[128 * j:128 * j + 128, half + 128 * j:half + 128 * j + 128] for j in range(22)])
    for n, (wi, wo) in enumerate(((a["w_ffn_in"][0], a["w_ffn_out"][0]), (a["ffn_w_in_2"][0], a["ffn_w_out_2"][0]),
                                  (a["ffn_w_in_2"][1], a["ffn_w_out_2"][1])), 1):
        d[f"ffn{n}_in"] = feature_tiles(wi, gate_up)
        d[f"ffn{n}_out"] = feature_tiles(wo)
    w = a["ret_w_in_2"][0]
    order = []
    for h in range(4):
        for base in (0, 1024):
            at = base + 256 * h
            order += [np.arange(at, at + 256, 2), np.arange(at + 1, at + 256, 2)]
        order.append(np.arange(4096 + 512 * h, 4096 + 512 * h + 512))
    d["ret_t"] = feature_tiles(w, np.concatenate(order))
    d["ret_v"] = token_tiles(w[:, 2048:4096])
    d["ret_out"] = feature_tiles(a["ret_w_out_2"][0])
    w = a["kv_w_2"]
    d["kv_t"] = feature_tiles(w, np.r_[0:512, 512:768, 1024:1280])
    d["kv_v"] = token_tiles(w[:, np.r_[768:1024, 1280:1536]])
    w = a["nsa_w_in_2"][0]
    d["nsa_t"] = feature_tiles(w)
    d["nsa_out"] = feature_tiles(a["nsa_w_out_2"][0])
    w1 = [a[n].reshape(16, 128, 256).transpose(1, 0, 2) for n in ("cmp_w1_k_2", "cmp_w1_v_2")]
    d["cmp_w1"] = np.stack(w1)
    w2 = [a[n].reshape(2, 128, 64).transpose(1, 0, 2) for n in ("cmp_w2_k_2", "cmp_w2_v_2")]
    w2 = np.stack(w2, axis=1)
    d["cmp_w2"] = np.concatenate([w2, w2], axis=3)
    return {k: np.ascontiguousarray(v) for k, v in d.items()}


def kernel(**inputs):
    import concourse.bacc as _bacc
    from concourse.bass_utils import run_bass_kernel_spmd as _run

    arrays = laid_out(inputs)
    nc = _bacc.Bacc("TRN2", target_bir_lowering=False, num_devices=1)
    D = {n: nc.dram_tensor("in_" + n, a.shape, F32, kind="ExternalInput").ap() for n, a in arrays.items()}
    D["scratch"] = nc.dram_tensor("scratch", (16, 640), F32, kind="Internal").ap()
    out = nc.dram_tensor("out", (8, 128, S), F32, kind="ExternalOutput").ap()
    build(nc, D, out)
    r = _run(nc, [{"in_" + n: a for n, a in arrays.items()}], core_ids=[0])
    got = np.asarray(r.results[0]["out"])
    return got.reshape(1024, S).T.reshape(1, S, 1024)
```

```python
import math
from contextlib import ExitStack

import concourse.bass as bass
import numpy as np
from concourse import mybir

F32 = mybir.dt.float32
F32R = mybir.dt.float32r
ACT = mybir.ActivationFunctionType
ALU = mybir.AluOpType
AX_X = mybir.AxisListType.X

S = 512
EPS = 1e-6
NEG = -1.0e30
GUARD = -1.0e20
TINY = 1.1754943508222875e-38

RAW_SLOTS = 3
W_SLOTS = 3
LOOK = 2
GEMM_BANKS = 4
ORDER = (0, 3, 1, 2)
TURN_BANKS = (2, 3, 6)

VEC_NAMES = [
    ("norm1", 8), ("norm2", 8), ("final_norm", 8), ("mix_pre0", 8), ("mix_post0", 8), ("ffn_pre0", 8),
    ("ffn_post0", 8), ("kv_norm", 8), ("mix_pre1", 8), ("mix_post1", 8), ("ffn_pre1", 8), ("ffn_post1", 8),
    ("conv_w", 16), ("conv_b", 4), ("lru_ba", 4), ("lru_bi", 4), ("lru_lambda", 4), ("b_alpha", 2),
    ("gla_norm", 1), ("pe_k", 16), ("pe_v", 16),
]
VEC_AT = {}
_n = 0
for _name, _w in VEC_NAMES:
    VEC_AT[_name] = _n
    _n += _w
NVEC = _n

FEATURE_MAJOR = {"w_in_t": 8, "w_out": 8, "ffn1_in": 8, "ffn1_out": 22, "ret_t": 8, "ret_out": 16, "ffn2_in": 8,
                 "ffn2_out": 22, "kv_t": 8, "nsa_t": 8, "nsa_out": 8, "ffn3_in": 8, "ffn3_out": 22}
UNITS_TOTAL = 21 + 8 + 68 + 48 + 16 + 68 + 12 + 9 + 8 + 68


class Queue:

    def __init__(self, sem):
        self.sem, self.count, self.items = sem, 0, []

    def __call__(self, fn, *waits, inc=True):
        self.items.append((fn, waits, inc))
        if not inc:
            return None
        self.count += 1
        return (self.sem, self.count)

    def now(self):
        return (self.sem, self.count)

    def play(self, eng):
        seen = {}

        def need(w):
            if w is None:
                return
            if isinstance(w, list):
                for x in w:
                    need(x)
                return
            sem, value = w
            if value > seen.get(sem.name, 0):
                seen[sem.name] = value
                eng.wait_ge(sem, value)

        for fn, waits, inc in self.items:
            need(list(waits))
            ins = fn(eng)
            if inc:
                ins.then_inc(self.sem, 1)


def build(nc, D, out):
    with ExitStack() as ctx:
        def sem(name):
            return ctx.enter_context(nc.semaphore(name))

        def sb(name, shape, dt=F32, stack=ctx):
            return stack.enter_context(nc.sbuf_tensor(name, shape, dt))

        PE, AC, DV, SP, PO = (Queue(sem(n)) for n in ("pe", "act", "dve", "sp", "pool"))
        every = (PE, AC, DV)

        def fence():
            return [q.now() for q in every]

        XT = sb("XT", [128, 8, S])
        AH = sb("AH", [128, 8, S], F32R)
        AL = sb("AL", [128, 8, S], F32R)
        RAW = [sb(f"RAW{i}", [128, 1024]) for i in range(RAW_SLOTS)]
        WH = [sb(f"WH{i}", [128, 1024], F32R) for i in range(W_SLOTS)]
        WL = [sb(f"WL{i}", [128, 1024], F32R) for i in range(W_SLOTS)]
        ident = sb("ident", [128, 128])
        ones = sb("ones", [128, 1])
        RS = sb("RS", [128, S])
        ACC = sb("ACC", [128, S])
        SQ = [sb(f"SQ{i}", [128, S]) for i in range(2)]
        T = [sb(f"T{i}", [128, S]) for i in range(4)]
        vec = sb("vec", [128, NVEC])
        small = sb("small", [128, 64])
        rtok = sb("rtok", [128, 16])
        rstok = sb("rstok", [128, 4])
        rso = sb("rso", [128, 16])
        sums = sb("sums", [128, 4])
        BANK = [ctx.enter_context(nc.psum_tensor(f"bank{i}", [128, 512], F32)) for i in range(8)]
        bank_free = [[] for _ in range(8)]

        def V(name, i=0, n=1):
            at = VEC_AT[name] + i
            return vec[:, at:at + n]

        s_const = sem("s_const")
        s_x = [sem(f"s_x{f}") for f in range(8)]
        const_ready = (s_const, 32)

        def load_x(f):
            SP(lambda e: e.dma_start(XT[:, f, :], D["xT"][:, f * S:(f + 1) * S]).then_inc(s_x[f], 16), inc=False)

        AC(lambda e: e.dma_start(vec[:, :], D["vec"]).then_inc(s_const, 16), inc=False)
        AC(lambda e: e.dma_start(ident[:, :], D["ident"]).then_inc(s_const, 16), inc=False)
        t_ones = DV(lambda e: e.memset(ones[:, :], 1.0))

        s_raw = [sem(f"s_raw{i}") for i in range(RAW_SLOTS)]
        units = []
        unit_hi, unit_lo, unit_used = {}, {}, {}
        state = {"dma": 0, "prep": 0, "bank": 0, "hold": UNITS_TOTAL}

        def weight_dma():
            u = state["dma"]
            if u >= UNITS_TOTAL:
                return
            state["dma"] += 1
            r = u % RAW_SLOTS

            def go(e):
                src, n = units[u]
                e.dma_start(RAW[r][:, 0:n], src).then_inc(s_raw[r], 16)
            SP(go, unit_hi.get(u - RAW_SLOTS), unit_lo.get(u - RAW_SLOTS), inc=False)

        def weight_prep():
            u = state["prep"]
            if u >= UNITS_TOTAL:
                return
            state["prep"] += 1
            r, w = u % RAW_SLOTS, u % W_SLOTS
            landed = (s_raw[r], 16 * (u // RAW_SLOTS + 1))
            used = unit_used.get(u - W_SLOTS)
            unit_hi[u] = AC(lambda e: e.activation(WH[w][:, 0:units[u][1]], RAW[r][:, 0:units[u][1]], ACT.Copy),
                            landed, used)
            unit_lo[u] = DV(lambda e: e.tensor_tensor(WL[w][:, 0:units[u][1]], RAW[r][:, 0:units[u][1]],
                                                      WH[w][:, 0:units[u][1]], ALU.subtract),
                            landed, used, unit_hi[u])
            weight_dma()

        for f in range(RAW_SLOTS):
            load_x(f)
            weight_dma()
        for f in range(RAW_SLOTS, 8):
            load_x(f)

        def look_ahead(u):
            while state["prep"] <= min(u + LOOK, UNITS_TOTAL - 1):
                weight_prep()

        def next_unit(src, n):
            u = len(units)
            units.append((src, n))
            look_ahead(min(u, state["hold"]))
            return u

        def gemm_bank():
            b = state["bank"]
            state["bank"] = (b + 1) % GEMM_BANKS
            return b

        def gemm_parts(name, mt, in_h, in_l, ready, b, by_pass=False):
            kt = FEATURE_MAJOR[name]
            done = []
            parts = []
            for kk in range(kt):
                def part(kk=kk, passes=range(3)):
                    k = kk % 8
                    if k == 0 and 0 in passes:
                        nk = min(8, kt - kk)
                        part_unit[0] = next_unit(D[name][mt, :, kk * 128:(kk + nk) * 128], nk * 128)
                    u = part_unit[0]
                    w = u % W_SLOTS
                    sl = slice(k * 128, (k + 1) * 128)
                    end = k == 7 or kk == kt - 1
                    for n in passes:
                        wt, x = ((WH[w], in_h), (WH[w], in_l), (WL[w], in_h))[n]
                        first, last = kk == 0 and n == 0, kk == kt - 1 and n == 2
                        waits = [ready[kk][n] if isinstance(ready[kk], list) else ready[kk]] if n < 2 else []
                        if first:
                            waits += [bank_free[b]]
                        waits += [unit_hi[u]] if n == 0 else [unit_lo[u]] if n == 2 else []
                        tok = PE(lambda e, wt=wt, x=x, first=first, last=last: e.matmul(
                            BANK[b][:, :], wt[:, sl], x[:, kk, :], start=first, stop=last), *waits,
                            inc=end and n == 2)
                    if end and 2 in passes:
                        unit_used[u] = tok
                    if kk == kt - 1 and 2 in passes:
                        done.append(tok)
                parts.append(part)
            part_unit = [None]
            if by_pass:
                parts = [lambda n=n, part=part: part(passes=(n,)) for n in range(3) for part in parts]
            return parts, done

        def gemm_tile(name, mt, in_h, in_l, ready, by_pass=False):
            b = gemm_bank()
            parts, done = gemm_parts(name, mt, in_h, in_l, ready, b, by_pass)
            for part in parts:
                part()
            return b, done[0]

        def gemm_tokens(name, c, in_h, in_l, ready):
            banks = [gemm_bank() for _ in range(4)]
            toks = [None] * 4
            for q in range(4):
                u = next_unit(D[name][c, :, q * 1024:(q + 1) * 1024], 1024)
                w = u % W_SLOTS
                for tt in range(4):
                    for k in range(2):
                        kk = 2 * q + k
                        sl = slice(k * 512, (k + 1) * 512)
                        for n, (wt, x) in enumerate(((WH[w], in_h), (WH[w], in_l), (WL[w], in_h))):
                            first = kk == 0 and n == 0
                            last = kk == 7 and n == 2
                            waits = [ready[kk]] + ([bank_free[banks[tt]]] if first else [])
                            waits += [unit_hi[u]] if n < 2 else [unit_lo[u]]
                            toks[tt] = PE(lambda e, b=banks[tt], wt=wt, x=x, sl=sl, kk=kk, tt=tt, first=first, last=last:
                                          e.matmul(BANK[b][:, :], x[:, kk, tt * 128:(tt + 1) * 128], wt[:, sl],
                                                   start=first, stop=last),
                                          *waits, inc=(k == 1 and n == 2))
                unit_used[u] = toks[3]
            return banks, toks

        background = []

        def tick(n=1):
            for _ in range(n):
                if background:
                    background.pop(0)()

        def flush():
            while background:
                background.pop(0)()

        st = {"acc": None, "sq": [None, None], "a_free": [], "rs_used": [], "sums": None}

        def square_in(f, src, ready, last=7):
            i = f % 2
            t = AC(lambda e: e.activation(SQ[i][:, :] if f else ACC[:, :], src, ACT.Square), *ready,
                   st["sq"][i], None if f else st.get("acc_read"), None if f else st["acc"])
            if f == last:
                st["tail"] = (i, t)
            elif f:
                st["acc"] = DV(lambda e: e.tensor_tensor(ACC[:, :], ACC[:, :], SQ[i][:, :], ALU.add), t, st["acc"])
                st["sq"][i] = st["acc"]
            else:
                st["acc"] = t
            return t

        def row_sums():
            i, tail = st["tail"]
            for tt in range(4):
                cols = slice(tt * 128, (tt + 1) * 128)
                PE(lambda e, tt=tt, cols=cols: e.matmul(BANK[4][:, tt:tt + 1], ACC[:, cols], ones[:, :], start=True,
                                                        stop=False), st["acc"], bank_free[4], t_ones, inc=False)
                tok = PE(lambda e, tt=tt, cols=cols: e.matmul(BANK[4][:, tt:tt + 1], SQ[i][:, cols], ones[:, :],
                                                              start=False, stop=True), tail, inc=(tt == 3))
            st["acc_read"], st["sq"][i] = tok, tok
            return tok

        def square_to_sums(f, src, ready):
            if f > 1 and f % 2 == 0:
                add_pair(f // 2 - 1)
            i = f % 2
            t = AC(lambda e: e.activation(SQ[i][:, :], src, ACT.Square), *ready, st["sq"][i])
            st["square", f] = t
            if f % 2:
                st["pair", f // 2] = None
            return t

        def add_pair(p):
            if st["pair", p] is None:
                t = DV(lambda e: e.tensor_tensor(SQ[1][:, :], SQ[1][:, :], SQ[0][:, :], ALU.add),
                       st["square", 2 * p], st["square", 2 * p + 1])
                st["pair", p] = st["sq"][0] = t

        def add_to_sums(f):
            if f % 2 == 0:
                return
            p = f // 2
            add_pair(p)
            for tt in range(4):
                tok = PE(lambda e, tt=tt: e.matmul(BANK[4][:, 4 * tt + p:4 * tt + p + 1],
                                                   SQ[1][:, tt * 128:(tt + 1) * 128], ones[:, :], start=True,
                                                   stop=True),
                         st["pair", p], bank_free[4] if p == 0 else None, t_ones, inc=(tt == 3))
            st["sq"][1] = tok
            if f == 7:
                t = DV(lambda e: e.tensor_reduce(sums[:, :], BANK[4][:, 0:16].rearrange("p (a f) -> p a f", f=4),
                                                 AX_X, ALU.add), tok, st.get("sums_read"))
                bank_free[4] = [t]
                st["sums"] = t

        def rms_rows(dst, src, n, count, tok, *after):
            a = AC(lambda e: e.activation(rtok[:, 0:n], src[:, 0:n], ACT.Sqrt, bias=small[:, 63:64],
                                          scale=1.0 / count), tok, t_eps, st.get("rtok_read"))
            if src is sums:
                st["sums_read"] = a
            else:
                bank_free[4] = [a]
            r = DV(lambda e: e.reciprocal(dst[:, 0:n], rtok[:, 0:n]), a, *after)
            st["rtok_read"] = r
            return r

        def rms_begin():
            src, tok = (sums, st["sums"]) if st["sums"] else (BANK[4], row_sums())
            st["sums"] = None
            st["rstok"] = rms_rows(rstok, src, 4, 1024, tok, st.get("rstok_read"), *st["rs_used"])

        def rms_end(keep=True):
            for tt in range(4):
                tok = PE(lambda e, tt=tt: e.matmul(BANK[5][:, tt * 128:(tt + 1) * 128],
                                                   rstok[:, tt:tt + 1].broadcast_to([128, 128]), ident[:, :],
                                                   start=True, stop=True),
                         st["rstok"], bank_free[5], const_ready, inc=(tt == 3))
            st["rstok_read"] = tok
            if not keep:
                return tok
            c = DV(lambda e: e.tensor_copy(RS[:, :], BANK[5][:, :]), tok, *st["rs_used"])
            bank_free[5] = [c]
            st["rs_used"] = []
            st["rs"] = c
            return c

        def rms_scale():
            rms_begin()
            return rms_end(keep=False)

        def high_part(f, gain, ready, write_after=()):
            return AC(lambda e: e.activation(AH[:, f, :], XT[:, f, :], ACT.Copy, scale=V(gain, f)), *ready,
                      const_ready, *write_after)

        def low_part(f, gain, high, ready, write_after=()):
            return DV(lambda e: e.scalar_tensor_tensor(AL[:, f, :], XT[:, f, :], V(gain, f), AH[:, f, :], ALU.mult,
                                                       ALU.subtract), high, *ready, *write_after)

        def split_in(f, gain, ready, write_after=()):
            h = high_part(f, gain, ready, write_after)
            return [h, low_part(f, gain, h, ready, write_after)]

        t_eps = DV(lambda e: e.memset(small[:, 63:64], EPS))

        a_ready = [None] * 8
        xt_read = [None] * 8

        def split_and_square(f, gain, ready, square=square_in):
            a_ready[f] = split_in(f, gain, ready, st["a_free"])
            xt_read[f] = [a_ready[f][1], square(f, XT[:, f, :], ready)]

        def pipelined(scale, update, gain):
            def arrive(f):
                t = final["h", f] = update(f)
                a_ready[f] = [high_part(f, gain, [t], st["a_free"])]
                xt_read[f] = [square_to_sums(f, XT[:, f, :], [t])]

            def low(f):
                t = low_part(f, gain, a_ready[f][0], [final["h", f]], st["a_free"])
                a_ready[f].append(t)
                xt_read[f].append(t)

            def produce(f):
                if f == 0:
                    scale(0)
                    arrive(0)
                    scale(1)
                    low(0)
                if f < 7:
                    arrive(f + 1)
                if f < 6:
                    scale(f + 2)
                if f > 0:
                    low(f)
            return produce

        def abreast(name, tiles, in_h, in_l, ready, skew=0, before=None, after=None, ahead=LOOK):
            banks = [gemm_bank() for _ in tiles]
            group = [gemm_parts(name, m, in_h, in_l, ready, b) for m, b in zip(tiles, banks)]
            state["hold"] = len(units)
            made = 0
            if skew:
                for made in range(1, 3):
                    weight_prep()
                    before(made - 1)
            look_ahead(len(units))
            for kk, n in sorted(((kk, n) for kk in range(8) for n in range(3)), key=lambda x: (x[0] + skew * x[1], x)):
                if before and made <= kk:
                    before(kk)
                    made += 1
                group[n][0][kk]()
                if after and n == (0 if skew else 2):
                    after(kk)
            state["hold"] = UNITS_TOTAL
            look_ahead(len(units) + ahead - LOOK)
            return [(b, done[0]) for b, (_, done) in zip(banks, group)]

        def opening(name, produce=None, tiles=range(4), skew=0):
            outs = abreast(name, tiles[:3], AH, AL, a_ready, skew, produce, add_to_sums if produce else None, 0)
            b = gemm_bank()
            parts, done = gemm_parts(name, tiles[3], AH, AL, a_ready, b, by_pass=True)
            u = len(units)
            state["hold"] = u - LOOK
            for kk, part in enumerate(parts):
                part()
                if kk == 0:
                    rms_begin()
                if kk == 9:
                    rms_end()
                    look_ahead(u)
            state["hold"] = UNITS_TOTAL
            return outs + [(b, done[0])]

        with ExitStack() as ar:
            MH = sb("MH", [128, 8, S], F32R, ar)
            ML = sb("ML", [128, 8, S], F32R, ar)
            XP = [sb(f"XP{i}", [128, S + 3], stack=ar) for i in range(2)]
            LB = [[sb(f"LB{i}_{j}", [128, S], stack=ar) for j in range(5)] for i in range(2)]
            HL = sb("HL", [128, 4, S], stack=ar)
            QG = sb("QG", [128, 2, S], stack=ar)
            KG = sb("KG", [128, 2, S], stack=ar)
            BC = sb("BC", [128, 2, S], stack=ar)
            EG = sb("EG", [128, 2, S], stack=ar)
            KT = sb("KT", [128, 4, 256], stack=ar)
            VG = sb("VG", [128, 4, 512], stack=ar)
            SG = sb("SG", [128, 2, 8, 128], stack=ar)
            bd = sb("bd", [128, 8, 128], stack=ar)
            wal = sb("wal", [16, 256], stack=ar)
            DG = sb("DG", [128, 2, 8], stack=ar)
            OG = [t[:, f, :] for t in (BC, EG) for f in range(2)]
            s_bd = sem("s_bd")
            m_ready = [None] * 8

            z = PO(lambda e: e.memset(bd[:, :, :], 0.0))
            for i, name in enumerate(("lru_wa", "lru_wi")):
                for half in range(2):
                    rows = slice(64 * half, 64 * half + 64)
                    PO(lambda e, i=i, name=name, rows=rows, half=half: e.dma_start(
                        bd[rows, 4 * i:4 * i + 4, rows], D[name].rearrange("(f a) i j -> a i f j", a=2)[half])
                       .then_inc(s_bd, 16), z, inc=False)
            PO(lambda e: e.dma_start(wal[:, :], D["w_alpha"]).then_inc(s_bd, 16), inc=False)
            bd_ready = (s_bd, 80)
            for i in range(2):
                xp_zero = DV(lambda e, i=i: e.memset(XP[i][:, 0:3], 0.0))

            first = opening("w_in_t", lambda f: split_and_square(f, "norm1", [(s_x[f], 16)], square_to_sums),
                            (0, 1, 16, 10), skew=2)
            t_rs = st["rs"]

            lru = {}
            lset_free = [[xp_zero], [xp_zero]]

            def lru_evac(f, b, tok):
                i = f % 2
                t = DV(lambda e: e.tensor_tensor(XP[i][:, 3:S + 3], BANK[b][:, :], RS[:, :], ALU.mult), tok, t_rs,
                       *lset_free[i])
                bank_free[b] = [t]
                lru[f] = t

            def lru_conv(f):
                i = f % 2
                y = LB[i][0]
                w = V("conv_w", 4 * f, 4)
                t = DV(lambda e: e.tensor_scalar(y[:, :], XP[i][:, 0:S], w[:, 0:1], V("conv_b", f), ALU.mult,
                                                 ALU.add), lru[f], const_ready)
                for j in range(1, 4):
                    t = DV(lambda e, j=j: e.scalar_tensor_tensor(y[:, :], XP[i][:, j:j + S], w[:, j:j + 1], y[:, :],
                                                                 ALU.mult, ALU.add), t)
                lru[f] = t

            def lru_gates(f):
                i = f % 2
                y, r, g, a, tt = LB[i]
                ga = PE(lambda e: e.matmul(BANK[6][:, :], bd[:, f, :], y[:, :], start=True, stop=True), lru[f],
                        bank_free[6], bd_ready)
                gi = PE(lambda e: e.matmul(BANK[7][:, :], bd[:, 4 + f, :], y[:, :], start=True, stop=True),
                        bank_free[7])
                tr = AC(lambda e: e.activation(r[:, :], BANK[6][:, :], ACT.Sigmoid, bias=V("lru_ba", f)), ga,
                        *lset_free[i])
                ti = AC(lambda e: e.activation(g[:, :], BANK[7][:, :], ACT.Sigmoid, bias=V("lru_bi", f)), gi)
                bank_free[6], bank_free[7] = [tr], [ti]
                lru[f] = (tr, ti)

            def lru_decay(f):
                i = f % 2
                y, r, g, a, tt = LB[i]
                tr, ti = lru[f]
                ta = AC(lambda e: e.activation(a[:, :], r[:, :], ACT.Exp, scale=cneg[:, f:f + 1]), tr, t_c)
                th = AC(lambda e: e.activation(tt[:, :], r[:, :], ACT.Tanh, scale=cpos[:, f:f + 1]))
                d1 = DV(lambda e: e.tensor_tensor(g[:, :], g[:, :], y[:, :], ALU.mult), ti)
                d2 = DV(lambda e: e.tensor_tensor(r[:, :], a[:, :], a[:, :], ALU.mult), ta, th)
                d3 = DV(lambda e: e.scalar_tensor_tensor(r[:, :], r[:, :], 1.0, tt[:, :], ALU.add, ALU.mult), d2)
                lru[f] = (d1, d3)

            def lru_scan(f):
                i = f % 2
                y, r, g, a, tt = LB[i]
                d1, d3 = lru[f]
                t = AC(lambda e: e.activation(tt[:, :], r[:, :], ACT.Sqrt), d3)
                t = DV(lambda e: e.tensor_tensor(g[:, :], g[:, :], tt[:, :], ALU.mult), t, d1)
                t = DV(lambda e: e.tensor_tensor_scan(HL[:, f, :], a[:, :], g[:, :], 0.0, ALU.mult, ALU.add), t)
                lset_free[i] = [t]
                lru[f] = t

            tfree = [[] for _ in range(4)]

            xp_free = [[], []]

            def lru_out_evac(f, b, tok):
                i = f % 2
                t = DV(lambda e: e.tensor_tensor(XP[i][:, 0:S], BANK[b][:, :], RS[:, :], ALU.mult), tok, t_rs,
                       *xp_free[i])
                bank_free[b] = [t]
                st["rs_used"].append(t)
                tg = AC(lambda e: e.activation(XP[i][:, 0:S], XP[i][:, 0:S], ACT.Gelu_apprx_tanh), t)

                def rest():
                    t = DV(lambda e: e.tensor_tensor(XP[i][:, 0:S], XP[i][:, 0:S], HL[:, f, :], ALU.mult), tg, lru[f])
                    h = AC(lambda e: e.activation(MH[:, 4 + f, :], XP[i][:, 0:S], ACT.Copy), t)
                    low = DV(lambda e: e.tensor_tensor(ML[:, 4 + f, :], XP[i][:, 0:S], MH[:, 4 + f, :], ALU.subtract),
                             h)
                    xp_free[i] = [low]
                    m_ready[4 + f] = [h, low]
                return rest

            qk = {}
            ZT = T[0]
            msk = T[3]
            tm = DV(lambda e: e.memset(msk[:, :], 1.0))
            tm = DV(lambda e: e.memset(msk[:, 0:S:64], 0.0), tm)

            def qk_evac(f, b, tok):
                dst = (QG if f < 2 else KG)[:, f % 2, :]
                qk[f] = DV(lambda e: e.scalar_tensor_tensor(dst, BANK[b][:, :], 0.125 if f < 2 else 1.0, RS[:, :],
                                                            ALU.mult, ALU.mult), tok, t_rs)
                bank_free[b] = [qk[f]]

            def z_evac(b, tok):
                qk["z"] = DV(lambda e: e.tensor_tensor(ZT[0:16, :], BANK[b][0:16, :], RS[0:16, :], ALU.mult), tok,
                             t_rs)
                bank_free[b] = [qk["z"]]

            def gla_decay_1():
                for f in range(2):
                    zf = PE(lambda e, f=f: e.matmul(BANK[6 + f][:, :], wal[:, f * 128:(f + 1) * 128], ZT[0:16, :],
                                                    start=True, stop=True), qk["z"], bd_ready, bank_free[6 + f])
                    za = AC(lambda e, f=f: e.activation(BC[:, f, :], BANK[6 + f][:, :], ACT.Identity,
                                                        bias=V("b_alpha", f)), zf)
                    bank_free[6 + f] = [za]
                    ab_ = AC(lambda e, f=f: e.activation(EG[:, f, :], BC[:, f, :], ACT.Abs), za)
                    ex = AC(lambda e, f=f: e.activation(EG[:, f, :], EG[:, f, :], ACT.Exp, scale=-1.0), ab_)
                    qk["l", f] = AC(lambda e, f=f: e.activation(EG[:, f, :], EG[:, f, :], ACT.Ln, bias=1.0), ex)
                tfree[0] = [zf]

            def gla_decay_2():
                for f in range(2):
                    la = DV(lambda e, f=f: e.scalar_tensor_tensor(EG[:, f, :], BC[:, f, :], 0.0, EG[:, f, :],
                                                                  ALU.min, ALU.subtract), qk["l", f])
                    bc = DV(lambda e, f=f: e.tensor_tensor_scan(BC[:, f, :], msk[:, :], EG[:, f, :], 0.0, ALU.mult,
                                                                ALU.add), la, tm)
                    bcv = BC[:, f, :].rearrange("p (c t) -> p c t", t=64)
                    egv = EG[:, f, :].rearrange("p (c t) -> p c t", t=64)
                    df = DV(lambda e, bcv=bcv, egv=egv: e.tensor_tensor(
                        egv, bcv[:, :, 63:64].broadcast_to([128, 8, 64]), bcv, ALU.subtract), bc)
                    qk["d", f] = AC(lambda e, f=f, bcv=bcv: e.activation(DG[:, f, :], bcv[:, :, 63], ACT.Exp,
                                                                        scale=1.0 / 16), bc)
                    ex = AC(lambda e, f=f: e.activation(EG[:, f, :], EG[:, f, :], ACT.Exp, scale=1.0 / 16), df)
                    qk["k", f] = DV(lambda e, f=f: e.tensor_tensor(KG[:, f, :], KG[:, f, :], EG[:, f, :], ALU.mult),
                                    ex, qk[2 + f])
                tfree[3] = [bc]

            def gla_turn():
                for f in range(2):
                    for tt in range(4):
                        tp = PE(lambda e, f=f, tt=tt: e.transpose(BANK[6 + f][:, tt * 128:(tt + 1) * 128],
                                                                  KG[:, f, tt * 128:(tt + 1) * 128], ident[:, :]),
                                qk["k", f], bank_free[6 + f], const_ready, inc=(tt == 3))
                    qk["t", f] = AC(lambda e, f=f: e.activation(
                        KT[:, :, f * 128:(f + 1) * 128], BANK[6 + f][:, :].rearrange("p (a b) -> p a b", b=128),
                        ACT.Copy), tp)
                    bank_free[6 + f] = [qk["t", f]]

            def tile(n):
                return gemm_tile("w_in_t", n, AH, AL, a_ready)

            lru_evac(0, *first[0])
            lru_evac(1, *first[1])
            z_evac(*first[2])
            qk_evac(2, *first[3])
            lru_conv(0)
            lam = V("lru_lambda", 0, 4)
            ab, ee, sden, ss, s2, pol, mx = (small[:, 4 * i:4 * i + 4] for i in range(7))
            cneg, cpos = small[:, 28:32], small[:, 32:36]
            t = AC(lambda e: e.activation(ab, lam, ACT.Abs), const_ready)
            t = AC(lambda e: e.activation(ee, ab, ACT.Exp, scale=-1.0), t)
            t = DV(lambda e: e.tensor_scalar(sden, ee, 2.0, None, ALU.add), t)
            t = DV(lambda e: e.reciprocal(sden, sden), t)
            t = DV(lambda e: e.tensor_tensor(ss, ee, sden, ALU.mult), t)
            t = DV(lambda e: e.tensor_tensor(s2, ss, ss, ALU.mult), t)
            t = DV(lambda e: e.tensor_scalar(pol, s2, 2.0 / 19, 2.0 / 17, ALU.mult, ALU.add), t)
            for d in (15, 13, 11, 9, 7, 5, 3, 1):
                t = DV(lambda e: e.tensor_tensor(pol, pol, s2, ALU.mult), t)
                t = DV(lambda e, d=d: e.tensor_scalar(pol, pol, 2.0 / d, None, ALU.add), t)
            t = DV(lambda e: e.tensor_tensor(pol, pol, ss, ALU.mult), t)
            t = DV(lambda e: e.tensor_scalar(mx, lam, -1.0, 0.0, ALU.mult, ALU.max), t, const_ready)
            t = DV(lambda e: e.tensor_tensor(mx, mx, pol, ALU.add), t)
            t = DV(lambda e: e.tensor_scalar(cpos, mx, 8.0, None, ALU.mult), t)
            t_c = DV(lambda e: e.tensor_scalar(cneg, mx, -8.0, None, ALU.mult), t)
            b, tok = tile(11)
            lru_gates(0)
            qk_evac(3, b, tok)
            lru_conv(1)
            b, tok = tile(8)
            gla_decay_1()
            lru_decay(0)
            qk_evac(0, b, tok)
            b, tok = tile(9)
            lru_gates(1)
            lru_scan(0)
            gla_decay_2()
            qk_evac(1, b, tok)
            b, tok = tile(2)
            lru_decay(1)
            lru_evac(2, b, tok)
            lru_scan(1)
            lru_conv(2)
            b, tok = tile(3)
            gla_turn()
            lru_evac(3, b, tok)
            lru_conv(3)
            banks, toks = gemm_tokens("w_in_v", 0, AH, AL, a_ready)
            lru_gates(2)
            tv = []
            for tt in range(4):
                tv.append(AC(lambda e, tt=tt, b=banks[tt]: e.activation(VG[:, tt, :], BANK[b][:, :], ACT.Copy,
                                                                        scale=rstok[:, tt:tt + 1]), toks[tt], t_rs))
                bank_free[banks[tt]] = [tv[tt]]
            st["rs_used"].append(tv[3])
            lru_decay(2)

            def gla_update():
                for pr in range(2):
                    for c in range(8):
                        tt, row = c // 2, 64 * (c % 2)
                        b = 4 + 2 * pr + c % 2
                        for hh in range(2):
                            h = 2 * pr + hh
                            tok = PE(lambda e, c=c, tt=tt, row=row, b=b, hh=hh, h=h: e.matmul(
                                BANK[b][64 * hh:64 * hh + 64, (c // 2) * 128:(c // 2) * 128 + 128],
                                KT[row:row + 64, tt, h * 64:h * 64 + 64], VG[row:row + 64, tt, h * 128:h * 128 + 128],
                                start=True, stop=True), qk["t", pr], tv[tt], bank_free[b], inc=(c >= 6 and hh == 1))
                        if c >= 6:
                            qk["u", pr, c % 2] = tok
                prev = [None, None]
                for c in range(8):
                    for pr in range(2):
                        b = 4 + 2 * pr + c % 2
                        src = BANK[b][:, (c // 2) * 128:(c // 2) * 128 + 128]
                        if c == 0:
                            prev[pr] = DV(lambda e, src=src, pr=pr: e.tensor_copy(SG[:, pr, 0, :], src),
                                          qk["u", pr, 0])
                        else:
                            prev[pr] = DV(lambda e, src=src, c=c, pr=pr: e.scalar_tensor_tensor(
                                SG[:, pr, c, :], SG[:, pr, c - 1, :], DG[:, pr, c:c + 1], src, ALU.mult, ALU.add),
                                prev[pr], qk["u", pr, c % 2], qk["d", pr])
                        bank_free[b] = [prev[pr]]
                        qk["s", pr] = prev[pr]

            def gla_out(pr):
                for hh in range(2):
                    h = 2 * pr + hh
                    for c in range(8):
                        tok = PE(lambda e, c=c, hh=hh: e.matmul(
                            BANK[6 + hh][:, c * 64:c * 64 + 64], SG[64 * hh:64 * hh + 64, pr, c, :],
                            QG[64 * hh:64 * hh + 64, pr, c * 64:c * 64 + 64], start=True, stop=True),
                            qk["s", pr], bank_free[6 + hh], qk[pr], inc=(c == 7))
                    i = h % 2
                    to = AC(lambda e, h=h, hh=hh: e.activation(OG[h], BANK[6 + hh][:, :], ACT.Copy,
                                                               scale=V("gla_norm")), tok, qk["d", 1], qk["k", 1])
                    ts = AC(lambda e, i=i, hh=hh: e.activation(SQ[i][:, :], BANK[6 + hh][:, :], ACT.Square), to,
                            st["sq"][i])
                    bank_free[6 + hh] = [ts]
                    qk["o", h] = to
                    qk["sq", h] = ts

            def gla_sums(pr):
                for h in (2 * pr, 2 * pr + 1):
                    i = h % 2
                    for tt in range(4):
                        tok = PE(lambda e, h=h, tt=tt, i=i: e.matmul(
                            BANK[4][:, 4 * h + tt:4 * h + tt + 1], SQ[i][:, tt * 128:(tt + 1) * 128], ones[:, :],
                            start=True, stop=True), qk["sq", h], bank_free[4], inc=(tt == 3))
                    st["sq"][i] = tok
                    qk["n", h] = tok

            def gla_scale():
                qk["r"] = rms_rows(rso, BANK[4], 16, 128, qk["n", 3])

            def gla_norm_out(h):
                bb = 5 + h % 2
                for tt in range(4):
                    tok = PE(lambda e, tt=tt: e.matmul(
                        BANK[bb][:, tt * 128:(tt + 1) * 128],
                        rso[:, 4 * h + tt:4 * h + tt + 1].broadcast_to([128, 128]), ident[:, :], start=True,
                        stop=True), qk["r"], bank_free[bb], inc=(tt == 3))
                qk["y", h] = DV(lambda e: e.tensor_tensor(OG[h], OG[h], BANK[bb][:, :], ALU.mult), tok,
                                qk["o", h])
                bank_free[bb] = [qk["y", h]]

            def silu_gate(h, b, tok):
                i = h % 4
                t = DV(lambda e: e.tensor_tensor(T[i][:, :], BANK[b][:, :], RS[:, :], ALU.mult), tok, *tfree[i])
                bank_free[b] = [t]
                ts = AC(lambda e: e.activation(T[i][:, :], T[i][:, :], ACT.Silu), t)
                st["rs_used"].append(t)

                def rest():
                    t = DV(lambda e: e.tensor_tensor(T[i][:, :], T[i][:, :], OG[h], ALU.mult), ts, qk["y", h])
                    hi = AC(lambda e: e.activation(MH[:, h, :], T[i][:, :], ACT.Copy), t)

                    def part():
                        low = DV(lambda e: e.tensor_tensor(ML[:, h, :], T[i][:, :], MH[:, h, :], ALU.subtract), hi)
                        tfree[i] = [low]
                        m_ready[h] = [hi, low]
                    return part
                return rest

            def finish_heads(heads):
                for h in heads:
                    gla_norm_out(h)
                lows = [gated[h]() for h in heads]
                for low in lows:
                    low()

            background += [lambda: (lru_scan(2), lru_gates(3)), lambda: (gla_update(), lru_decay(3)),
                           lambda: (lru_scan(3), gla_out(0)), lambda: (gla_sums(0), gla_out(1)),
                           lambda: (gla_sums(1), gla_scale()), lambda: None, lambda: finish_heads((0, 1)),
                           lambda: finish_heads((2, 3))]
            gated = []
            for h in range(4):
                b, tok = tile(12 + h)
                tick()
                gated.append(silu_gate(h, b, tok))
            late = []
            for f in range(4):
                b, tok = tile(4 + f)
                if f == 3:
                    look_ahead(len(units))
                tick()
                for fn in late:
                    fn()
                late = [lru_out_evac(f, b, tok)]
            st["a_free"] = [PE.now()]
            for fn in late:
                fn()

            def residual_mix1(f, b, tok):
                t = DV(lambda e: e.tensor_tensor(XT[:, f, :], XT[:, f, :], BANK[b][:, :], ALU.add), tok, *xt_read[f])
                bank_free[b] = [t]
                split_and_square(f, "norm2", [t])

            outs = abreast("w_out", range(3), MH, ML, m_ready)
            for f in range(8):
                b, tok = outs[f] if f < 3 else gemm_tile("w_out", f, MH, ML, m_ready, f == 3)
                residual_mix1(f, b, tok)
        st["rs_used"] = []

        def ffn_layer(names, finish, tag, produce=None):
            with ExitStack() as ar:
                HH = sb("HH" + tag, [128, 22, S], F32R, ar)
                HLO = sb("HLO" + tag, [128, 22, S], F32R, ar)
                h_ready = [None] * 22
                late = []

                def pair(j, bg, tg, bu, tu):
                    a, c = T[2 * (j % 2)], T[2 * (j % 2) + 1]
                    fa, fc = tfree[2 * (j % 2)], tfree[2 * (j % 2) + 1]
                    t1 = DV(lambda e: e.tensor_tensor(a[:, :], BANK[bg][:, :], RS[:, :], ALU.mult), tg, st["rs"], *fa)
                    bank_free[bg] = [t1]
                    t2 = AC(lambda e: e.activation(a[:, :], a[:, :], ACT.Silu), t1)
                    t3 = DV(lambda e: e.tensor_tensor(c[:, :], BANK[bu][:, :], RS[:, :], ALU.mult), tu, *fc)
                    bank_free[bu] = [t3]
                    st["rs_used"] = [t3]

                    def rest():
                        t4 = DV(lambda e: e.tensor_tensor(a[:, :], a[:, :], c[:, :], ALU.mult), t2, t3)
                        hi = AC(lambda e: e.activation(HH[:, j, :], a[:, :], ACT.Copy), t4, *fence_in)
                        low = DV(lambda e: e.tensor_tensor(HLO[:, j, :], a[:, :], HH[:, j, :], ALU.subtract), hi,
                                 *fence_in)
                        tfree[2 * (j % 2)] = [low]
                        tfree[2 * (j % 2) + 1] = [t4]
                        h_ready[j] = [hi, low]
                    return rest

                first = opening(names[0], produce)
                fence_in = st["fence"] = fence()
                late = [pair(0, *first[0], *first[1])]
                for j in range(1, 22):
                    bg, tg = first[2] if j == 1 else gemm_tile(names[0], 2 * j, AH, AL, a_ready)
                    for fn in late:
                        fn()
                    bu, tu = first[3] if j == 1 else gemm_tile(names[0], 2 * j + 1, AH, AL, a_ready)
                    late = [pair(j, bg, tg, bu, tu)]
                st["a_free"] = [PE.now()]
                for fn in late:
                    fn()
                for f in range(8):
                    b, tok = gemm_tile(names[1], f, HH, HLO, h_ready)
                    finish(f, b, tok)

        def finish_block1(f, b, tok):
            t = DV(lambda e: e.tensor_tensor(XT[:, f, :], XT[:, f, :], BANK[b][:, :], ALU.add), tok, *xt_read[f])
            bank_free[b] = [t]
            final["x", f] = [t, square_in(f, XT[:, f, :], [t])]

        final = {}
        ffn_layer(("ffn1_in", "ffn1_out"), finish_block1, "1")
        look_ahead(len(units))
        rs = rms_scale()

        def finish_norm(f):
            t = DV(lambda e: e.scalar_tensor_tensor(XT[:, f, :], XT[:, f, :], V("final_norm", f), BANK[5][:, :],
                                                    ALU.mult, ALU.mult), final["x", f], rs)
            bank_free[5] = [t]
            return t

        enter_block2 = pipelined(lambda f: None, finish_norm, "mix_pre0")

        def post_norm(M, m_tok, post, pre):
            look_ahead(len(units))
            rs = rms_scale()

            def scale(f):
                m_tok[f] = DV(lambda e: e.scalar_tensor_tensor(M[:, f, :], M[:, f, :], V(post, f), BANK[5][:, :],
                                                               ALU.mult, ALU.mult), m_tok[f], rs)
                bank_free[5] = [m_tok[f]]

            def update(f):
                return DV(lambda e: e.tensor_tensor(XT[:, f, :], XT[:, f, :], M[:, f, :], ALU.add), m_tok[f],
                          *xt_read[f])

            if pre:
                return pipelined(scale, update, pre)
            for f in range(8):
                scale(f)
                if f:
                    final["h", f - 1] = update(f - 1)
            final["h", 7] = update(7)

        def branch_out(M, m_tok, b, tok, f, after=()):
            square_in(f, BANK[b][:, :], [tok])
            t = AC(lambda e: e.activation(M[:, f, :], BANK[b][:, :], ACT.Copy), tok, *after)
            bank_free[b] = [t]
            m_tok[f] = t

        fence_in = fence()
        with ExitStack() as ar:
            RH = sb("RH", [128, 16, S], F32R, ar)
            RL = sb("RL", [128, 16, S], F32R, ar)
            CS = sb("CS", [128, 2, S], stack=ar)
            DEC = sb("DEC", [128, S], stack=ar)
            s_cs, s_dec = sem("s_cs"), sem("s_dec")
            PO(lambda e: e.dma_start(CS[:, :, :], D["cossin"].rearrange("p (a t) -> p a t", a=2)).then_inc(s_cs, 16),
               *fence_in, inc=False)
            r_ready = [None] * 16
            with ExitStack() as ar2:
                OH = sb("OH", [33, 656], stack=ar2)
                BV = sb("BV", [16, 640], stack=ar2)
                s_bias, s_scr = sem("s_bias"), sem("s_scr")
                PO(lambda e: e.dma_start(OH[:, :], D["onehot"]).then_inc(s_bias, 16), *fence_in, inc=False)

                def distance_bias():
                    for n in range(2):
                        cols = slice(320 * n, 320 * n + 320)
                        t = PE(lambda e, cols=cols, n=n: e.matmul(BANK[6 + n][0:16, 0:320], OH[:, 640:656],
                                                                  OH[:, cols], start=True, stop=True),
                               (s_bias, 16), bank_free[6 + n])
                        t = DV(lambda e, cols=cols, n=n: e.tensor_copy(BV[:, cols], BANK[6 + n][0:16, 0:320]), t,
                               *fence_in)
                        bank_free[6 + n] = [t]
                    PO(lambda e: e.dma_start(D["scratch"], BV[:, :]).then_inc(s_scr, 16), t, inc=False)

                QR = sb("QR", [128, 2, S], stack=ar2)
                KR = sb("KR", [128, 2, S], stack=ar2)
                VR = sb("VR", [128, 4, 512], stack=ar2)
                OR = sb("OR", [128, 4, S], stack=ar2)
                ST = [sb(f"ST{j}", [128, S - 128 * j], stack=ar2) for j in range(4)]
                q_read, v_read, st_read, dec_read, or_read = [], [], [None] * 4, [], []
                ret = {}

                def rotate(h, dst, b0, t0, b1, t1):
                    rd = list(q_read)
                    d = [DV(lambda e: e.tensor_tensor(T[0][:, :], BANK[b0][:, :], CS[:, 0, :], ALU.mult), t0,
                            ret["cs"], *tfree[0]),
                         DV(lambda e: e.tensor_tensor(T[1][:, :], BANK[b0][:, :], CS[:, 1, :], ALU.mult), *tfree[1])]
                    bank_free[b0] = [d[1]]
                    d += [DV(lambda e: e.tensor_tensor(T[2][:, :], BANK[b1][:, :], CS[:, 1, :], ALU.mult), t1,
                             *tfree[2]),
                          DV(lambda e: e.tensor_tensor(T[3][:, :], BANK[b1][:, :], CS[:, 0, :], ALU.mult),
                             *tfree[3])]
                    bank_free[b1] = [d[3]]
                    e0 = DV(lambda e: e.tensor_tensor(dst[:, 0, :], T[0][:, :], T[2][:, :], ALU.subtract), d[2], *rd,
                            *fence_in)
                    e1 = DV(lambda e: e.tensor_tensor(dst[:, 1, :], T[1][:, :], T[3][:, :], ALU.add), d[3], *rd)
                    tfree[0], tfree[2] = [e0], [e0]
                    tfree[1], tfree[3] = [e1], [e1]
                    return e1

                def heads_qkv(h):
                    if h == 0:
                        first = opening("ret_t", enter_block2)
                        c = DV(lambda e: e.tensor_tensor(CS[:, 0, :], CS[:, 0, :], RS[:, :], ALU.mult), st["rs"],
                               (s_cs, 16))
                        ret["cs"] = DV(lambda e: e.tensor_tensor(CS[:, 1, :], CS[:, 1, :], RS[:, :], ALU.mult), c)
                        ret["q"] = rotate(h, QR, *first[0], *first[1])
                        ret["k"] = rotate(h, KR, *first[2], *first[3])
                    else:
                        b0, t0 = gemm_tile("ret_t", 8 * h, AH, AL, a_ready)
                        b1, t1 = gemm_tile("ret_t", 8 * h + 1, AH, AL, a_ready)
                        ret["q"] = rotate(h, QR, b0, t0, b1, t1)
                        b0, t0 = gemm_tile("ret_t", 8 * h + 2, AH, AL, a_ready)
                        b1, t1 = gemm_tile("ret_t", 8 * h + 3, AH, AL, a_ready)
                        ret["k"] = rotate(h, KR, b0, t0, b1, t1)
                    banks, toks = gemm_tokens("ret_v", h, AH, AL, a_ready)
                    ret["v"] = []
                    for tt in range(4):
                        ret["v"].append(AC(lambda e, tt=tt, b=banks[tt]: e.activation(
                            VR[:, tt, :], BANK[b][:, :], ACT.Copy, scale=rstok[:, tt:tt + 1]), toks[tt], st["rs"],
                            *v_read, *fence_in))
                        bank_free[banks[tt]] = [ret["v"][tt]]
                    PO(lambda e: e.dma_start(DEC[:, :], D["decay"][h]).then_inc(s_dec, 16), *dec_read, *fence_in,
                       inc=False)
                    ret["dec"] = (s_dec, 16 * (h + 1))

                def scores(h):
                    for j in range(4):
                        n = S - 128 * j
                        b = gemm_bank()
                        for d in range(2):
                            tok = PE(lambda e, d=d, j=j, n=n, b=b: e.matmul(
                                BANK[b][:, 0:n], KR[:, d, j * 128:(j + 1) * 128], QR[:, d, j * 128:S],
                                start=(d == 0), stop=(d == 1)), ret["q"], ret["k"], bank_free[b], inc=(d == 1))
                        ret["s", j] = DV(lambda e, j=j, n=n, b=b: e.tensor_tensor(
                            ST[j][:, :], BANK[b][:, 0:n], DEC[:, 0:n], ALU.mult), tok, ret["dec"], st_read[j],
                            *fence_in)
                        bank_free[b] = [ret["s", j]]
                    q_read[:] = [tok]
                    dec_read[:] = [ret["s", 3]]

                def values(h):
                    for j in range(4):
                        n = S - 128 * j
                        for et in range(4):
                            tok = PE(lambda e, et=et, j=j, n=n: e.matmul(
                                BANK[4 + et][:, j * 128:S], VR[:, j, et * 128:(et + 1) * 128], ST[j][:, :],
                                start=(j == 0), stop=(j == 3)), ret["s", j], ret["v"][j],
                                bank_free[4 + et] if j == 0 else None, inc=(j == 3 or et == 3))
                            if j == 3:
                                ret["o", et] = tok
                        st_read[j] = tok
                    v_read[:] = [tok]
                    for et in range(4):
                        ret["oc", et] = AC(lambda e, et=et: e.activation(OR[:, et, :], BANK[4 + et][:, :], ACT.Copy),
                                           ret["o", et], *or_read, *fence_in)
                        bank_free[4 + et] = [ret["oc", et]]

                def head_norm(h):
                    for et in range(4):
                        square_in(et, OR[:, et, :], [ret["oc", et]], last=3)
                    ret["rso"] = rms_rows(rso, BANK[4], 4, 512, row_sums(), ret.get("rso_read"))

                def head_norm_spread(h):
                    for tt in range(4):
                        tok = PE(lambda e, tt=tt: e.matmul(
                            BANK[5][:, tt * 128:(tt + 1) * 128], rso[:, tt:tt + 1].broadcast_to([128, 128]),
                            ident[:, :], start=True, stop=True), ret["rso"], bank_free[5], inc=(tt == 3))
                    ret["rso_read"] = tok
                    for et in range(4):
                        ret["on", et] = DV(lambda e, et=et: e.tensor_tensor(OR[:, et, :], OR[:, et, :],
                                                                           BANK[5][:, :], ALU.mult), tok,
                                           st["acc"], st["tail"][1], ret["oc", et])
                    bank_free[5] = [ret["on", 3]]

                def gate_evac(h, et, b, tok):
                    i = et % 4
                    t = DV(lambda e: e.tensor_tensor(T[i][:, :], BANK[b][:, :], RS[:, :], ALU.mult), tok, *tfree[i])
                    bank_free[b] = [t]
                    st["rs_used"] = [t, ret["v"][3]]
                    ts = AC(lambda e: e.activation(T[i][:, :], T[i][:, :], ACT.Silu), t)

                    def rest():
                        k = 4 * h + et
                        t = DV(lambda e: e.tensor_tensor(T[i][:, :], T[i][:, :], OR[:, et, :], ALU.mult), ts,
                               ret["on", et])
                        hi = AC(lambda e: e.activation(RH[:, k, :], T[i][:, :], ACT.Copy), t, *fence_in)
                        low = DV(lambda e: e.tensor_tensor(RL[:, k, :], T[i][:, :], RH[:, k, :], ALU.subtract), hi,
                                 *fence_in)
                        tfree[i] = [low]
                        r_ready[k] = [hi, low]
                        or_read[:] = [t]
                    return rest

                for h in range(4):
                    heads_qkv(h)
                    if h == 0:
                        distance_bias()
                    scores(h)
                    background += [lambda h=h: values(h), lambda h=h: head_norm(h), lambda h=h: head_norm_spread(h)]
                    late = []
                    for et in range(4):
                        b, tok = gemm_tile("ret_t", 8 * h + 4 + et, AH, AL, a_ready)
                        tick()
                        late.append(gate_evac(h, et, b, tok))
                    for fn in late:
                        fn()
                st["a_free"] = [PE.now()]
            fence_m = fence()
            MR = sb("MR", [128, 8, S], stack=ar)
            m_tok = [None] * 8
            for f in range(8):
                b, tok = gemm_tile("ret_out", f, RH, RL, r_ready)
                branch_out(MR, m_tok, b, tok, f, fence_m)
            update = post_norm(MR, m_tok, "mix_post0", "ffn_pre0")

        def ffn_block2(names, update, post, pre, tag):
            with ExitStack() as am:
                MF = sb("MF" + tag, [128, 8, S], stack=am)
                m_tok = [None] * 8
                ffn_layer(names, lambda f, b, tok: branch_out(MF, m_tok, b, tok, f, st["fence"]), tag, update)
                return post_norm(MF, m_tok, post, pre)

        update = ffn_block2(("ffn2_in", "ffn2_out"), update, "ffn_post0", "kv_norm", "2")

        first = opening("kv_t", update)
        fence_in = fence()
        with ExitStack() as ar:
            TT = [sb(f"TT{i}", [128, 4, S], stack=ar) for i in range(2)]
            KHH = sb("KHH", [128, 8, S], F32R, ar)
            KLL = sb("KLL", [128, 8, S], F32R, ar)
            VS = sb("VS", [128, 4, 512], stack=ar)
            GT = sb("GT", [128, 4, 48], stack=ar)
            KCH = sb("KCH", [128, 4, 32], F32R, ar)
            KCL = sb("KCL", [128, 4, 32], F32R, ar)
            VC = sb("VC", [32, 4, 64], stack=ar)
            s_w1, s_w2 = sem("s_w1"), sem("s_w2")
            s_tt = [sem(f"s_tt{i}") for i in range(2)]
            at = {}

            def load_bias(g, *free):
                PO(lambda e: e.dma_start(TT[g % 2][:, :, :],
                                         bass.AP(D["scratch"].tensor, 4 * g * 640, [[1, 128], [640, 4], [1, 512]]))
                   .then_inc(s_tt[g % 2], 16), (s_scr, 16), *free, inc=False)

            def stack_parts(src, half, hi_own, hi_other, lo_own, lo_other, ready, *after):
                own = slice(64 * half, 64 * half + 64)
                other = slice(64 - 64 * half, 128 - 64 * half)
                h = AC(lambda e: e.activation(hi_own[own], src[own], ACT.Copy), ready, *after)
                t = [h]
                if hi_other is not None:
                    t.append(AC(lambda e: e.activation(hi_other[other], src[own], ACT.Copy)))
                for dst, rows in ((lo_own, own), (lo_other, other)):
                    if dst is not None:
                        t.append(DV(lambda e, dst=dst, rows=rows: e.tensor_tensor(dst[rows], src[own], hi_own[own],
                                                                                 ALU.subtract), h, *after))
                return t

            with ExitStack() as ac:
                CK = sb("CK", [128, 4, S], stack=ac)
                X2 = sb("X2", [128, 16, 124], stack=ac)
                W1 = sb("W1", [128, 16, 256], stack=ac)
                HC = sb("HC", [128, 2, 124], stack=ac)
                W2 = sb("W2", [128, 2, 2, 128], stack=ac)
                PO(lambda e: e.dma_start(W1[:, :, :], D["cmp_w1"][0]).then_inc(s_w1, 16), *fence_in, inc=False)
                PO(lambda e: e.dma_start(W2[:, :, :, :], D["cmp_w2"]).then_inc(s_w2, 16), inc=False)
                load_bias(0)
                load_bias(1)
                kc_zero = [DV(lambda e, k=k: e.memset(k[:, :, :].bitcast(F32), 0.0), *fence_in) for k in (KCH, KCL)]

                def kv_tile(n):
                    b, tok = first[n] if n < 4 else gemm_tile("kv_t", n, AH, AL, a_ready)
                    if n < 4:
                        t = DV(lambda e: e.tensor_tensor(CK[:, n, :], BANK[b][:, :], RS[:, :], ALU.mult), tok,
                               st["rs"], *fence_in)
                        at["kv", n] = t
                    else:
                        i = n % 4
                        t = DV(lambda e: e.tensor_tensor(T[i][:, :], BANK[b][:, :], RS[:, :], ALU.mult), tok,
                               st["rs"], *tfree[i])
                        done = []
                        for half in range(2):
                            k = 4 * (n // 2 - 2) + 2 * (n % 2) + half
                            at["k", k] = stack_parts(T[i], half, KHH[:, k, :], KHH[:, k, :], KLL[:, k, :],
                                                     KLL[:, k, :], t, *fence_in)
                            done += at["k", k]
                        tfree[i] = done
                    bank_free[b] = [t]

                def spread(i):
                    for g in range(4):
                        for par in range(2):
                            src = CK[64 * (g % 2):64 * (g % 2) + 64, 2 * i + g // 2, :]
                            win = bass.AP(src.tensor, src.offset + par, [src.ap[0], [2, 16], [16, 31]])
                            t = DV(lambda e, g=g, par=par, win=win: e.tensor_copy(
                                X2[64 * par:64 * par + 64, :, 31 * g:31 * g + 31], win), at["kv", 2 * i + g // 2],
                                at.get("hid"), *fence_in)
                    pe = V("pe_k" if i == 0 else "pe_v", 0, 16).rearrange("p (l o) -> p l o", o=1)
                    at["x2"] = DV(lambda e: e.tensor_tensor(X2[:, :, :], X2[:, :, :],
                                                            pe.broadcast_to([128, 16, 124]), ALU.add), t)

                def hidden(i):
                    for ht in range(2):
                        for lp in range(16):
                            t = PE(lambda e, ht=ht, lp=lp: e.matmul(
                                BANK[4 + ht][:, 0:124], W1[:, lp, ht * 128:ht * 128 + 128], X2[:, lp, :],
                                start=(lp == 0), stop=(lp == 15)), at["x2"], (s_w1, 16 * (i + 1)),
                                bank_free[4 + ht], inc=(lp == 15))
                        at["hc", ht] = AC(lambda e, ht=ht: e.activation(HC[:, ht, :], BANK[4 + ht][:, 0:124],
                                                                        ACT.Silu), t, at.get("hc_read"), *fence_in)
                        bank_free[4 + ht] = [at["hc", ht]]
                    at["hid"] = t
                    if i == 0:
                        PO(lambda e: e.dma_start(W1[:, :, :], D["cmp_w1"][1]).then_inc(s_w1, 16), t, inc=False)

                def compressed(i):
                    b = 6 + i
                    for g in range(4):
                        for ht in range(2):
                            hc = HC[:, ht, 31 * g:31 * g + 31]
                            w2 = W2[:, i, ht, 0:128 - 64 * i]
                            if i == 0:
                                t = PE(lambda e, g=g, ht=ht, hc=hc, w2=w2: e.matmul(
                                    BANK[b][:, 32 * g:32 * g + 31], w2, hc, start=(ht == 0), stop=(ht == 1)),
                                    at["hc", ht], (s_w2, 16), bank_free[b], inc=(g == 3 and ht == 1))
                            else:
                                t = PE(lambda e, g=g, ht=ht, hc=hc, w2=w2: e.matmul(
                                    BANK[b][0:31, 64 * g:64 * g + 64], hc, w2, start=(ht == 0), stop=(ht == 1)),
                                    at["hc", ht], (s_w2, 16), bank_free[b], inc=(g == 3 and ht == 1))
                    at["hc_read"] = t
                    if i == 0:
                        src = BANK[b][:, 0:128].rearrange("p (g n) -> p g n", g=4)[:, :, 0:31]
                        h = AC(lambda e: e.activation(KCH[:, :, 0:31], src, ACT.Copy), t, *kc_zero)
                        t = DV(lambda e: e.tensor_tensor(KCL[:, :, 0:31], src, KCH[:, :, 0:31], ALU.subtract), h)
                        at["kc"] = t
                    else:
                        t = DV(lambda e: e.tensor_copy(VC[0:31, :, :], BANK[b][0:31, 0:256].rearrange(
                            "p (g d) -> p g d", g=4)), t, *fence_in)
                        at["vc"] = t
                    bank_free[b] = [t]

                for n in range(6):
                    kv_tile(n)
                spread(0)
                kv_tile(6)
                kv_tile(7)
                banks, toks = gemm_tokens("kv_v", 0, AH, AL, a_ready)
                st["a_free"] = [PE.now()]
                at["v"] = []
                for tt in range(4):
                    at["v"].append(AC(lambda e, tt=tt, b=banks[tt]: e.activation(
                        VS[:, tt, :], BANK[b][:, :], ACT.Copy, scale=rstok[:, tt:tt + 1]), toks[tt], st["rs"],
                        *fence_in))
                    bank_free[banks[tt]] = [at["v"][tt]]
                for f in range(8):
                    a_ready[f] = split_in(f, "mix_pre1", [final["h", f]], st["a_free"])
                    xt_read[f] = [xt_read[f], a_ready[f]]
                hidden(0)
                spread(1)
                compressed(0)
                b, tok = gemm_tile("nsa_t", 8, AH, AL, a_ready)
                t = DV(lambda e, b=b: e.tensor_tensor(T[3][0:48, :], BANK[b][0:48, :], RS[0:48, :], ALU.mult), tok,
                       st["rs"], *tfree[3])
                bank_free[b] = [t]
                t_sig = AC(lambda e: e.activation(T[3][0:48, :], T[3][0:48, :], ACT.Sigmoid), t)
                hidden(1)
                compressed(1)
            fence_q = fence() + [(s_w1, 32)]
            QHL = [sb(f"QHL{i}", [128, 4, S], F32R, ar) for i in range(2)]
            OT = sb("OT", [128, 4, 1024], stack=ar)
            SS = [sb(f"SS{i}", [128, S], stack=ar) for i in range(4)] + SQ
            PT = [sb(f"PT{i}", [128, S], stack=ar) for i in range(3)] + [ACC]
            NM = sb("NM", [128, 8], stack=ar)
            SM = sb("SM", [128, 4, 4], stack=ar)
            CF = sb("CF", [128, 4, 4], stack=ar)
            q_read = {}
            info = {}

            def query_evac(n, b, tok):
                g, i = n // 2, n % 4
                t = DV(lambda e: e.scalar_tensor_tensor(T[i][:, :], BANK[b][:, :], 0.125, RS[:, :], ALU.mult,
                                                        ALU.mult), tok, st["rs"], *tfree[i])
                bank_free[b] = [t]
                st["rs_used"] = [t, at["v"][3]]
                done = []
                for half in range(2):
                    q = QHL[g % 2][:, 2 * (n % 2) + half, :]
                    done += stack_parts(T[i], half, q, None, None, q, t, *fence_q, q_read.get(g - 2))
                tfree[i] = done
                at["q", n] = done

            for n in range(2):
                b, tok = gemm_tile("nsa_t", n, AH, AL, a_ready)
                query_evac(n, b, tok)
                if n == 0:
                    for tt in range(4):
                        tok = PE(lambda e, tt=tt: e.transpose(BANK[6][:, 48 * tt:48 * tt + 48],
                                                              T[3][0:48, tt * 128:(tt + 1) * 128], ident[0:48, 0:48]),
                                 t_sig, bank_free[6], inc=(tt == 3))
                    tfree[3] = [tok]
                    at["gate"] = DV(lambda e: e.tensor_copy(GT[:, :, :], BANK[6][:, 0:192].rearrange(
                        "p (a b) -> p a b", a=4)), tok, *fence_in)
                    bank_free[6] = [at["gate"]]

            steps = [(g, i, r, br) for g in range(4) for r in range(4) for i in ORDER for br in range(3)]
            TURN, MIX = 3, 6
            first_step, last_step = (ORDER[0], 0, 0), (ORDER[-1], 3, 2)
            NSS, NPT = len(SS), len(PT)
            ss_free, pt_free = {}, {}
            between = []

            def fill(n=1):
                for _ in range(n):
                    if between:
                        between.pop(0)()


            def step_scores(s):
                g, i, r, br = steps[s]
                h = 4 * g + r
                keys = 7 + 8 * i if br == 0 else 128 * (i + 1)
                even = keys + keys % 2
                b = s % 2
                q = QHL[g % 2][:, r, i * 128:(i + 1) * 128]
                if br == 0:
                    parts = (KCH[:, g, 0:even], KCL[:, g, 0:even])
                    k_ready = [at["kc"]]
                else:
                    parts = (KHH[:, 4 * (br - 1) + g, 0:keys], KLL[:, 4 * (br - 1) + g, 0:keys])
                    k_ready = at["k", 4 * (br - 1) + g]
                for n, k in enumerate(parts):
                    t = PE(lambda e, n=n, k=k: e.matmul(BANK[b][:, 0:even], q, k, start=(n == 0), stop=(n == 1)),
                           at["q", h // 2], k_ready, bank_free[b], inc=(n == 1))
                if (i, r, br) == last_step:
                    q_read[g] = t
                row = TT[g % 2][:, r, :]
                bias = bass.AP(row.tensor, row.offset + 128 * i + (96 if br == 0 else 127),
                               [row.ap[0], [-16 if br == 0 else -1, keys]])
                m = s % 8
                t = DV(lambda e: e.tensor_tensor_reduce(SS[s % NSS][:, 0:keys], BANK[b][:, 0:keys], bias, -1.0, -GUARD,
                                                        ALU.add, ALU.min, NM[:, m:m + 1]), t,
                       (s_tt[g % 2], 16 * (g // 2 + 1)), ss_free.get(s - NSS), info.get(("e", s - 8)), *fence_q)
                bank_free[b] = [t]
                fill()
                if (i, r, br) == last_step and g < 2:
                    load_bias(g + 2, t)
                o = (s // 3) % 4
                info["e", s] = AC(lambda e: e.activation(SS[s % NSS][:, 0:keys], SS[s % NSS][:, 0:keys], ACT.Exp,
                                                         bias=NM[:, m:m + 1], scale=-1.0,
                                                         accum_out=SM[:, o, br:br + 1]), t,
                                  info.get(("cf", s // 3 - 4)), *fence_q)

            def step_turn(s):
                g, i, r, br = steps[s]
                b = TURN_BANKS[s % 3]
                k = 7 + 8 * i if br == 0 else 128
                n = 1 if br == 0 else i + 1
                for j in range(n):
                    t = PE(lambda e, j=j: e.transpose(BANK[b][0:k, j * 128:(j + 1) * 128],
                                                      SS[s % NSS][:, j * 128:j * 128 + k], ident[:, :]),
                           info["e", s], bank_free[b], inc=(j == n - 1))
                ss_free[s] = t
                to, frm = PT[s % NPT][0:k, 0:128 * n], BANK[b][0:k, 0:128 * n]
                t = AC(lambda e: e.activation(to, frm, ACT.Copy), t, pt_free.get(s - NPT), *fence_q)
                bank_free[b] = [t]
                info["p", s] = t

            def step_values(s):
                g, i, r, br = steps[s]
                h = 4 * g + r
                b = 4 + (s // 3) % 2
                k = 7 + 8 * i
                o = (s // 3) % 4
                if br == 0:
                    t = PE(lambda e: e.matmul(BANK[b][:, 0:64], PT[s % NPT][0:k, 0:128], VC[0:k, g, :], start=True,
                                              stop=True), info["p", s], at["vc"], bank_free[b])
                    c = SM[:, o, 0:3]

                    def floor():
                        info["d"] = DV(lambda e: e.tensor_scalar(c, c, TINY, None, ALU.max), info["e", s + 2])

                    def invert():
                        info["d"] = DV(lambda e: e.reciprocal(c, c), info["d"])

                    def weigh():
                        info["cf", s // 3] = DV(lambda e: e.tensor_tensor(
                            CF[:, o, 0:3], c, GT[:, i, 3 * h:3 * h + 3], ALU.mult), info["d"], at["gate"],
                            info.get(("done", s // 3 - 4)), *fence_q)
                    between.extend([floor, invert, weigh])
                else:
                    c = 64 * g + 256 * (br - 1)
                    for j in range(i + 1):
                        t = PE(lambda e, j=j: e.matmul(BANK[b][:, 64 * br:64 * br + 64],
                                                       PT[s % NPT][:, j * 128:(j + 1) * 128], VS[:, j, c:c + 64],
                                                       start=(j == 0), stop=(j == i)), info["p", s], at["v"][j],
                               inc=(j == i))
                pt_free[s] = t
                if br == 2:
                    dst = OT[:, i, 64 * h:64 * h + 64]

                    def first():
                        info["o"] = DV(lambda e: e.tensor_scalar(dst, BANK[b][:, 0:64], CF[:, o, 0:1], None,
                                                                 ALU.mult), t, info["cf", s // 3], *fence_q)

                    def add(q):
                        info["o"] = DV(lambda e: e.scalar_tensor_tensor(
                            dst, BANK[b][:, 64 * q:64 * q + 64], CF[:, o, q:q + 1], dst, ALU.mult, ALU.add),
                            info["o"])
                        if q == 2:
                            bank_free[b] = [info["o"]]
                            info["done", s // 3] = info["o"]
                    between.extend([first, lambda: add(1), lambda: add(2)])

            def projection_pieces(n):
                parts, done = gemm_parts("nsa_t", n, AH, AL, a_ready, 7)

                def last():
                    parts[-1]()
                    query_evac(n, 7, done[0])
                return parts[:-1] + [last]

            N = len(steps)
            for s in range(N + MIX):
                if s < N:
                    g, i, r, br = steps[s]
                    if (i, r, br) == first_step and g < 3:
                        flush()
                        background += projection_pieces(2 * g + 2) + projection_pieces(2 * g + 3)
                if TURN <= s < N + TURN:
                    step_turn(s - TURN)
                if s < N:
                    step_scores(s)
                fill()
                if s >= MIX:
                    step_values(s - MIX)
                tick()
            fill(len(between))
            flush()
            assert not between
            st["sq"] = [[PE.now()], [PE.now()]]
            st["acc_read"] = PE.now()
            st["a_free"] = [PE.now()]
            fence_o = [DV.now()]
            for f in range(8):
                b = 2 + f % 4
                for i in range(4):
                    t = PE(lambda e, f=f, i=i, b=b: e.transpose(BANK[b][:, i * 128:(i + 1) * 128],
                                                               OT[:, i, f * 128:(f + 1) * 128], ident[:, :]),
                           *fence_o, bank_free[b], inc=(i == 3))
                hi = AC(lambda e, f=f, b=b: e.activation(AH[:, f, :], BANK[b][:, :], ACT.Copy), t, *st["a_free"])
                low = DV(lambda e, f=f, b=b: e.tensor_tensor(AL[:, f, :], BANK[b][:, :], AH[:, f, :], ALU.subtract),
                         hi, *st["a_free"])
                bank_free[b] = [low]
                a_ready[f] = [hi, low]
        fence_m = fence()
        with ExitStack() as ar:
            MN = sb("MN", [128, 8, S], stack=ar)
            m_tok = [None] * 8
            outs = abreast("nsa_out", range(3), AH, AL, a_ready)
            for f in range(8):
                b, tok = outs[f] if f < 3 else gemm_tile("nsa_out", f, AH, AL, a_ready, f == 3)
                branch_out(MN, m_tok, b, tok, f, fence_m)
            st["a_free"] = [PE.now()]
            update = post_norm(MN, m_tok, "mix_post1", "ffn_pre1")
        ffn_block2(("ffn3_in", "ffn3_out"), update, "ffn_post1", None, "3")

        s_out = sem("s_out")
        for f in range(8):
            SP(lambda e, f=f: e.dma_start(out[f], XT[:, f, :]).then_inc(s_out, 16), final["h", f], inc=False)
        assert len(units) == UNITS_TOTAL, len(units)

        block = ctx.enter_context(nc.Block())

        @block.sync
        def _(eng):
            SP.play(eng)
            eng.wait_ge(s_out, 128)

        @block.scalar
        def _(eng):
            AC.play(eng)

        @block.vector
        def _(eng):
            DV.play(eng)

        @block.tensor
        def _(eng):
            PE.play(eng)

        @block.gpsimd
        def _(eng):
            PO.play(eng)


def feature_tiles(w, columns=None):
    w = w if columns is None else w[:, columns]
    k, m = w.shape
    if m % 128:
        w = np.concatenate([w, np.zeros((k, 128 - m % 128), w.dtype)], axis=1)
        m = w.shape[1]
    return np.ascontiguousarray(w.reshape(k // 128, 128, m // 128, 128).transpose(2, 1, 0, 3).reshape(m // 128, 128, k))


def token_tiles(w):
    k, m = w.shape
    return np.ascontiguousarray(w.reshape(8, 128, m // 512, 512).transpose(2, 1, 0, 3).reshape(m // 512, 128, 4096))


def shape_constants():
    f32 = np.float32
    pos = np.arange(S, dtype=f32)
    theta = (f32(1.0) / np.power(f32(10000.0), np.linspace(0.0, 1.0, 128, dtype=f32))).astype(f32)
    ang = (theta[:, None] * pos[None, :]).astype(f32)
    cossin = np.concatenate([np.cos(ang), np.sin(ang)], axis=1).astype(f32)
    log_gamma = np.log(f32(1.0) - np.power(f32(2.0), f32(-5.0) - np.arange(4, dtype=f32))).astype(f32)
    rel = pos[None, :] - np.arange(128, dtype=f32)[:, None]
    decay = np.where(rel >= 0, np.exp(np.maximum(rel, 0.0)[None] * log_gamma[:, None, None]), 0.0) / 16.0
    dist = np.arange(640) - 127
    n = np.maximum(dist, 0)
    large = 16 + (np.log(np.maximum(n, 1).astype(f32) / f32(16)) / f32(math.log(8.0)) * f32(16)).astype(np.int32)
    bucket = np.where(n < 16, n, np.minimum(large, 31))
    onehot = (bucket[None, :] == np.arange(32)[:, None]) & (dist >= 0)[None, :]
    onehot = np.concatenate([onehot, (dist < 0)[None, :]], axis=0)
    return {"ident": np.eye(128, dtype=f32), "cossin": cossin, "decay": decay.astype(f32),
            "onehot": onehot.astype(f32)}


def laid_out(inp):
    a = {k: np.asarray(v) for k, v in inp.items()}
    cols = lambda v: v.reshape(-1, 128).T
    vecs = {
        "norm1": cols(a["norm1"][0]), "norm2": cols(a["norm2"][0]), "final_norm": cols(a["final_norm"]),
        "mix_pre0": cols(a["mix_norm_pre_2"][0]), "mix_post0": cols(a["mix_norm_post_2"][0]),
        "ffn_pre0": cols(a["ffn_norm_pre_2"][0]), "ffn_post0": cols(a["ffn_norm_post_2"][0]),
        "kv_norm": cols(a["kv_norm_2"]),
        "mix_pre1": cols(a["mix_norm_pre_2"][1]), "mix_post1": cols(a["mix_norm_post_2"][1]),
        "ffn_pre1": cols(a["ffn_norm_pre_2"][1]), "ffn_post1": cols(a["ffn_norm_post_2"][1]),
        "conv_w": a["conv_w"][0].reshape(4, 4, 128).transpose(2, 1, 0).reshape(128, 16),
        "conv_b": cols(a["conv_b"][0]), "lru_ba": cols(a["lru_ba"][0]), "lru_bi": cols(a["lru_bi"][0]),
        "lru_lambda": cols(a["lru_lambda"][0]), "b_alpha": cols(a["gla_b_alpha"][0]),
        "gla_norm": cols(a["gla_norm"][0]),
        "pe_k": a["cmp_pe_k_2"].reshape(16, 128).T, "pe_v": a["cmp_pe_v_2"].reshape(16, 128).T,
    }
    c = shape_constants()
    d = {
        "xT": a["x"][0].reshape(S, 8, 128).transpose(2, 1, 0).reshape(128, 8 * S),
        "vec": np.concatenate([vecs[n] for n, _ in VEC_NAMES], axis=1),
        "ident": c["ident"], "cossin": c["cossin"], "decay": c["decay"],
        "onehot": np.concatenate(
            [c["onehot"], np.concatenate([a["rel_bias_2"], np.full((1, 16), NEG, np.float32)], axis=0)], axis=1),
        "lru_wa": a["lru_wa"][0], "lru_wi": a["lru_wi"][0], "w_alpha": a["gla_w_alpha"][0],
    }
    w = a["w_in"][0]
    d["w_in_t"] = feature_tiles(w, np.r_[0:1536, 2048:2576])
    d["w_in_v"] = token_tiles(w[:, 1536:2048])
    d["w_out"] = feature_tiles(a["w_out"][0][np.r_[512:1024, 0:512]])
    half = 2816
    gate_up = np.concatenate([np.r_[128 * j:128 * j + 128, half + 128 * j:half + 128 * j + 128] for j in range(22)])
    for n, (wi, wo) in enumerate(((a["w_ffn_in"][0], a["w_ffn_out"][0]), (a["ffn_w_in_2"][0], a["ffn_w_out_2"][0]),
                                  (a["ffn_w_in_2"][1], a["ffn_w_out_2"][1])), 1):
        d[f"ffn{n}_in"] = feature_tiles(wi, gate_up)
        d[f"ffn{n}_out"] = feature_tiles(wo)
    w = a["ret_w_in_2"][0]
    order = []
    for h in range(4):
        for base in (0, 1024):
            at = base + 256 * h
            order += [np.arange(at, at + 256, 2), np.arange(at + 1, at + 256, 2)]
        order.append(np.arange(4096 + 512 * h, 4096 + 512 * h + 512))
    d["ret_t"] = feature_tiles(w, np.concatenate(order))
    d["ret_v"] = token_tiles(w[:, 2048:4096])
    d["ret_out"] = feature_tiles(a["ret_w_out_2"][0])
    w = a["kv_w_2"]
    d["kv_t"] = feature_tiles(w, np.r_[0:512, 512:768, 1024:1280])
    d["kv_v"] = token_tiles(w[:, np.r_[768:1024, 1280:1536]])
    w = a["nsa_w_in_2"][0]
    d["nsa_t"] = feature_tiles(w)
    d["nsa_out"] = feature_tiles(a["nsa_w_out_2"][0])
    w1 = [a[n].reshape(16, 128, 256).transpose(1, 0, 2) for n in ("cmp_w1_k_2", "cmp_w1_v_2")]
    d["cmp_w1"] = np.stack(w1)
    w2 = [a[n].reshape(2, 128, 64).transpose(1, 0, 2) for n in ("cmp_w2_k_2", "cmp_w2_v_2")]
    w2 = np.stack(w2, axis=1)
    d["cmp_w2"] = np.concatenate([w2, w2], axis=3)
    return {k: np.ascontiguousarray(v) for k, v in d.items()}


def kernel(**inputs):
    import concourse.bacc as _bacc
    from concourse.bass_utils import run_bass_kernel_spmd as _run

    arrays = laid_out(inputs)
    nc = _bacc.Bacc("TRN2", target_bir_lowering=False, num_devices=1)
    D = {n: nc.dram_tensor("in_" + n, a.shape, F32, kind="ExternalInput").ap() for n, a in arrays.items()}
    D["scratch"] = nc.dram_tensor("scratch", (16, 640), F32, kind="Internal").ap()
    out = nc.dram_tensor("out", (8, 128, S), F32, kind="ExternalOutput").ap()
    build(nc, D, out)
    r = _run(nc, [{"in_" + n: a for n, a in arrays.items()}], core_ids=[0])
    got = np.asarray(r.results[0]["out"])
    return got.reshape(1024, S).T.reshape(1, S, 1024)
```
